# Optimizing a Trainium2 kernel written in Bass

```python
import jax, jax.numpy as jnp
from jax import lax
import numpy as np

D_MODEL = 1024
BATCH = 1
SEQ = 1024
DEPTH = 2
DEC_BATCH = 8
DEC_SEQ = 4
PAST_LEN = 1024
PAGE_SIZE = 128

MIX_WIDTH = D_MODEL
HEAD_DIM = 64
RET_HEADS = 4
RET_V = MIX_WIDTH // 4 // RET_HEADS
RET_QK = RET_V // 2
RET_THETA = 10000.0
HG_HEADS = 4
HG_V = MIX_WIDTH // 4 // HG_HEADS
HG_K = HG_V
SWA_HD = HEAD_DIM
SWA_HEADS = (MIX_WIDTH // 2) // SWA_HD
SWA_KV = 2
SWA_GROUP = SWA_HEADS // SWA_KV
WINDOW = 128
SWA_BUF = WINDOW
ROT_DIM = SWA_HD // 4
ROPE_THETA = 500000.0
CHUNK = 128
D_FF = 4 * D_MODEL
ALPHA = (2.0 * DEPTH) ** 0.25
BETA = (8.0 * DEPTH) ** -0.25
LN_EPS = 1e-5
RMS_EPS = 1e-6

IN_SPLITS = (RET_HEADS * RET_QK, RET_HEADS * RET_QK, RET_HEADS * RET_V, RET_HEADS * RET_V,
             HG_HEADS * HG_K, HG_HEADS * HG_K, HG_HEADS * HG_V, HG_HEADS * HG_V,
             SWA_HEADS * SWA_HD, SWA_KV * SWA_HD, SWA_KV * SWA_HD)
HEAD_SHAPES = ((RET_HEADS, RET_QK), (RET_HEADS, RET_QK), (RET_HEADS, RET_V), (RET_HEADS, RET_V),
               (HG_HEADS, HG_K), (HG_HEADS, HG_K), (HG_HEADS, HG_V), (HG_HEADS, HG_V),
               (SWA_HEADS, SWA_HD), (SWA_KV, SWA_HD), (SWA_KV, SWA_HD))
V_PARTS = (2, 6, 10)
IN_COLS = sum(IN_SPLITS)

kernel_name = 'hymba_retention_hgrn2_swa_deepnorm_step'

def _layernorm(x, g, b):
    xf = x.astype(jnp.float32)
    mu = jnp.mean(xf, -1, keepdims=True)
    var = jnp.mean(jnp.square(xf - mu), -1, keepdims=True)
    return ((xf - mu) * lax.rsqrt(var + LN_EPS) * g.astype(jnp.float32) + b.astype(jnp.float32)).astype(x.dtype)

def _rmsnorm(x):
    xf = x.astype(jnp.float32)
    return xf * lax.rsqrt(jnp.mean(jnp.square(xf), -1, keepdims=True) + RMS_EPS)

def _rope(x, pos, inv_freq):
    r = 2 * inv_freq.shape[0]
    ang = pos.astype(jnp.float32)[:, None] * inv_freq[None, :]
    cos = jnp.cos(ang)[:, None, :]
    sin = jnp.sin(ang)[:, None, :]
    xr = x[..., :r].astype(jnp.float32)
    x1, x2 = xr[..., :r // 2], xr[..., r // 2:]
    rot = jnp.concatenate([x1 * cos - x2 * sin, x2 * cos + x1 * sin], -1).astype(x.dtype)
    return jnp.concatenate([rot, x[..., r:]], -1)

def _project(x, w_in):
    n, l = x.shape[:2]
    h = jnp.einsum('nld,dc->nlc', x, w_in)
    offs = [int(o) for o in np.cumsum(IN_SPLITS)[:-1]]
    parts = jnp.split(h, offs, axis=-1)
    return [p.reshape(n, l, *hs) for p, hs in zip(parts, HEAD_SHAPES)]

def _ret_log_decay():
    return jnp.log(1.0 - 2.0 ** (-5.0 - jnp.arange(RET_HEADS, dtype=jnp.float32)))

def _ret_qk(rq, rk, pos):
    inv = RET_THETA ** (-jnp.linspace(0.0, 1.0, RET_QK // 2, dtype=jnp.float32))
    return _rope(rq, pos, inv), _rope(rk, pos, inv) * (RET_QK ** -0.5)

def _swa_rope(x, pos):
    inv = ROPE_THETA ** (-jnp.arange(0, ROT_DIM, 2, dtype=jnp.float32) / ROT_DIM)
    return _rope(x, pos, inv)

def _hg_gates(hf, lb):
    lb = lb.reshape(HG_HEADS, HG_K)
    logf = jnp.logaddexp(jnp.log(lb), jnp.log1p(-lb) + jax.nn.log_sigmoid(hf.astype(jnp.float32)))
    return logf, -jnp.expm1(logf)

def _ret_chunk(q, k, v, s0):
    q, k, v, s0 = (a.astype(jnp.float32) for a in (q, k, v, s0))
    L = q.shape[1]
    lg = _ret_log_decay()
    idx = jnp.arange(L, dtype=jnp.float32)
    diff = idx[:, None] - idx[None, :]
    dec = jnp.where(diff >= 0, jnp.exp(jnp.maximum(diff, 0.0)[None] * lg[:, None, None]), 0.0)
    a = jnp.einsum('nthk,nshk->nhts', q, k) * dec[None]
    inter = jnp.exp((idx + 1.0)[:, None] * lg[None, :])[None, :, :, None]
    o = jnp.einsum('nhts,nshv->nthv', a, v) + jnp.einsum('nthk,nhkv->nthv', q, s0) * inter
    kdec = k * jnp.exp((L - 1.0 - idx)[:, None] * lg[None, :])[None, :, :, None]
    s = jnp.exp(L * lg)[None, :, None, None] * s0 + jnp.einsum('nshk,nshv->nhkv', kdec, v)
    return o, s

def _hg_chunk(q, k, v, logf, s0):
    q, k, v, s0 = (a.astype(jnp.float32) for a in (q, k, v, s0))
    L = q.shape[1]
    b = jnp.cumsum(logf, axis=1)
    causal = jnp.tril(jnp.ones((L, L), dtype=bool))
    rel = b[:, :, None] - b[:, None, :]
    dec = jnp.where(causal[None, :, :, None, None], jnp.exp(jnp.minimum(rel, 0.0)), 0.0)
    a = jnp.einsum('nthk,nshk,ntshk->nhts', q, k, dec)
    o = jnp.einsum('nhts,nshv->nthv', a, v) + jnp.einsum('nthk,nhkv->nthv', q * jnp.exp(b), s0)
    bl = b[:, -1]
    s = jnp.exp(bl)[..., None] * s0 + jnp.einsum('nshk,nshv->nhkv', k * jnp.exp(bl[:, None] - b), v)
    return o, s

def _scan_chunks(chunk_fn, arrays, s0):
    n, S = arrays[0].shape[:2]
    nc = S // CHUNK
    xs = tuple(jnp.moveaxis(a.reshape(n, nc, CHUNK, *a.shape[2:]), 1, 0) for a in arrays)

    def step(s, c):
        o, s = chunk_fn(*c, s)
        return s, o

    s, o = lax.scan(step, s0, xs)
    o = jnp.moveaxis(o, 0, 1)
    return o.reshape(n, S, *o.shape[3:]), s

def _sink_attn(q, k, v, mask, sinks):
    s = jnp.einsum('nmqkgd,nmskd->nmkgqs', q, k).astype(jnp.float32) * (SWA_HD ** -0.5)
    s = jnp.where(mask[None, :, None, None], s, -jnp.inf)
    sink = sinks.astype(jnp.float32).reshape(SWA_KV, SWA_GROUP)[None, None, :, :, None, None]
    m = jnp.maximum(jnp.max(s, -1, keepdims=True), sink)
    p = jnp.exp(s - m)
    den = jnp.sum(p, -1, keepdims=True) + jnp.exp(sink - m)
    o = jnp.einsum('nmkgqs,nmskd->nmqkgd', p / den, v.astype(jnp.float32))
    n, mb, lq = o.shape[:3]
    return o.reshape(n, mb * lq, SWA_HEADS * SWA_HD)

def _swa_prompt(q, k, v, sinks):
    n, S = q.shape[:2]
    nb = S // WINDOW
    qb = q.reshape(n, nb, WINDOW, SWA_KV, SWA_GROUP, SWA_HD)
    kb = k.reshape(n, nb, WINDOW, SWA_KV, SWA_HD)
    vb = v.reshape(n, nb, WINDOW, SWA_KV, SWA_HD)
    pad = ((0, 0), (1, 0), (0, 0), (0, 0), (0, 0))
    kk = jnp.concatenate([jnp.pad(kb, pad)[:, :-1], kb], axis=2)
    vv = jnp.concatenate([jnp.pad(vb, pad)[:, :-1], vb], axis=2)
    blk = jnp.arange(nb)[:, None]
    qpos = blk * WINDOW + jnp.arange(WINDOW)[None, :]
    kpos = (blk - 1) * WINDOW + jnp.arange(2 * WINDOW)[None, :]
    d = qpos[:, :, None] - kpos[:, None, :]
    mask = (d >= 0) & (d <= WINDOW) & (kpos[:, None, :] >= 0)
    return _sink_attn(qb, kk, vv, mask, sinks)

def _swa_sample(q, k, v, ck, cv, sinks):
    n, L = q.shape[:2]
    kk = jnp.concatenate([ck.astype(k.dtype), k], axis=1)
    vv = jnp.concatenate([cv.astype(v.dtype), v], axis=1)
    qpos = PAST_LEN + jnp.arange(L)
    kpos = PAST_LEN - SWA_BUF + jnp.arange(SWA_BUF + L)
    d = qpos[:, None] - kpos[None, :]
    mask = ((d >= 0) & (d <= WINDOW))[None]
    o = _sink_attn(q.reshape(n, 1, L, SWA_KV, SWA_GROUP, SWA_HD), kk[:, None], vv[:, None], mask, sinks)
    return o, kk[:, -SWA_BUF:], vv[:, -SWA_BUF:]

def _merge(o_r, g_r, o_h, g_h, o_s, hg_norm_w, w_out, dtype):
    n, l = o_r.shape[:2]
    ret = _rmsnorm(o_r) * jax.nn.silu(g_r.astype(jnp.float32))
    hg = _rmsnorm(o_h) * hg_norm_w.astype(jnp.float32) * jax.nn.silu(g_h.astype(jnp.float32))
    cat = jnp.concatenate([ret.reshape(n, l, -1), hg.reshape(n, l, -1),
                           o_s.astype(jnp.float32)], -1).astype(dtype)
    return jnp.einsum('nlc,cd->nld', cat, w_out)

def _mix_prompt(x, w_in, w_out, sinks, lb, hg_norm_w):
    n, S = x.shape[:2]
    pos = jnp.arange(S)
    rq, rk, rv, rg, hq, hf, hi, hgt, sq, sk, sv = _project(x, w_in)
    q_r, k_r = _ret_qk(rq, rk, pos)
    o_r, st_r = _scan_chunks(_ret_chunk, (q_r, k_r, rv), jnp.zeros((n, RET_HEADS, RET_QK, RET_V), jnp.float32))
    logf, k_h = _hg_gates(hf, lb)
    o_h, st_h = _scan_chunks(_hg_chunk, (hq, k_h, hi, logf), jnp.zeros((n, HG_HEADS, HG_K, HG_V), jnp.float32))
    q_s, k_s = _swa_rope(sq, pos), _swa_rope(sk, pos)
    o_s = _swa_prompt(q_s, k_s, sv, sinks)
    m = _merge(o_r, rg, o_h, hgt, o_s, hg_norm_w, w_out, x.dtype)
    return m, st_r, st_h, k_s[:, -SWA_BUF:], sv[:, -SWA_BUF:]

def _mix_sample(x, s_r, s_h, ck, cv, w_in, w_out, sinks, lb, hg_norm_w):
    L = x.shape[1]
    pos = PAST_LEN + jnp.arange(L)
    rq, rk, rv, rg, hq, hf, hi, hgt, sq, sk, sv = _project(x, w_in)
    q_r, k_r = _ret_qk(rq, rk, pos)
    o_r, st_r = _ret_chunk(q_r, k_r, rv, s_r)
    logf, k_h = _hg_gates(hf, lb)
    o_h, st_h = _hg_chunk(hq, k_h, hi, logf, s_h)
    q_s, k_s = _swa_rope(sq, pos), _swa_rope(sk, pos)
    o_s, nk, nv = _swa_sample(q_s, k_s, sv, ck, cv, sinks)
    m = _merge(o_r, rg, o_h, hgt, o_s, hg_norm_w, w_out, x.dtype)
    return m, st_r, st_h, nk, nv

def _post_block(x, mix, g1, b1, w_up, w_down, g2, b2):
    x = _layernorm(ALPHA * x + mix, g1, b1)
    h = jax.nn.relu(jnp.einsum('nld,df->nlf', x, w_up))
    return _layernorm(ALPHA * x + jnp.einsum('nlf,fd->nld', h * h, w_down), g2, b2)

def setup_inputs(seed: int = 0) -> dict:
    key = jax.random.key(seed)
    ks = jax.random.split(key, 20)
    nrm = jax.random.normal
    col_scale = jnp.concatenate([jnp.full((c,), BETA if i in V_PARTS else 1.0, jnp.float32)
                                 for i, c in enumerate(IN_SPLITS)])
    return {
        'x_prompt': nrm(ks[0], (BATCH, SEQ, D_MODEL), jnp.float32),
        'x_sample': nrm(ks[1], (DEC_BATCH, DEC_SEQ, D_MODEL), jnp.float32),
        'state_ret': 0.5 * nrm(ks[2], (DEPTH, DEC_BATCH, RET_HEADS, RET_QK, RET_V), jnp.float32),
        'state_hgrn': 0.5 * nrm(ks[3], (DEPTH, DEC_BATCH, HG_HEADS, HG_K, HG_V), jnp.float32),
        'cache_swa_k': nrm(ks[4], (DEPTH, DEC_BATCH, SWA_BUF, SWA_KV, SWA_HD), jnp.float32),
        'cache_swa_v': nrm(ks[5], (DEPTH, DEC_BATCH, SWA_BUF, SWA_KV, SWA_HD), jnp.float32),
        'w_in': nrm(ks[6], (DEPTH, D_MODEL, IN_COLS), jnp.float32) * (D_MODEL ** -0.5) * col_scale,
        'w_out': nrm(ks[7], (DEPTH, MIX_WIDTH, D_MODEL), jnp.float32) * (MIX_WIDTH ** -0.5) * BETA,
        'swa_sinks': 0.5 * nrm(ks[8], (DEPTH, SWA_HEADS), jnp.float32),
        'hg_lb_raw': 0.1 * nrm(ks[9], (DEPTH, HG_HEADS * HG_K), jnp.float32),
        'hg_norm_w': 1.0 + 0.1 * nrm(ks[10], (DEPTH, HG_V), jnp.float32),
        'ln_mix_g': 1.0 + 0.1 * nrm(ks[11], (DEPTH, D_MODEL), jnp.float32),
        'ln_mix_b': 0.1 * nrm(ks[12], (DEPTH, D_MODEL), jnp.float32),
        'w_up': nrm(ks[13], (DEPTH, D_MODEL, D_FF), jnp.float32) * (D_MODEL ** -0.5),
        'w_down': nrm(ks[14], (DEPTH, D_FF, D_MODEL), jnp.float32) * (D_FF ** -0.5) * BETA,
        'ln_ffn_g': 1.0 + 0.1 * nrm(ks[15], (DEPTH, D_MODEL), jnp.float32),
        'ln_ffn_b': 0.1 * nrm(ks[16], (DEPTH, D_MODEL), jnp.float32),
    }

def reference(x_prompt, x_sample, state_ret, state_hgrn, cache_swa_k, cache_swa_v,
              w_in, w_out, swa_sinks, hg_lb_raw, hg_norm_w, ln_mix_g, ln_mix_b,
              w_up, w_down, ln_ffn_g, ln_ffn_b):
    lb_all = jnp.cumsum(jax.nn.softmax(hg_lb_raw.astype(jnp.float32), axis=0), axis=0)
    lb = lb_all - lb_all[0:1]
    xp, xs = x_prompt, x_sample
    p_r, p_h, p_k, p_v = [], [], [], []
    s_r, s_h, s_k, s_v = [], [], [], []
    for l in range(DEPTH):
        m, a, b, c, d = _mix_prompt(xp, w_in[l], w_out[l], swa_sinks[l], lb[l], hg_norm_w[l])
        xp = _post_block(xp, m, ln_mix_g[l], ln_mix_b[l], w_up[l], w_down[l], ln_ffn_g[l], ln_ffn_b[l])
        p_r.append(a); p_h.append(b); p_k.append(c); p_v.append(d)
        m, a, b, c, d = _mix_sample(xs, state_ret[l], state_hgrn[l], cache_swa_k[l], cache_swa_v[l],
                                    w_in[l], w_out[l], swa_sinks[l], lb[l], hg_norm_w[l])
        xs = _post_block(xs, m, ln_mix_g[l], ln_mix_b[l], w_up[l], w_down[l], ln_ffn_g[l], ln_ffn_b[l])
        s_r.append(a); s_h.append(b); s_k.append(c); s_v.append(d)
    return (xp, xs, jnp.stack(p_r), jnp.stack(p_h), jnp.stack(p_k), jnp.stack(p_v),
            jnp.stack(s_r), jnp.stack(s_h), jnp.stack(s_k), jnp.stack(s_v))


_drawn_inputs = setup_inputs


def setup_inputs(seed=0):
    import zlib

    import numpy as np

    out = dict(_drawn_inputs(seed))
    spreads = {}
    factors = {'swa_sinks': 125.339, 'hg_norm_w': 3.218}
    for name, (base, spread) in spreads.items():
        noise = np.random.default_rng([zlib.crc32(name.encode()), seed]).standard_normal(out[name].shape)
        drawn = base * np.exp(spread * noise) if base else spread * noise
        out[name] = __import__('jax').numpy.asarray(drawn.astype(out[name].dtype))
    for name, factor in factors.items():
        out[name] = (out[name] * factor).astype(out[name].dtype)
    return out
```

```python
from contextlib import ExitStack

import numpy as np

import concourse.bass as bass
from concourse import mybir

F32 = mybir.dt.float32
F32R = mybir.dt.float32r
I32 = mybir.dt.int32
ALU = mybir.AluOpType
ACT = mybir.ActivationFunctionType
AX = mybir.AxisListType.X

P = 128
DM = 1024
KT = DM // P
DEPTH = 2
SEQ = 1024
NB, NL = 8, 4
ROWS_S = NB * NL
TOK = SEQ + ROWS_S
CHUNKS = SEQ // P
TILES = CHUNKS + 1
COLS = 2560
GROUP = 320
GROUPS = COLS // GROUP
FF = 4 * DM
FBLOCK = 256
FBLOCKS = FF // FBLOCK
NCH = 352
TCH = TOK // NCH
RQ, RK, RV, RG, HQ, HF, HI, HGT, SQ, SK, SV = 0, 128, 256, 512, 768, 1024, 1280, 1536, 1792, 2304, 2432
WIN = 128
ALPHA = (2.0 * DEPTH) ** 0.25
LN_EPS = 1e-5
RMS_EPS = 1e-6
NEG = -1e30
HALVES = [64, 32, 16, 8, 4, 2, 1]
NLEV = len(HALVES)
LG = [float(np.log1p(-(2.0 ** (-5.0 - h)))) for h in range(4)]

CONST = {}
_at = 0
for _name, _w in (("ident", 128), ("sel", 2), ("band", 128), ("smask", 320), ("dec", 512), ("decs", 512),
                  ("inter", 128), ("inters", 128), ("kdec", 4), ("kdecs", 4), ("run", 1), ("runs", 128),
                  ("bm", 256), ("tb", 8)):
    CONST[_name] = (_at, _w)
    _at += _w
NCONST = _at


def shape_constants():
    p = np.arange(P)
    t = np.arange(P)
    c = np.zeros((P, NCONST), np.float32)

    def put(name, value):
        a, w = CONST[name]
        c[:, a:a + w] = np.asarray(value, np.float64).reshape(P, w)

    put("ident", np.eye(P))
    put("sel", p[:, None] // 64 == np.arange(2)[None])
    put("band", np.where(t[None] >= p[:, None], 0.0, NEG))
    sm = np.full((P, 2, WIN + ROWS_S), NEG)
    for r in range(P):
        b, l = r // 32, r % 4
        for rt in range(2):
            sm[r, rt, l:WIN] = 0.0
            sm[r, rt, WIN + 4 * (4 * rt + b):WIN + 4 * (4 * rt + b) + l + 1] = 0.0
    put("smask", sm)
    lg = np.array(LG)
    d = t[None, None, :] - p[:, None, None]
    dec = np.where(d >= 0, np.exp(np.maximum(d, 0) * lg[None, :, None]), 0.0) * 32 ** -0.5
    put("dec", dec)
    same = (t[None, None, :] // NL == p[:, None, None] // NL) & (t[None, None, :] < ROWS_S)
    put("decs", np.where(same, dec, 0.0))
    put("inter", np.exp((t[None] + 1) * lg[p // 32][:, None]))
    put("inters", np.exp((t[None] % NL + 1) * lg[p // 32][:, None]))
    put("kdec", np.exp((P - 1 - p)[:, None] * lg[None]) * 32 ** -0.5)
    put("kdecs", np.exp((NL - 1 - p % NL)[:, None] * lg[None]) * 32 ** -0.5)
    put("run", np.ones((P, 1)))
    put("runs", np.broadcast_to(t % NL != 0, (P, P)))
    put("bm", np.broadcast_to((np.arange(ROWS_S)[None] // NL == np.arange(NB)[:, None])[None], (P, NB, ROWS_S)))
    put("tb", p[:, None] // NL == np.arange(NB)[None])
    lev = np.zeros((P, 2, NLEV, 64), np.int32)
    for i, half in enumerate(HALVES):
        blk, off = np.divmod(np.arange(64), half)
        lo = blk * 2 * half
        m = (p[:, None] >= lo[None]) & (p[:, None] < lo[None] + half)
        lev[:, 0, i] = m
        lev[:, 1, i] = m if half < NL else 0
    swa = np.zeros((P, 3, WIN), np.float32)
    swa[:, 0] = swa[:, 2] = np.where(t[None] <= p[:, None], 0.0, NEG)
    swa[:, 1] = NEG
    pos = np.concatenate([np.arange(SEQ), np.tile(SEQ + np.arange(NL), NB)]).astype(np.float32)
    inv_r = (10000.0 ** (-np.linspace(0.0, 1.0, 16, dtype=np.float32))).astype(np.float32)
    inv_s = (500000.0 ** (-np.arange(0, 16, 2, dtype=np.float32) / 16)).astype(np.float32)
    ar = (pos[:, None] * inv_r[None]).astype(np.float32).astype(np.float64)
    as_ = (pos[:, None] * inv_s[None]).astype(np.float32).astype(np.float64)
    rope = np.concatenate([np.cos(ar), np.sin(ar), np.cos(as_), np.sin(as_)], 1).astype(np.float32)
    return c, lev, swa, rope


class Steps:

    def __init__(self, sem, names):
        self.sem, self.names, self.next = sem, names.split(), 0

    def step(self, name):
        assert self.names[self.next] == name, (self.names[self.next], name)
        self.next = (self.next + 1) % len(self.names)
        return self.sem

    def at(self, name, n):
        return n * len(self.names) + (self.names.index(name) + 1)


def build(nc, A):
    ctx = ExitStack()
    with ctx:
        where = [16512]

        def place(name, shape, dt, at):
            n = 4
            for s in shape[1:]:
                n *= s
            assert at + n <= 229344, (name, at + n)
            return nc.alloc_sbuf_tensor_at(name, shape, dt, offset=at), at + n

        def region(start):
            here = [start]

            def sb(name, shape, dt=F32):
                t, end = place(name, shape, dt, here[0])
                here[0] = (end + 31) // 32 * 32
                return t
            sb.here = here
            return sb

        def sem(name):
            return ctx.enter_context(nc.semaphore(name))

        sb = region(where[0])
        const = sb("const", [P, NCONST])
        lev_mask = sb("lev_mask", [P, 2, NLEV, 64], I32)
        swa_mask = sb("swa_mask", [P, 3, WIN])
        lb_raw = sb("lb_raw", [P, DEPTH, 2])
        lb_exp = sb("lb_exp", [P, DEPTH, 2])
        lb_tmp = sb("lb_tmp", [P, 4])
        lb_all = sb("lb_all", [P, DEPTH, 2])
        lb = sb("lb", [P, 2])
        omlb = sb("omlb", [P, 2])
        hg_w = sb("hg_w", [P, 64])
        sink_b = sb("sink_b", [P, 8])
        sink_r = sb("sink_r", [P, 1])
        u0 = sb.here[0]
        sb = region(u0)
        u_hi = sb("u_hi", [P, KT, TOK], F32R)
        u_lo = sb("u_lo", [P, KT, TOK], F32R)
        v0 = sb.here[0]
        v_hi = sb("v_hi", [P, KT, TOK], F32R)
        v_lo = sb("v_lo", [P, KT, TOK], F32R)
        r0 = sb.here[0]

        def cst(name):
            a, w = CONST[name]
            return const[:, a:a + w]

        ident = cst("ident")

        sb = region(v0)
        wi_raw = sb("wi_raw", [P, KT, GROUP])
        wi_hi = [sb(f"wi_hi{i}", [P, KT, GROUP], F32R) for i in range(2)]
        wi_lo = [sb(f"wi_lo{i}", [P, KT, GROUP], F32R) for i in range(2)]
        h_out = [sb(f"h_out{i}", [P, GROUP]) for i in range(3)]

        sb = region(v0)
        hb = [sb(f"hb{i}", [P, COLS]) for i in range(2)]
        rt = [sb(f"rt{i}", [P, 48]) for i in range(2)]
        rope_a = sb("rope_a", [P, 256])
        rope_b = sb("rope_b", [P, 256])
        rope_sa = sb("rope_sa", [P, 10, 2, 8])
        rope_sb = sb("rope_sb", [P, 10, 2, 8])
        rot_r = sb("rot_r", [P, 256])
        rot_q = sb("rot_q", [P, 4, 2, 64])
        rot_k = sb("rot_k", [P, 2, 64])
        g_e = sb("g_e", [P, 2, P])
        g_r = sb("g_r", [P, 2, P])
        g_s = sb("g_s", [P, 2, P])
        g_k = sb("g_k", [P, 2, P])
        g_f = sb("g_f", [P, 2, P])
        g_b = sb("g_b", [P, 2, P])
        g_q = sb("g_q", [P, 2, P])
        g_p = sb("g_p", [P, 2, P])
        g_eb = sb("g_eb", [P, 2, P])
        g_qe = sb("g_qe", [P, 2, P])
        g_ka = sb("g_ka", [P, 2, P])
        g_kt = sb("g_kt", [P, 2, P])
        lev_e = sb("lev_e", [P, NLEV, 2, P])
        lev_x = sb("lev_x", [P, NLEV, 2, P])
        diag = sb("diag", [P, 4])
        hg_a = sb("hg_a", [P, 4, P])
        r_kT = sb("r_kT", [P, P])
        r_qx = sb("r_qx", [P, 4, P])
        r_qi = sb("r_qi", [P, P])
        r_a = sb("r_a", [P, 4, P])
        r_kd = sb("r_kd", [P, 4, 32])
        s_qT = sb("s_qT", [P, 4, P])
        s_kT = sb("s_kT", [P, 2, P])
        s_v = sb("s_v", [P, 2, P])
        st_r = sb("st_r", [P, 256])
        st_h = sb("st_h", [P, 2, P])
        mx = sb("mx", [P, 8])
        m = sb("m", [P, 8])
        nm = sb("nm", [P, 8])
        sk = sb("sk", [P, 8])
        esk = sb("esk", [P, 8])
        ssum = sb("ssum", [P, 8])
        den = sb("den", [P, 8])
        rden = sb("rden", [P, 8])
        gate = sb("gate", [P, 2, 256])
        gate_e = sb("gate_e", [P, 2, 256])
        rms_sq = sb("rms_sq", [P, 8, 64])
        rms = sb("rms", [P, 8])
        rms_v = sb("rms_v", [P, 8])
        rms_l = sb("rms_l", [P, 8])
        rms_t = sb("rms_t", [P, 8])
        cat = sb("cat", [P, DM])
        p0 = sb.here[0]
        prob = sb("prob", [P, 8, 256])
        probT = sb("probT", [P, 16, P])
        p1 = sb.here[0]
        qm_r = sb("qm_r", [P, NB, ROWS_S])
        qm_h = sb("qm_h", [P, 2, NB, ROWS_S])
        kdm = sb("kdm", [P, NB, P])
        ksm = sb("ksm", [P, 2, NB, P])
        s0_r = sb("s0_r", [P, NB, 256])
        s0_h = sb("s0_h", [P, 2, NB, P])
        spT = sb("spT", [P, 2, P])
        spN = sb("spN", [P, 2, P])
        sb = region(p0)
        ck = sb("ck", [P, NB, P])
        cv = sb("cv", [P, NB, P])
        ckT = sb("ckT", [P, NB, P])
        qxs = sb("qxs", [P, NB, 2, 4, NL])
        s_prob = sb("s_prob", [P, 2, WIN + ROWS_S])
        assert sb.here[0] <= p1, (sb.here[0], p1)
        sb = region(v0)
        wo_raw = sb("wo_raw", [P, KT, P])
        wo_hi = [sb(f"wo_hi{i}", [P, KT, P], F32R) for i in range(2)]
        wo_lo = [sb(f"wo_lo{i}", [P, KT, P], F32R) for i in range(2)]
        sb = region(r0)
        acc = sb("acc", [P, KT, TOK])
        n0 = sb.here[0]
        stage = sb("stage", [P, KT, P])
        xin = [sb(f"xin{i}", [P, DM]) for i in range(2)]
        xn = [sb(f"xn{i}", [P, DM]) for i in range(2)]
        stats = sb("stats", [P, 2, 2, 6])
        aggr = sb("aggr", [P, 2, 2])
        rstd = sb("rstd", [P, 2])
        var = sb("var", [P, 2])
        logv = sb("logv", [P, 2])
        newt = sb("newt", [P, 2])
        ln_g = sb("ln_g", [P, DM])
        ln_b = sb("ln_b", [P, DM])
        sb = region(u0)
        hid_hi = [sb(f"hid_hi{i}", [P, 2, TOK], F32R) for i in range(2)]
        hid_lo = [sb(f"hid_lo{i}", [P, 2, TOK], F32R) for i in range(2)]
        wu_hi = sb("wu_hi", [P, KT, FBLOCK], F32R)
        wu_lo = sb("wu_lo", [P, KT, FBLOCK], F32R)
        wd_hi = sb("wd_hi", [P, 2, DM], F32R)
        wd_lo = sb("wd_lo", [P, 2, DM], F32R)
        assert sb.here[0] <= v0
        sb = region(n0)
        wu_raw = sb("wu_raw", [P, KT, FBLOCK])
        wd_raw = sb("wd_raw", [P, 2, DM])
        relu = [sb(f"relu{i}", [P, NCH]) for i in range(3)]
        sq = [sb(f"sq{i}", [P, NCH]) for i in range(3)]

        ps = ctx.enter_context(nc.psum_tensor("ps", [P, 8, 512], F32))

        const_in = sem("const_in")
        par_in = sem("par_in")
        phase_end = sem("phase_end")
        marks = sem("marks")
        lbd = Steps(sem("bound_dve"), "max sub0 sub1 sum inv p0 p1 cum lb0 lb1")
        lba = Steps(sem("bound_act"), "exp")
        zd = Steps(sem("layer_dve"), "lb omlb r h kT v qx sr sh")
        x_in = [sem(f"x_in{i}") for i in range(2)]
        x_out = [sem(f"x_out{i}") for i in range(2)]
        na = Steps(sem("norm_act"), "stage")
        npe = Steps(sem("norm_pe"), "T")
        nd = Steps(sem("norm_dve"), "res st0 st1 aggr var n0 n1 rstd xn")
        nr = Steps(sem("norm_rstd_act"), "ln r")
        npl = Steps(sem("norm_pool"), "g b")
        spe = Steps(sem("split_pe"), "T")
        sa = Steps(sem("split_act"), "hi")
        sd = Steps(sem("split_dve"), "lo")
        wi_in = sem("wi_in")
        wi_hi_done = sem("wi_hi_done")
        wi_lo_done = sem("wi_lo_done")
        proj_ready = sem("proj_ready")
        proj_free = sem("proj_free")
        h_stored = [sem(f"h_stored{i}") for i in range(3)]
        wo_in = sem("wo_in")
        wo_hi_done = sem("wo_hi_done")
        wo_lo_done = sem("wo_lo_done")
        out_ready = sem("out_ready")
        out_free = sem("out_free")
        wu_in = sem("wu_in")
        wd_in = sem("wd_in")
        wu_hi_done = sem("wu_hi_done")
        wu_lo_done = sem("wu_lo_done")
        wd_hi_done = sem("wd_hi_done")
        wd_lo_done = sem("wd_lo_done")
        up_ready = sem("up_ready")
        up_free = sem("up_free")
        sq_done = sem("sq_done")
        hid_hi_done = sem("hid_hi_done")
        hid_lo_done = sem("hid_lo_done")
        down_ready = sem("down_ready")
        down_free = sem("down_free")
        acc_zero = sem("acc_zero")
        h_in = [sem(f"h_in{i}") for i in range(2)]
        levels = [f"{i}" for i in range(NLEV)]
        rp = Steps(sem("rope_pool"), "ra rb0 rb1 r0 r1 sa sb0 sb1 q0 q1 k0 k1 qc kc gc kd v g1 sg sw sr")
        tpe = Steps(sem("mixT_pe"), "h r q")
        ga = Steps(sem("gate_act"), "e q kTr kTs qT f eb E ka eg")
        gd = Steps(sem("gate_dve"), "clip one r s k0 k1 f0 f1 b0 b1 p ka " + " ".join(f"ar{i} al{i}" for i in levels))
        gp = Steps(sem("lev_pool"), "qe kst " + " ".join(f"r{i} l{i}" for i in levels))
        rd = Steps(sem("ret_dve"), "x0 x1 x2 x3 qi a")
        mpe = Steps(sem("heads_pe"), "ret lev0 lev1 kt o st")
        hd = Steps(sem("heads_dve"), "diag a " + " ".join("c" + i for i in levels) + " kt")
        md = Steps(sem("merge_dve"), "r ss ms n0 n1 rstd rh")
        ma = Steps(sem("merge_act"), "sq ln r")
        cpe = Steps(sem("cat_pe"), "T0 T1")
        ca = Steps(sem("cat_act"), "hi")
        cd = Steps(sem("cat_dve"), "lo")
        wpe = Steps(sem("window_pe"), "s T0 T1 o")
        wd = Steps(sem("window_dve"), "s band mx m nm sk den rden T o")
        wa = Steps(sem("window_act"), "e0 e1 e2 e3 e4 e5 e6 e7 sk T")
        sdv = Steps(sem("state_dve"), "r0 r1 r2 r3 h0 h1 h2 h3")
        dp = Steps(sem("decode_pool"), "qr qh0 qh1 kd ks0 ks1")
        dpe = Steps(sem("decode_pe"), "ckT s T o st_h")
        dd = Steps(sem("decode_dve"), "zx x0 x1 s mx m nm sk den rden p0 p1 T o0 o1 r0 r1 r2 r3 hm h0 h1 h2 h3")
        da = Steps(sem("decode_act"), "ck e0 e1 sk T o0 o1")
        kv_out = sem("kv_out")
        state_out = sem("state_out")
        s0_in = sem("s0_in")
        cache_in = sem("cache_in")
        cache_out = sem("cache_out")

        block = ctx.enter_context(nc.Block())

        def apart(eng):
            eng.sem_inc(marks, 1)

        def barrier(eng, k):
            apart(eng)
            eng.drain().then_inc(phase_end, 1)
            eng.wait_ge(phase_end, 5 * k)
            apart(eng)

        def phase(l, j):
            return l * 6 + (2 + j)

        def tile_rows(t):
            return P if t < CHUNKS else ROWS_S

        def x_count(l, which, t, i=0):
            return (l * 2 + (which + 1)) * (5 - t % 2) + (i + (t // 2 + 1))

        @block.sync
        def _(sp):
            sp.dma_start(const[:], A["c_const"]).then_inc(const_in, 16)
            sp.dma_start(lev_mask[:], A["c_lev"]).then_inc(const_in, 16)
            with nc.allow_non_contiguous_dma(reason="512 words"):
                sp.dma_start(lb_raw[:], A["hg_lb_raw"].rearrange("l (t p) -> p l t", p=P)).then_inc(const_in, 16)
            for t in range(TILES):
                p, rows = t % 2, tile_rows(t)
                if t >= 2:
                    sp.wait_ge(spe.sem, spe.at("T", t - 2))
                    sp.wait_ge(x_out[p], 16 * (t // 2))
                sp.dma_start(xn[p][0:rows, :], A["x"][t * P:t * P + rows, :]).then_inc(x_in[p], 16)
                sp.wait_ge(x_in[p], 16 * (t // 2 + 1))
                sp.dma_start(A["y"][t * P:t * P + rows, :], xn[p][0:rows, :]).then_inc(x_out[p], 16)
            sp.wait_ge(x_out[0], 16 * 5)
            sp.wait_ge(x_out[1], 16 * 4)
            barrier(sp, 1)

            with sp.Fori(0, DEPTH) as l:
                sp.dma_start(swa_mask[:], A["c_swa"]).then_inc(par_in, 16)
                sp.dma_start(hg_w[:], A["hg_norm_w"][bass.ds(l, 1), :].broadcast_to([P, 64])).then_inc(par_in, 16)
                sp.dma_start(sink_b[:], A["swa_sinks"][bass.ds(l, 1), :].broadcast_to([P, 8])).then_inc(par_in, 16)
                with nc.allow_non_contiguous_dma(reason="128 words"):
                    sp.dma_start(sink_r[:], A["sink_rows"][:, bass.ds(l, 1)]).then_inc(par_in, 16)

                def load_wi(g):
                    G = l * GROUPS + g
                    sp.wait_ge(wi_hi_done, G)
                    sp.wait_ge(wi_lo_done, G)
                    sp.dma_start(wi_raw[:], A["w_in"][bass.ds(l, 1), :, bass.ds(g * GROUP, GROUP)]
                                 .rearrange("l (k p) c -> p (l k) c", p=P)).then_inc(wi_in, 16)

                def store_h(g):
                    for t in range(TILES):
                        rows = tile_rows(t)
                        sp.wait_ge(proj_free, (l * GROUPS + g) * TILES + (t + 4))
                        sp.dma_start(A["hscr"][t * P:t * P + rows, bass.ds(g * GROUP, GROUP)],
                                     h_out[t % 3][0:rows, :]).then_inc(h_stored[t % 3], 16)

                load_wi(0)
                load_wi(1)
                with sp.Fori(0, GROUPS // 2 - 1) as i:
                    for q in range(2):
                        store_h(i * 2 + q)
                        load_wi(i * 2 + (q + 2))
                store_h(GROUPS - 2)
                store_h(GROUPS - 1)
                for j in range(3):
                    sp.wait_ge(h_stored[j], (l + 1) * (16 * 3 * GROUPS))
                apart(sp)
                barrier(sp, phase(l, 0))

                def load_h(c, p, rows=P):
                    sp.dma_start(hb[p][0:rows, :], A["hscr"][bass.ds(c * P, rows), :]).then_inc(h_in[p], 16)
                    sp.dma_start(rt[p][0:rows, :], A["c_rope"][bass.ds(c * P, rows), :]).then_inc(h_in[p], 16)

                def hb_used(n):
                    sp.wait_ge(mpe.sem, mpe.at("st", n))
                    sp.wait_ge(rp.sem, rp.at("sg", n))

                sp.wait_ge(zd.sem, zd.at("sh", l))
                for h in range(4):
                    pr, j = h // 2, h % 2
                    sp.dma_start(s0_r[32 * h:32 * h + 32, :, 64 * h:64 * h + 64],
                                 A["state_ret"][bass.ds(l, 1), :, h, :, :].rearrange("l b k v -> k (l b) v"))\
                      .then_inc(s0_in, 16)
                    sp.dma_start(s0_h[64 * j:64 * j + 64, pr, :, 64 * j:64 * j + 64],
                                 A["state_hgrn"][bass.ds(l, 1), :, h, :, :].rearrange("l b k v -> k (l b) v"))\
                      .then_inc(s0_in, 16)
                for name, src in (("s_swa_k", "cache_swa_k"), ("s_swa_v", "cache_swa_v")):
                    sp.dma_start(A[name][bass.ds(l, 1), :, 0:WIN - NL, :],
                                 A[src][bass.ds(l, 1), :, NL:WIN, :]).then_inc(cache_out, 16)
                load_h(0, 0)
                load_h(1, 1)
                with sp.Fori(0, CHUNKS // 2 - 1) as i:
                    for p in range(2):
                        hb_used(l * TILES + i * 2 + p)
                        load_h(i * 2 + (p + 2), p)
                hb_used(l * TILES + (CHUNKS - 2))
                load_h(CHUNKS, 0, ROWS_S)
                n7 = l * TILES + (CHUNKS - 1)
                sp.wait_ge(rp.sem, rp.at("v", n7))
                sp.dma_start(A["p_swa_k"][bass.ds(l, 1), :, :], rot_k[:, :, :]).then_inc(kv_out, 16)
                sp.dma_start(A["p_swa_v"][bass.ds(l, 1), :, :], s_v[:, 1, :]).then_inc(kv_out, 16)
                sp.wait_ge(wpe.sem, wpe.at("o", l * CHUNKS + (CHUNKS - 1)))
                sp.dma_start(ck[:], A["cache_swa_k"][bass.ds(l, 1)].rearrange("l b s c -> s (l b) c"))\
                  .then_inc(cache_in, 16)
                sp.dma_start(cv[:], A["cache_swa_v"][bass.ds(l, 1)].rearrange("l b s c -> s (l b) c"))\
                  .then_inc(cache_in, 16)
                sp.wait_ge(sdv.sem, sdv.at("h3", l * CHUNKS + (CHUNKS - 1)))
                for h in range(4):
                    pr, j = h // 2, h % 2
                    sp.dma_start(A["p_state_ret"][bass.ds(l, 1), h, :, :],
                                 st_r[32 * h:32 * h + 32, 64 * h:64 * h + 64]).then_inc(state_out, 16)
                    sp.dma_start(A["p_state_hgrn"][bass.ds(l, 1), h, :, :],
                                 st_h[64 * j:64 * j + 64, pr, 64 * j:64 * j + 64]).then_inc(state_out, 16)
                sp.wait_ge(rp.sem, rp.at("v", l * TILES + CHUNKS))
                for b in range(NB):
                    rows = slice(NL * b, NL * b + NL)
                    sp.dma_start(A["s_swa_k"][bass.ds(l, 1), b, WIN - NL:WIN, :], rot_k[rows, :, :])\
                      .then_inc(cache_out, 16)
                    sp.dma_start(A["s_swa_v"][bass.ds(l, 1), b, WIN - NL:WIN, :], s_v[rows, 0, :])\
                      .then_inc(cache_out, 16)
                sp.wait_ge(dd.sem, dd.at("h3", l))
                for h in range(4):
                    pr, j = h // 2, h % 2
                    sp.dma_start(A["s_state_ret"][bass.ds(l, 1), :, h, :, :].rearrange("l b k v -> k (l b) v"),
                                 s0_r[32 * h:32 * h + 32, :, 64 * h:64 * h + 64]).then_inc(state_out, 16)
                    sp.dma_start(A["s_state_hgrn"][bass.ds(l, 1), :, h, :, :].rearrange("l b k v -> k (l b) v"),
                                 s0_h[64 * j:64 * j + 64, pr, :, 64 * j:64 * j + 64]).then_inc(state_out, 16)
                sp.wait_ge(kv_out, (l + 1) * 32)
                apart(sp)
                sp.wait_ge(state_out, (l + 1) * 256)
                apart(sp)
                sp.wait_ge(cache_out, (l + 1) * (16 * (2 + 2 * NB)))
                apart(sp)
                barrier(sp, phase(l, 1))

                def load_wo(j):
                    J = l * KT + j
                    cols = bass.ds(j * P, P)
                    sp.wait_ge(wo_hi_done, J)
                    sp.wait_ge(wo_lo_done, J)
                    sp.dma_start(wo_raw[:, 0:4, :], A["w_out"][bass.ds(l, 1), 0:512, cols]
                                 .rearrange("l (k p) c -> p (l k) c", p=P)).then_inc(wo_in, 16)
                    for kv in range(2):
                        sp.dma_start(wo_raw[64 * kv:64 * kv + 64, 4:8, :],
                                     A["w_out"][bass.ds(l, 1), 512 + 256 * kv:768 + 256 * kv, cols]
                                     .rearrange("l (g d) c -> d (l g) c", d=64)).then_inc(wo_in, 16)

                with sp.Fori(0, KT) as j:
                    load_wo(j)
                barrier(sp, phase(l, 2))

                def norm_tiles(which, gname, bname):
                    sp.dma_start(ln_g[:], A[gname][bass.ds(l, 1), :].broadcast_to([P, DM])).then_inc(par_in, 16)
                    sp.dma_start(ln_b[:], A[bname][bass.ds(l, 1), :].broadcast_to([P, DM])).then_inc(par_in, 16)
                    base = (l * 2 + which) * TILES

                    def load(t, p, rows):
                        sp.dma_start(xin[p][0:rows, :], A["y"][bass.ds(t * P, rows), :]).then_inc(x_in[p], 16)

                    def store(t, p, rows):
                        sp.wait_ge(npl.sem, npl.at("b", base + t))
                        sp.dma_start(A["y"][bass.ds(t * P, rows), :], xn[p][0:rows, :]).then_inc(x_out[p], 16)

                    with sp.Fori(0, CHUNKS // 2) as i:
                        for p in range(2):
                            load(i * 2 + p, p, P)
                        for p in range(2):
                            store(i * 2 + p, p, P)
                    load(CHUNKS, 0, ROWS_S)
                    store(CHUNKS, 0, ROWS_S)
                    sp.wait_ge(x_out[0], (l * 2 + (which + 2)) * (5 * 16))
                    apart(sp)
                    sp.wait_ge(x_out[1], (l * 2 + (which + 2)) * (4 * 16))
                    apart(sp)

                norm_tiles(0, "ln_mix_g", "ln_mix_b")
                barrier(sp, phase(l, 3))

                def load_wu(b):
                    B = l * FBLOCKS + b
                    sp.wait_ge(wu_hi_done, B)
                    sp.wait_ge(wu_lo_done, B)
                    sp.dma_start(wu_raw[:], A["w_up"][bass.ds(l, 1), :, bass.ds(b * FBLOCK, FBLOCK)]
                                 .rearrange("l (k p) c -> p (l k) c", p=P)).then_inc(wu_in, 16)

                def load_wd(b):
                    B = l * FBLOCKS + b
                    sp.wait_ge(wd_hi_done, B)
                    sp.wait_ge(wd_lo_done, B)
                    sp.dma_start(wd_raw[:], A["w_down"][bass.ds(l, 1), bass.ds(b * FBLOCK, FBLOCK), :]
                                 .rearrange("l (f p) d -> p (l f) d", p=P)).then_inc(wd_in, 16)

                load_wu(0)
                with sp.Fori(0, FBLOCKS - 1) as b:
                    load_wu(b + 1)
                    load_wd(b)
                load_wd(FBLOCKS - 1)
                barrier(sp, phase(l, 4))
                norm_tiles(1, "ln_ffn_g", "ln_ffn_b")
                barrier(sp, phase(l, 5))

        @block.tensor
        def _(pe):
            def transpose(out, in_, rows):
                return nc.tensor.transpose(out, in_, ident[0:rows, 0:rows])

            def three(out, a_hi, a_lo, b_hi, b_lo, start, stop):
                nc.tensor.matmul(out, a_hi, b_hi, start=start, stop=False)
                nc.tensor.matmul(out, a_hi, b_lo, start=False, stop=False)
                return nc.tensor.matmul(out, a_lo, b_hi, start=False, stop=stop)

            def split_tile(m, p, rows, first=False):
                if not first:
                    pe.wait_ge(sa.sem, sa.at("hi", m - 2))
                    pe.wait_ge(sd.sem, sd.at("lo", m - 2))
                    apart(pe)
                for k in range(KT):
                    last = transpose(ps[:, 4 + 2 * p + k // 4, (k % 4) * P:(k % 4) * P + rows],
                                     xn[p][0:rows, k * P:(k + 1) * P], rows)
                last.then_inc(spe.step("T"), 1)

            pe.wait_ge(const_in, 48)
            for t in range(TILES):
                pe.wait_ge(x_in[t % 2], 16 * (t // 2 + 1))
                split_tile(t, t % 2, tile_rows(t), first=t < 2)
            barrier(pe, 1)

            with pe.Fori(0, DEPTH) as l:
                with pe.Fori(0, GROUPS // 2) as i:
                    for q in range(2):
                        G = l * GROUPS + i * 2 + q
                        pe.wait_ge(wi_hi_done, G + 1)
                        pe.wait_ge(wi_lo_done, G + 1)
                        for t in range(TILES):
                            rows = tile_rows(t)
                            pe.wait_ge(proj_free, G * TILES + (t + 1))
                            tok = slice(t * P, t * P + rows)
                            for k in range(KT):
                                last = three(ps[0:rows, t % 3, 0:GROUP], u_hi[:, k, tok], u_lo[:, k, tok],
                                             wi_hi[q][:, k, :], wi_lo[q][:, k, :], k == 0, k == KT - 1)
                            last.then_inc(proj_ready, 1)
                barrier(pe, phase(l, 0))

                def chunk(n, w, p, rows, loads):
                    prompt = rows == P
                    x = hb[p]
                    pe.wait_ge(h_in[p], loads * 32)
                    pe.wait_ge(md.sem, n * len(md.names))
                    for j in range(2):
                        transpose(ps[:, 0, j * P:(j + 1) * P], x[:, HF + j * P:HF + (j + 1) * P], P)
                    for j in range(2):
                        last = transpose(ps[:, 0, (2 + j) * P:(3 + j) * P], x[:, HQ + j * P:HQ + (j + 1) * P], P)
                    last.then_inc(tpe.step("h"), 1)
                    pe.wait_ge(rp.sem, rp.at("kc", n))
                    pe.wait_ge(wd.sem, w * len(wd.names))
                    transpose(ps[:, 1, 0:P], rot_r[:, 0:P], P)
                    transpose(ps[:, 1, P:2 * P], rot_r[:, P:2 * P], P)
                    transpose(ps[:, 1, 2 * P:3 * P], rot_k[:, :, :].rearrange("p a b -> p (a b)"), P)\
                        .then_inc(tpe.step("r"), 1)
                    pe.wait_ge(ca.sem, n)
                    pe.wait_ge(cd.sem, n)
                    for g in range(4):
                        last = transpose(ps[:, 2, g * P:(g + 1) * P],
                                         rot_q[:, g, :, :].rearrange("p a b -> p (a b)"), P)
                    last.then_inc(tpe.step("q"), 1)
                    if prompt:
                        pe.wait_ge(ga.sem, ga.at("qT", n))
                        pe.wait_ge(wa.sem, w * len(wa.names))
                        pe.wait_ge(sdv.sem, w * len(sdv.names))
                        for kv in range(2):
                            d = slice(64 * kv, 64 * kv + 64)
                            for g in range(4):
                                last = nc.tensor.matmul(ps[:, 4 + 2 * kv + g // 2, (g % 2) * 256:(g % 2) * 256 + 256],
                                                        s_qT[d, g, :], s_kT[d, :, :].rearrange("p a b -> p (a b)"),
                                                        start=True, stop=True)
                        last.then_inc(wpe.step("s"), 1)
                    else:
                        pe.wait_ge(cache_in, (l + 1) * 32)
                        pe.wait_ge(wa.sem, w * len(wa.names))
                        for b in range(NB):
                            last = transpose(ps[:, 4 + b // 4, (b % 4) * P:(b % 4) * P + P], ck[:, b, :], P)
                        last.then_inc(dpe.step("ckT"), 1)
                        pe.wait_ge(ga.sem, ga.at("qT", n))
                        pe.wait_ge(dd.sem, dd.at("x1", l))
                        pe.wait_ge(da.sem, da.at("ck", l))
                        for b in range(NB):
                            r = slice(32 * (b % 4), 32 * (b % 4) + 32)
                            nc.tensor.matmul(ps[r, 6 + b // 4, 0:WIN], qxs[:, b, :, :, :].rearrange("p a b c -> p (a b c)"),
                                             ckT[:, b, :], start=True, stop=True)
                        for r in range(2):
                            last = nc.tensor.matmul(ps[:, 6 + r, WIN:WIN + ROWS_S],
                                                    qxs[:, 4 * r:4 * r + 4, :, :, :].rearrange("p e a b c -> p (e a b c)"),
                                                    s_kT[:, 0, 0:ROWS_S], start=True, stop=True)
                        last.then_inc(dpe.step("s"), 1)
                    pe.wait_ge(ga.sem, ga.at("kTr", n))
                    pe.wait_ge(rd.sem, rd.at("qi", n))
                    nc.tensor.matmul(ps[:, 3, :], r_kT[:], r_qx[:, :, :].rearrange("p a b -> p (a b)"),
                                     start=True, stop=True).then_inc(mpe.step("ret"), 1)
                    for half, (first, some) in enumerate((("l3", range(4)), ("l6", range(4, NLEV)))):
                        pe.wait_ge(gp.sem, gp.at(first, n))
                        if prompt:
                            pe.wait_ge(wd.sem, wd.at("s", w))
                        elif half == 0:
                            pe.wait_ge(da.sem, da.at("ck", l))
                        else:
                            pe.wait_ge(dd.sem, dd.at("s", l))
                        for i in some:
                            h2 = 2 * HALVES[i]
                            for pr in range(2):
                                for j in range(2):
                                    d = slice(64 * j, 64 * j + 64)
                                    rhs = lev_x[d, i, pr, :].rearrange("p (k w) -> p k w", w=h2)[:, :, h2 // 2:h2]
                                    at = pr * 256 + (i % 4) * 64
                                    last = nc.tensor.matmul(ps[:, 4 + 2 * half + j, at:at + 64], lev_x[d, i, pr, :], rhs,
                                                            start=True, stop=True)
                        if half == 0:
                            last.then_inc(mpe.step("lev0"), 1)
                    pe.wait_ge(gd.sem, gd.at("p", n))
                    for pr in range(2):
                        last = nc.tensor.matmul(ps[:, 6, pr * 256 + 192:pr * 256 + 194], g_p[:, pr, :], cst("sel"),
                                                start=True, stop=True)
                    last.then_inc(mpe.step("lev1"), 1)
                    if prompt:
                        for half in range(2):
                            pe.wait_ge(wa.sem, wa.at("e7" if half else "e3", w))
                            pe.wait_ge(hd.sem, hd.at("c6" if half else "c3", n))
                            for e in range(8 * half, 8 * half + 8):
                                last = transpose(ps[:, 4 + e // 4, (e % 4) * P:(e % 4) * P + P],
                                                 prob[:, e // 2, (e % 2) * P:(e % 2) * P + P], P)
                            last.then_inc(wpe.step(f"T{half}"), 1)
                    else:
                        pe.wait_ge(dd.sem, dd.at("p1", l))
                        pe.wait_ge(hd.sem, hd.at("c6", n))
                        for r in range(2):
                            transpose(ps[:, 4, r * P:(r + 1) * P], s_prob[:, r, 0:WIN], P)
                        for r in range(2):
                            last = transpose(ps[0:ROWS_S, 4, (2 + r) * P:(3 + r) * P], s_prob[:, r, WIN:WIN + ROWS_S], P)
                        last.then_inc(dpe.step("T"), 1)
                    pe.wait_ge(gp.sem, gp.at("kst", n))
                    pe.wait_ge(rd.sem, rd.at("a", n))
                    for j in range(2):
                        last = transpose(ps[:, 3, j * P:(j + 1) * P], g_ka[:, j, :], P)
                    last.then_inc(mpe.step("kt"), 1)
                    if prompt:
                        pe.wait_ge(wa.sem, wa.at("T", w))
                        pe.wait_ge(wd.sem, wd.at("T", w))
                        pe.wait_ge(rp.sem, rp.at("v", n))
                        for kv in range(2):
                            for g in range(4):
                                e = (kv * 4 + g) * 2
                                at = (g * 2 + kv) * 64
                                for s in range(2):
                                    last = nc.tensor.matmul(ps[:, 1, at:at + 64], probT[:, e + s, :],
                                                            s_v[:, s, 64 * kv:64 * kv + 64], start=(s == 0), stop=(s == 1))
                        last.then_inc(wpe.step("o"), 1)
                    else:
                        pe.wait_ge(da.sem, da.at("T", l))
                        pe.wait_ge(dd.sem, dd.at("T", l))
                        pe.wait_ge(rp.sem, rp.at("v", n))
                        for b in range(NB):
                            r = slice(32 * (b % 4), 32 * (b % 4) + 32)
                            nc.tensor.matmul(ps[:, 5, 32 * b:32 * b + 32], cv[:, b, :], spT[:, b // 4, r],
                                             start=True, stop=False)
                            last = nc.tensor.matmul(ps[:, 5, 32 * b:32 * b + 32], s_v[0:ROWS_S, 0, :],
                                                    spN[0:ROWS_S, b // 4, r], start=False, stop=True)
                        last.then_inc(dpe.step("o"), 1)
                    pe.wait_ge(ga.sem, ga.at("q", n))
                    pe.wait_ge(gp.sem, gp.at("qe", n))
                    pe.wait_ge(hd.sem, hd.at("c6", n))
                    if prompt:
                        pe.wait_ge(sdv.sem, w * len(sdv.names))
                        pe.wait_ge(zd.sem, zd.at("h", l))
                    else:
                        pe.wait_ge(dp.sem, dp.at("qh1", l))
                        pe.wait_ge(s0_in, (l + 1) * 128)
                    if prompt:
                        nc.tensor.matmul(ps[:, 0, 0:256], r_qi[:], st_r[:], start=True, stop=False)
                    else:
                        for b in range(NB):
                            nc.tensor.matmul(ps[0:rows, 0, 0:256], qm_r[:, b, :], s0_r[:, b, :], start=(b == 0), stop=False)
                    for h in range(4):
                        nc.tensor.matmul(ps[0:rows, 0, 64 * h:64 * h + 64], r_a[0:rows, h, 0:rows],
                                         x[0:rows, RV + 64 * h:RV + 64 * h + 64], start=False, stop=(h == 3))
                    for pr in range(2):
                        c0 = 256 + pr * P
                        if prompt:
                            nc.tensor.matmul(ps[:, 0, c0:c0 + P], g_qe[:, pr, :], st_h[:, pr, :], start=True, stop=False)
                        else:
                            for b in range(NB):
                                nc.tensor.matmul(ps[0:rows, 0, c0:c0 + P], qm_h[:, pr, b, :], s0_h[:, pr, b, :],
                                                 start=(b == 0), stop=False)
                        for j in range(2):
                            last = nc.tensor.matmul(ps[0:rows, 0, c0 + 64 * j:c0 + 64 * j + 64],
                                                    hg_a[0:rows, 2 * j + pr, 0:rows],
                                                    x[0:rows, HI + (c0 - 256) + 64 * j:HI + (c0 - 256) + 64 * j + 64],
                                                    start=False, stop=(j == 1))
                    last.then_inc(mpe.step("o"), 1)
                    pe.wait_ge(rp.sem, rp.at("kd", n))
                    pe.wait_ge(hd.sem, hd.at("kt", n))
                    if prompt:
                        nc.tensor.matmul(ps[:, 2, 0:256], r_kd[:, :, :].rearrange("p a b -> p (a b)"),
                                         x[:, RV:RV + 256], start=True, stop=True)
                        for pr in range(2):
                            last = nc.tensor.matmul(ps[:, 2, 256 + pr * P:256 + (pr + 1) * P], g_kt[:, pr, :],
                                                    x[:, HI + pr * P:HI + (pr + 1) * P], start=True, stop=True)
                        last.then_inc(mpe.step("st"), 1)
                    else:
                        pe.wait_ge(dp.sem, dp.at("ks1", l))
                        pe.wait_ge(dd.sem, dd.at("o1", l))
                        for b in range(NB):
                            last = nc.tensor.matmul(ps[:, 4 + b // 2, (b % 2) * 256:(b % 2) * 256 + 256], kdm[0:rows, b, :],
                                                    x[0:rows, RV:RV + 256], start=True, stop=True)
                        last.then_inc(mpe.step("st"), 1)
                        pe.wait_ge(dd.sem, dd.at("hm", l))
                        for pr in range(2):
                            for b in range(NB):
                                last = nc.tensor.matmul(ps[:, 4 + 2 * pr + b // 4, (b % 4) * P:(b % 4) * P + P],
                                                        ksm[0:rows, pr, b, :], x[0:rows, HI + pr * P:HI + (pr + 1) * P],
                                                        start=True, stop=True)
                        last.then_inc(dpe.step("st_h"), 1)
                    pe.wait_ge(md.sem, md.at("rh", n))
                    apart(pe)
                    if prompt:
                        pe.wait_ge(sdv.sem, sdv.at("h3", w))
                    for k in range(4):
                        last = transpose(ps[:, 2, k * P:k * P + rows], cat[0:rows, k * P:(k + 1) * P], rows)
                        if k == 2 and not prompt:
                            last.then_inc(cpe.step("T0"), 1)
                    if prompt:
                        last.then_inc(cpe.step("T0"), 1)
                        pe.wait_ge(wd.sem, wd.at("o", w))
                        for k in range(4):
                            last = transpose(ps[:, 3, k * P:(k + 1) * P], cat[:, 512 + k * P:512 + (k + 1) * P], P)
                    last.then_inc(cpe.step("T1"), 1)

                with pe.Fori(0, CHUNKS // 2) as i:
                    for p in range(2):
                        chunk(l * TILES + i * 2 + p, l * CHUNKS + i * 2 + p, p, P, l * (5 - p) + i + 1)
                chunk(l * TILES + CHUNKS, (l + 1) * CHUNKS, 0, ROWS_S, (l + 1) * 5)
                barrier(pe, phase(l, 1))

                with pe.Fori(0, KT // 2) as i:
                    for q in range(2):
                        J = l * KT + i * 2 + q
                        pe.wait_ge(wo_hi_done, J + 1)
                        pe.wait_ge(wo_lo_done, J + 1)
                        for c in range(TCH):
                            pe.wait_ge(out_free, J * TCH + (c + 1))
                            tok = slice(c * NCH, (c + 1) * NCH)
                            for k in range(KT):
                                last = three(ps[:, c, 0:NCH], wo_hi[q][:, k, :], wo_lo[q][:, k, :],
                                             u_hi[:, k, tok], u_lo[:, k, tok], k == 0, k == KT - 1)
                            last.then_inc(out_ready, 1)
                barrier(pe, phase(l, 2))

                def norm_tiles(which):
                    base = (l * 2 + which) * TILES

                    def back(t, p, rows):
                        n = base + t
                        pe.wait_ge(na.sem, na.at("stage", n))
                        pe.wait_ge(nd.sem, (n - p) * len(nd.names))
                        for k in range(KT):
                            last = transpose(ps[0:rows, 2 * p + k // 4, (k % 4) * P:(k % 4 + 1) * P],
                                             stage[:, k, 0:rows], P)
                        last.then_inc(npe.step("T"), 1)

                    def again(t, p, rows):
                        pe.wait_ge(npl.sem, npl.at("b", base + t))
                        split_tile(base + TILES + t, p, rows)

                    with pe.Fori(0, CHUNKS // 2) as i:
                        for p in range(2):
                            back(i * 2 + p, p, P)
                        for p in range(2):
                            again(i * 2 + p, p, P)
                    back(CHUNKS, 0, ROWS_S)
                    again(CHUNKS, 0, ROWS_S)

                norm_tiles(0)
                barrier(pe, phase(l, 3))

                def up(b, q):
                    B = l * FBLOCKS + b
                    pe.wait_ge(wu_hi_done, B + 1)
                    pe.wait_ge(wu_lo_done, B + 1)
                    for f in range(2):
                        for c in range(TCH):
                            pe.wait_ge(up_free, B * 6 + (f * TCH + c + 1))
                            tok = slice(c * NCH, (c + 1) * NCH)
                            cols = slice(f * P, (f + 1) * P)
                            for k in range(KT):
                                last = three(ps[:, c, 0:NCH], wu_hi[:, k, cols], wu_lo[:, k, cols],
                                             v_hi[:, k, tok], v_lo[:, k, tok], k == 0, k == KT - 1)
                            last.then_inc(up_ready, 1)

                def down(b, q):
                    B = l * FBLOCKS + b
                    pe.wait_ge(wd_hi_done, B + 1)
                    pe.wait_ge(wd_lo_done, B + 1)
                    pe.wait_ge(hid_lo_done, (B + 1) * 6)
                    for d in range(KT):
                        for c in range(TCH):
                            pe.wait_ge(down_free, B * (KT * TCH) + (d * TCH + c + 1))
                            tok = slice(c * NCH, (c + 1) * NCH)
                            cols = slice(d * P, (d + 1) * P)
                            for f in range(2):
                                last = three(ps[:, 3 + c, 0:NCH], wd_hi[:, f, cols], wd_lo[:, f, cols],
                                             hid_hi[q][:, f, tok], hid_lo[q][:, f, tok], f == 0, f == 1)
                            last.then_inc(down_ready, 1)

                up(0, 0)
                with pe.Fori(0, FBLOCKS // 2 - 1) as i:
                    for q in range(2):
                        up(i * 2 + (q + 1), 1 - q)
                        down(i * 2 + q, q)
                up(FBLOCKS - 1, 1)
                down(FBLOCKS - 2, 0)
                down(FBLOCKS - 1, 1)
                barrier(pe, phase(l, 4))
                norm_tiles(1)
                barrier(pe, phase(l, 5))

        @block.scalar
        def _(act):
            nc.scalar.preload_act_table_set("natural_log_exp_and_others")
            act.sem_inc(proj_free, 3)
            copy = nc.scalar.copy
            dest = (u_hi, v_hi)

            def split_tile(m, t, p, rows, out):
                act.wait_ge(spe.sem, spe.at("T", m))
                copy(out[:, :, bass.ds(t * P, rows)],
                     ps[:, 4 + 2 * p:6 + 2 * p, :].rearrange("p b (k c) -> p (b k) c", c=P)[:, :, 0:rows])\
                    .then_inc(sa.step("hi"), 1)

            act.wait_ge(lbd.sem, 3)
            nc.scalar.activation(lb_exp[:], lb_raw[:], ACT.Exp).then_inc(lba.step("exp"), 1)
            for t in range(TILES):
                split_tile(t, t, t % 2, tile_rows(t), u_hi)
            barrier(act, 1)

            with act.Fori(0, DEPTH) as l:
                def split_wi(g, q, free):
                    G = l * GROUPS + g
                    act.wait_ge(wi_in, (G + 1) * 16)
                    if free:
                        act.wait_ge(proj_ready, (G - 1) * TILES)
                    copy(wi_hi[q][:], wi_raw[:]).then_inc(wi_hi_done, 1)

                def evacuate(g, q, i):
                    G = l * GROUPS + g
                    for t in range(TILES):
                        rows = tile_rows(t)
                        act.wait_ge(proj_ready, G * TILES + (t + 1))
                        act.wait_ge(h_stored[t % 3], (G * 3 + t // 3) * 16)
                        copy(h_out[t % 3][0:rows, :], ps[0:rows, t % 3, 0:GROUP]).then_inc(proj_free, 1)

                split_wi(0, 0, False)
                split_wi(1, 1, False)
                with act.Fori(0, GROUPS // 2 - 1) as i:
                    for q in range(2):
                        evacuate(i * 2 + q, q, i)
                        split_wi(i * 2 + (q + 2), q, True)
                evacuate(GROUPS - 2, 0, 0)
                evacuate(GROUPS - 1, 1, 0)
                barrier(act, phase(l, 0))

                def chunk(n, w, p, t, rows):
                    prompt = rows == P
                    act.wait_ge(gd.sem, gd.at("clip", n))
                    nc.scalar.activation(g_e[:], g_e[:], ACT.Exp).then_inc(ga.step("e"), 1)
                    act.wait_ge(tpe.sem, tpe.at("h", n))
                    act.wait_ge(gp.sem, n * len(gp.names))
                    act.wait_ge(gd.sem, gd.at("clip", n))
                    copy(g_q[:], ps[:, 0, 256:512].rearrange("p (a b) -> p a b", a=2)).then_inc(ga.step("q"), 1)
                    act.wait_ge(tpe.sem, tpe.at("r", n))
                    act.wait_ge(rd.sem, rd.at("qi", n))
                    copy(r_kT[:], ps[:, 1, P:2 * P]).then_inc(ga.step("kTr"), 1)
                    copy(s_kT[:, p, :], ps[:, 1, 2 * P:3 * P]).then_inc(ga.step("kTs"), 1)
                    act.wait_ge(tpe.sem, tpe.at("q", n))
                    copy(s_qT[:], ps[:, 2, :].rearrange("p (a b) -> p a b", a=4)).then_inc(ga.step("qT"), 1)
                    act.wait_ge(gd.sem, gd.at("f1", n))
                    nc.scalar.activation(g_f[:], g_f[:], ACT.Ln).then_inc(ga.step("f"), 1)
                    if not prompt:
                        act.wait_ge(dpe.sem, dpe.at("ckT", l))
                        copy(ckT[:], ps[:, 4:6, :].rearrange("p b (k c) -> p (b k) c", c=P)).then_inc(da.step("ck"), 1)
                    act.wait_ge(gd.sem, gd.at("b1", n))
                    act.wait_ge(sdv.sem, w * len(sdv.names))
                    nc.scalar.activation(g_eb[:], g_b[:], ACT.Exp).then_inc(ga.step("eb"), 1)
                    act.wait_ge(gd.sem, gd.at("al6", n))
                    nc.scalar.activation(lev_e[:], lev_e[:], ACT.Exp).then_inc(ga.step("E"), 1)
                    nc.scalar.activation(g_ka[:], g_ka[:], ACT.Exp).then_inc(ga.step("ka"), 1)
                    act.wait_ge(rp.sem, rp.at("gc", n))
                    nc.scalar.activation(gate_e[:], gate_e[:], ACT.Exp, scale=-1.0).then_inc(ga.step("eg"), 1)
                    if prompt:
                        act.wait_ge(wd.sem, wd.at("sk", w))
                        for h in range(8):
                            nc.scalar.activation(prob[:, h, :], prob[:, h, :], ACT.Exp, bias=nm[:, h:h + 1], scale=0.125,
                                                 accum_out=ssum[:, h:h + 1]).then_inc(wa.step(f"e{h}"), 1)
                        nc.scalar.activation(esk[:], sk[:], ACT.Exp).then_inc(wa.step("sk"), 1)
                        act.wait_ge(wpe.sem, wpe.at("T0", w))
                        copy(probT[:, 0:8, :], ps[:, 4:6, :].rearrange("p b (k c) -> p (b k) c", c=P))\
                            .then_inc(wa.step("T"), 1)
                    else:
                        act.wait_ge(dd.sem, dd.at("sk", l))
                        for r in range(2):
                            nc.scalar.activation(s_prob[:, r, :], s_prob[:, r, :], ACT.Exp, bias=nm[:, r:r + 1], scale=0.125,
                                                 accum_out=ssum[:, r:r + 1]).then_inc(da.step(f"e{r}"), 1)
                        nc.scalar.activation(esk[:, 0:2], sk[:, 0:2], ACT.Exp).then_inc(da.step("sk"), 1)
                        act.wait_ge(dpe.sem, dpe.at("T", l))
                        act.wait_ge(dd.sem, dd.at("T", l))
                        copy(spN[0:rows, :, :], ps[0:rows, 4, 256:512].rearrange("p (a b) -> p a b", a=2))\
                            .then_inc(da.step("T"), 1)
                        act.wait_ge(dpe.sem, dpe.at("o", l))
                        for kv in range(2):
                            d = slice(64 * kv, 64 * kv + 64)
                            src = ps[d, 5, 0:256].rearrange("p (b kv g l) -> p kv g b l", b=NB, kv=2, g=4)[:, kv]
                            copy(u_hi[d, 4:8, SEQ:TOK].rearrange("p g (b l) -> p g b l", b=NB), src)\
                                .then_inc(da.step(f"o{kv}"), 1)
                    act.wait_ge(mpe.sem, mpe.at("o", n))
                    act.wait_ge(md.sem, n * len(md.names))
                    nc.scalar.activation(rms_sq[0:rows], ps[0:rows, 0, :].rearrange("p (a b) -> p a b", a=8), ACT.Square)\
                        .then_inc(ma.step("sq"), 1)
                    act.wait_ge(md.sem, md.at("ms", n))
                    nc.scalar.activation(rms_l[0:rows], rms_v[0:rows], ACT.Ln).then_inc(ma.step("ln"), 1)
                    act.wait_ge(ma.sem, ma.at("ln", n))
                    nc.scalar.activation(rms[0:rows], rms_l[0:rows], ACT.Exp, scale=-0.5).then_inc(ma.step("r"), 1)
                    act.wait_ge(cpe.sem, cpe.at("T1", n))
                    if prompt:
                        copy(u_hi[:, :, bass.ds(t * P, P)], ps[:, 2:4, :].rearrange("p b (k c) -> p (b k) c", c=P))\
                            .then_inc(ca.step("hi"), 1)
                    else:
                        copy(u_hi[:, 0:4, SEQ:TOK], ps[:, 2, :].rearrange("p (k c) -> p k c", c=P)[:, :, 0:rows])\
                            .then_inc(ca.step("hi"), 1)

                with act.Fori(0, CHUNKS // 2) as i:
                    for p in range(2):
                        chunk(l * TILES + i * 2 + p, l * CHUNKS + i * 2 + p, p, i * 2 + p, P)
                chunk(l * TILES + CHUNKS, (l + 1) * CHUNKS, 0, CHUNKS, ROWS_S)
                barrier(act, phase(l, 1))

                def split_wo(j, q, free):
                    J = l * KT + j
                    act.wait_ge(wo_in, (J + 1) * 48)
                    if free:
                        act.wait_ge(out_ready, (J - 1) * TCH)
                    copy(wo_hi[q][:], wo_raw[:]).then_inc(wo_hi_done, 1)

                split_wo(0, 0, False)
                split_wo(1, 1, False)
                with act.Fori(0, KT // 2 - 1) as i:
                    for q in range(2):
                        split_wo(i * 2 + (q + 2), q, True)
                barrier(act, phase(l, 2))

                def norm_tiles(which):
                    base = (l * 2 + which) * TILES
                    out = (v_hi, u_hi)[which]

                    def back(t, p, rows):
                        n = base + t
                        act.wait_ge(npe.sem, n)
                        copy(stage[:, :, 0:rows], acc[:, :, bass.ds(t * P, rows)]).then_inc(na.step("stage"), 1)

                    def root(t, p, rows):
                        n = base + t
                        rs = slice(0, rows)
                        act.wait_ge(nd.sem, nd.at("var", n))
                        nc.scalar.activation(logv[rs, p:p + 1], var[rs, p:p + 1], ACT.Ln).then_inc(nr.step("ln"), 1)
                        act.wait_ge(nr.sem, nr.at("ln", n))
                        nc.scalar.activation(rstd[rs, p:p + 1], logv[rs, p:p + 1], ACT.Exp, scale=-0.5)\
                            .then_inc(nr.step("r"), 1)

                    with act.Fori(0, CHUNKS // 2) as i:
                        for p in range(2):
                            back(i * 2 + p, p, P)
                        for p in range(2):
                            root(i * 2 + p, p, P)
                        for p in range(2):
                            split_tile(base + TILES + i * 2 + p, i * 2 + p, p, P, out)
                    back(CHUNKS, 0, ROWS_S)
                    root(CHUNKS, 0, ROWS_S)
                    split_tile(base + TILES + CHUNKS, CHUNKS, 0, ROWS_S, out)

                norm_tiles(0)
                barrier(act, phase(l, 3))

                def split_wu(b):
                    B = l * FBLOCKS + b
                    act.wait_ge(wu_in, (B + 1) * 16)
                    act.wait_ge(up_ready, B * 6)
                    copy(wu_hi[:], wu_raw[:]).then_inc(wu_hi_done, 1)

                def split_wd(b):
                    B = l * FBLOCKS + b
                    act.wait_ge(wd_in, (B + 1) * 16)
                    act.wait_ge(down_ready, B * (KT * TCH))
                    copy(wd_hi[:], wd_raw[:]).then_inc(wd_hi_done, 1)

                def hidden(b, q):
                    B = l * FBLOCKS + b
                    def high(f, c):
                        act.wait_ge(sq_done, B * 6 + (f * TCH + c + 1))
                        copy(hid_hi[q][:, f, c * NCH:(c + 1) * NCH], sq[c][:]).then_inc(hid_hi_done, 1)

                    units = [(f, c) for f in range(2) for c in range(TCH)]
                    for u, (f, c) in enumerate(units):
                        act.wait_ge(up_ready, B * 6 + (u + 1))
                        nc.scalar.activation(relu[c][:], ps[:, c, 0:NCH], ACT.Relu).then_inc(up_free, 1)
                        if u:
                            high(*units[u - 1])
                    high(*units[-1])

                split_wu(0)
                hidden(0, 0)
                with act.Fori(0, FBLOCKS // 2 - 1) as i:
                    for q in range(2):
                        split_wu(i * 2 + (q + 1))
                        split_wd(i * 2 + q)
                        hidden(i * 2 + (q + 1), 1 - q)
                split_wu(FBLOCKS - 1)
                split_wd(FBLOCKS - 2)
                hidden(FBLOCKS - 1, 1)
                split_wd(FBLOCKS - 1)
                barrier(act, phase(l, 4))
                norm_tiles(1)
                barrier(act, phase(l, 5))

        @block.vector
        def _(dve):
            v = nc.vector
            dve.sem_inc(out_free, 3)
            dve.sem_inc(up_free, 3)
            dve.sem_inc(down_free, 3)

            def split_tile(m, t, p, rows, hi, lo):
                dve.wait_ge(sa.sem, sa.at("hi", m))
                tok = bass.ds(t * P, rows)
                v.tensor_tensor(lo[:, :, tok], ps[:, 4 + 2 * p:6 + 2 * p, :]
                                .rearrange("p b (k c) -> p (b k) c", c=P)[:, :, 0:rows], hi[:, :, tok], ALU.subtract)\
                    .then_inc(sd.step("lo"), 1)

            def newton(r, x, t, dve, S, n):
                v.tensor_tensor(t, r, r, ALU.mult).then_inc(S.step("n0"), 1)
                dve.wait_ge(S.sem, S.at("n0", n))
                v.scalar_tensor_tensor(out=t, in0=t, scalar=-0.5, in1=x, op0=ALU.mult, op1=ALU.mult)\
                    .then_inc(S.step("n1"), 1)
                dve.wait_ge(S.sem, S.at("n1", n))
                v.scalar_tensor_tensor(out=r, in0=t, scalar=1.5, in1=r, op0=ALU.add, op1=ALU.mult)\
                    .then_inc(S.step("rstd"), 1)

            dve.wait_ge(const_in, 48)
            v.tensor_tensor(lb_tmp[:, 0:2], lb_raw[:, 0, :], lb_raw[:, 1, :], ALU.max).then_inc(lbd.step("max"), 1)
            dve.wait_ge(lbd.sem, 1)
            v.tensor_tensor(lb_raw[:, 0, :], lb_raw[:, 0, :], lb_tmp[:, 0:2], ALU.subtract).then_inc(lbd.step("sub0"), 1)
            v.tensor_tensor(lb_raw[:, 1, :], lb_raw[:, 1, :], lb_tmp[:, 0:2], ALU.subtract).then_inc(lbd.step("sub1"), 1)
            dve.wait_ge(lba.sem, 1)
            v.tensor_tensor(lb_tmp[:, 2:4], lb_exp[:, 0, :], lb_exp[:, 1, :], ALU.add).then_inc(lbd.step("sum"), 1)
            dve.wait_ge(lbd.sem, 4)
            v.reciprocal(lb_tmp[:, 2:4], lb_tmp[:, 2:4]).then_inc(lbd.step("inv"), 1)
            dve.wait_ge(lbd.sem, 5)
            v.tensor_tensor(lb_exp[:, 0, :], lb_exp[:, 0, :], lb_tmp[:, 2:4], ALU.mult).then_inc(lbd.step("p0"), 1)
            v.tensor_tensor(lb_exp[:, 1, :], lb_exp[:, 1, :], lb_tmp[:, 2:4], ALU.mult).then_inc(lbd.step("p1"), 1)
            dve.wait_ge(lbd.sem, 7)
            v.tensor_tensor(lb_tmp[:, 0:2], lb_exp[:, 0, :], lb_exp[:, 1, :], ALU.add).then_inc(lbd.step("cum"), 1)
            v.tensor_tensor(lb_all[:, 0, :], lb_exp[:, 0, :], lb_exp[:, 0, :], ALU.subtract).then_inc(lbd.step("lb0"), 1)
            dve.wait_ge(lbd.sem, 8)
            v.tensor_tensor(lb_all[:, 1, :], lb_tmp[:, 0:2], lb_exp[:, 0, :], ALU.subtract).then_inc(lbd.step("lb1"), 1)
            for t in range(TILES):
                split_tile(t, t, t % 2, tile_rows(t), u_hi, u_lo)
            barrier(dve, 1)

            with dve.Fori(0, DEPTH) as l:
                def split_wi(g, q, free):
                    G = l * GROUPS + g
                    dve.wait_ge(wi_hi_done, G + 1)
                    if free:
                        dve.wait_ge(proj_ready, (G - 1) * TILES)
                    v.tensor_tensor(wi_lo[q][:], wi_raw[:], wi_hi[q][:], ALU.subtract).then_inc(wi_lo_done, 1)

                split_wi(0, 0, False)
                split_wi(1, 1, False)
                with dve.Fori(0, GROUPS // 2 - 1) as i:
                    for q in range(2):
                        split_wi(i * 2 + (q + 2), q, True)
                barrier(dve, phase(l, 0))

                v.tensor_copy(lb[:], lb_all[:, bass.ds(l, 1), :].rearrange("p l t -> p (l t)"))\
                    .then_inc(zd.step("lb"), 1)
                dve.wait_ge(zd.sem, zd.at("lb", l))
                v.tensor_scalar(omlb[:], lb[:], -1.0, 1.0, ALU.mult, ALU.add).then_inc(zd.step("omlb"), 1)
                v.memset(st_r[:], 0.0).then_inc(zd.step("r"), 1)
                v.memset(st_h[:], 0.0).then_inc(zd.step("h"), 1)
                v.memset(s_kT[:, 1, :], 0.0).then_inc(zd.step("kT"), 1)
                v.memset(s_v[:, 1, :], 0.0).then_inc(zd.step("v"), 1)
                v.memset(r_qx[:], 0.0).then_inc(zd.step("qx"), 1)
                v.memset(s0_r[:], 0.0).then_inc(zd.step("sr"), 1)
                v.memset(s0_h[:], 0.0).then_inc(zd.step("sh"), 1)
                dve.wait_ge(zd.sem, zd.at("sh", l))
                dve.wait_ge(par_in, (l * 8 + 4) * 16)
                apart(dve)

                def chunk(n, w, p, t, rows):
                    prompt = rows == P
                    var = "" if prompt else "s"
                    dve.wait_ge(tpe.sem, tpe.at("h", n))
                    v.tensor_scalar(g_e[:], ps[:, 0, 0:256].rearrange("p (a b) -> p a b", a=2), -1.0, 80.0,
                                    ALU.mult, ALU.min).then_inc(gd.step("clip"), 1)
                    dve.wait_ge(tpe.sem, tpe.at("r", n))
                    for h in range(4):
                        d = slice(32 * h, 32 * h + 32)
                        v.tensor_copy(r_qx[d, h, :], ps[d, 1, 0:P]).then_inc(rd.step(f"x{h}"), 1)
                    v.tensor_tensor(r_qi[:], ps[:, 1, 0:P], cst("inter" + var), ALU.mult).then_inc(rd.step("qi"), 1)
                    dve.wait_ge(ga.sem, ga.at("e", n))
                    v.tensor_scalar(g_r[:], g_e[:], 1.0, None, ALU.add).then_inc(gd.step("one"), 1)
                    dve.wait_ge(gd.sem, gd.at("one", n))
                    v.reciprocal(g_r[:], g_r[:]).then_inc(gd.step("r"), 1)
                    dve.wait_ge(gd.sem, gd.at("r", n))
                    v.tensor_tensor(g_s[:], g_e[:], g_r[:], ALU.mult).then_inc(gd.step("s"), 1)
                    dve.wait_ge(gd.sem, gd.at("s", n))
                    dve.wait_ge(gp.sem, n * len(gp.names))
                    for j in range(2):
                        v.tensor_scalar(g_k[:, j, :], g_s[:, j, :], omlb[:, j:j + 1], None, ALU.mult)\
                            .then_inc(gd.step(f"k{j}"), 1)
                    for j in range(2):
                        v.scalar_tensor_tensor(out=g_f[:, j, :], in0=g_s[:, j, :], scalar=lb[:, j:j + 1], in1=g_r[:, j, :],
                                               op0=ALU.mult, op1=ALU.add).then_inc(gd.step(f"f{j}"), 1)
                    if prompt:
                        dve.wait_ge(wpe.sem, wpe.at("s", w))
                        v.tensor_tensor(prob[:], ps[:, 4:8, :].rearrange("p b (h s) -> p (b h) s", s=256),
                                        swa_mask[:, p:p + 2, :].rearrange("p a b -> p (a b)").unsqueeze(1)
                                        .broadcast_to([P, 8, 256]), ALU.add).then_inc(wd.step("s"), 1)
                        dve.wait_ge(wd.sem, wd.at("s", w))
                        v.tensor_copy(swa_mask[:, 1, :], cst("band")).then_inc(wd.step("band"), 1)
                        v.tensor_reduce(mx[:], prob[:], axis=AX, op=ALU.max).then_inc(wd.step("mx"), 1)
                        S, L, K, sink = wd, w, 8, sink_b[:]
                    else:
                        v.memset(qxs[:], 0.0).then_inc(dd.step("zx"), 1)
                        dve.wait_ge(ga.sem, ga.at("qT", n))
                        dve.wait_ge(dd.sem, dd.at("zx", l))
                        for kv in range(2):
                            d = slice(64 * kv, 64 * kv + 64)
                            v.tensor_copy(qxs[d, :, kv, :, :],
                                          ps[d, 2, :].rearrange("p (g t) -> p g t", g=4)[:, :, 0:rows]
                                          .rearrange("p g (b l) -> p b g l", b=NB)).then_inc(dd.step(f"x{kv}"), 1)
                        dve.wait_ge(dpe.sem, dpe.at("s", l))
                        v.tensor_tensor(s_prob[:], ps[:, 6:8, 0:WIN + ROWS_S],
                                        cst("smask").rearrange("p (a b) -> p a b", a=2), ALU.add).then_inc(dd.step("s"), 1)
                        dve.wait_ge(dd.sem, dd.at("s", l))
                        v.tensor_reduce(mx[:, 0:2], s_prob[:], axis=AX, op=ALU.max).then_inc(dd.step("mx"), 1)
                        S, L, K, sink = dd, l, 2, sink_r[:, 0:1].broadcast_to([P, 2])
                    dve.wait_ge(S.sem, S.at("mx", L))
                    v.scalar_tensor_tensor(out=m[:, 0:K], in0=mx[:, 0:K], scalar=0.125, in1=sink, op0=ALU.mult,
                                           op1=ALU.max).then_inc(S.step("m"), 1)
                    dve.wait_ge(S.sem, S.at("m", L))
                    v.tensor_scalar(nm[:, 0:K], m[:, 0:K], -1.0, None, ALU.mult).then_inc(S.step("nm"), 1)
                    v.tensor_tensor(sk[:, 0:K], sink, m[:, 0:K], ALU.subtract).then_inc(S.step("sk"), 1)
                    dve.wait_ge(ga.sem, ga.at("f", n))
                    carry = cst("run").broadcast_to([P, P]) if prompt else cst("runs")
                    for j in range(2):
                        v.tensor_tensor_scan(g_b[:, j, :], carry, g_f[:, j, :], 0.0, ALU.mult, ALU.add)\
                            .then_inc(gd.step(f"b{j}"), 1)
                    v.tensor_tensor(g_p[:], g_q[:], g_k[:], ALU.mult).then_inc(gd.step("p"), 1)
                    dve.wait_ge(gd.sem, gd.at("b1", n))
                    if prompt:
                        v.tensor_tensor(g_ka[:], g_b[:, :, P - 1:P].broadcast_to([P, 2, P]), g_b[:], ALU.subtract)\
                            .then_inc(gd.step("ka"), 1)
                    else:
                        gb4 = g_b[:, :, :].rearrange("p a (k w) -> p (a k) w", w=NL)
                        v.tensor_tensor(g_ka[:, :, :].rearrange("p a (k w) -> p (a k) w", w=NL),
                                        gb4[:, :, NL - 1:NL].broadcast_to([P, 2 * P // NL, NL]), gb4, ALU.subtract)\
                            .then_inc(gd.step("ka"), 1)
                    for i, half in enumerate(HALVES):
                        gb = g_b[:, :, :].rearrange("p a (k w) -> p (a k) w", w=2 * half)
                        to = lev_e[:, i, :, :].rearrange("p a (k w) -> p (a k) w", w=2 * half)
                        mid = gb[:, :, half - 1:half].broadcast_to([P, P // half, half])
                        v.tensor_tensor(to[:, :, half:], gb[:, :, half:], mid, ALU.subtract).then_inc(gd.step(f"ar{i}"), 1)
                        v.tensor_tensor(to[:, :, 0:half], mid, gb[:, :, 0:half], ALU.subtract)\
                            .then_inc(gd.step(f"al{i}"), 1)
                    dve.wait_ge(mpe.sem, mpe.at("ret", n))
                    v.tensor_tensor(r_a[:], ps[:, 3, :].rearrange("p (a b) -> p a b", a=4),
                                    cst("dec" + var).rearrange("p (a b) -> p a b", a=4), ALU.mult).then_inc(rd.step("a"), 1)
                    S2 = wa if prompt else da
                    dve.wait_ge(S2.sem, S2.at("sk", L))
                    v.tensor_tensor(den[:, 0:K], ssum[:, 0:K], esk[:, 0:K], ALU.add).then_inc(S.step("den"), 1)
                    dve.wait_ge(S.sem, S.at("den", L))
                    v.reciprocal(rden[:, 0:K], den[:, 0:K]).then_inc(S.step("rden"), 1)
                    dve.wait_ge(S.sem, S.at("rden", L))
                    if not prompt:
                        for r in range(2):
                            v.tensor_scalar(s_prob[:, r, :], s_prob[:, r, :], rden[:, r:r + 1], None, ALU.mult)\
                                .then_inc(dd.step(f"p{r}"), 1)
                    dve.wait_ge(rp.sem, rp.at("g1", n))
                    v.reciprocal(gate_e[:], gate_e[:]).then_inc(md.step("r"), 1)
                    dve.wait_ge(mpe.sem, mpe.at("lev1", n))
                    v.tensor_copy(diag[:, :].rearrange("p (j a) -> p a j", a=2),
                                  ps[:, 6, :].rearrange("p (a c) -> p a c", a=2)[:, :, 192:194]).then_inc(hd.step("diag"), 1)
                    dve.wait_ge(hd.sem, hd.at("diag", n))
                    v.tensor_tensor(hg_a[:], ident.unsqueeze(1).broadcast_to([P, 4, P]),
                                    diag[:, :].unsqueeze(2).broadcast_to([P, 4, P]), ALU.mult).then_inc(hd.step("a"), 1)
                    for i, half in enumerate(HALVES):
                        dve.wait_ge(hd.sem, hd.at(f"c{i - 1}" if i else "a", n))
                        apart(dve)
                        src = ps[:, 4 + 2 * (i // 4):6 + 2 * (i // 4), :].rearrange("p b (a c) -> p (b a) c", a=2)
                        at = (i % 4) * 64
                        v.copy_predicated(hg_a[:, :, :].rearrange("p h (k w) -> p h k w", w=2 * half)[:, :, :, half:],
                                          lev_mask[:, 0 if prompt else 1, i, :].unsqueeze(1).broadcast_to([P, 4, 64])
                                          .rearrange("p h (k w) -> p h k w", w=half),
                                          src[:, :, at:at + 64].rearrange("p h (k w) -> p h k w", w=half))\
                            .then_inc(hd.step(f"c{i}"), 1)
                    if prompt:
                        dve.wait_ge(wpe.sem, wpe.at("T1", w))
                        v.tensor_copy(probT[:, 8:16, :], ps[:, 6:8, :].rearrange("p b (k c) -> p (b k) c", c=P))\
                            .then_inc(wd.step("T"), 1)
                    else:
                        dve.wait_ge(dpe.sem, dpe.at("T", l))
                        v.tensor_copy(spT[:], ps[:, 4, 0:256].rearrange("p (a b) -> p a b", a=2)).then_inc(dd.step("T"), 1)
                    dve.wait_ge(mpe.sem, mpe.at("kt", n))
                    v.tensor_copy(g_kt[:], ps[:, 3, 0:256].rearrange("p (a b) -> p a b", a=2)).then_inc(hd.step("kt"), 1)
                    if prompt:
                        dve.wait_ge(wpe.sem, wpe.at("o", w))
                        v.tensor_tensor(cat[:, 512:1024].rearrange("p (g k d) -> p g k d", g=4, k=2),
                                        ps[:, 1, :].rearrange("p (g k d) -> p g k d", g=4, k=2),
                                        rden[:, :].rearrange("p (k g) -> p g k", k=2).unsqueeze(3)
                                        .broadcast_to([P, 4, 2, 64]), ALU.mult).then_inc(wd.step("o"), 1)
                    else:
                        for kv in range(2):
                            d = slice(64 * kv, 64 * kv + 64)
                            dve.wait_ge(da.sem, da.at(f"o{kv}", l))
                            src = ps[d, 5, 0:256].rearrange("p (b kv g l) -> p kv g b l", b=NB, kv=2, g=4)[:, kv]
                            tok = (d, slice(4, 8), slice(SEQ, TOK))
                            v.tensor_tensor(u_lo[tok].rearrange("p g (b l) -> p g b l", b=NB), src,
                                            u_hi[tok].rearrange("p g (b l) -> p g b l", b=NB), ALU.subtract)\
                                .then_inc(dd.step(f"o{kv}"), 1)
                    dve.wait_ge(ma.sem, ma.at("sq", n))
                    v.tensor_reduce(rms[0:rows], rms_sq[0:rows], axis=AX, op=ALU.add).then_inc(md.step("ss"), 1)
                    dve.wait_ge(md.sem, md.at("ss", n))
                    v.tensor_scalar(rms_v[0:rows], rms[0:rows], 1.0 / 64, RMS_EPS, ALU.mult, ALU.add)\
                        .then_inc(md.step("ms"), 1)
                    dve.wait_ge(ma.sem, ma.at("r", n))
                    newton(rms[0:rows], rms_v[0:rows], rms_t[0:rows], dve, md, n)
                    dve.wait_ge(rp.sem, rp.at("sr", n))
                    v.tensor_tensor(cat[0:rows, 0:512], ps[0:rows, 0, :], gate[0:rows].rearrange("p a b -> p (a b)"),
                                    ALU.mult).then_inc(md.step("rh"), 1)
                    dve.wait_ge(mpe.sem, mpe.at("st", n))
                    for h in range(4):
                        d, c = slice(32 * h, 32 * h + 32), slice(64 * h, 64 * h + 64)
                        if prompt:
                            v.scalar_tensor_tensor(out=st_r[d, c], in0=st_r[d, c], scalar=float(np.exp(P * LG[h])),
                                                   in1=ps[d, 2, c], op0=ALU.mult, op1=ALU.add).then_inc(sdv.step(f"r{h}"), 1)
                        else:
                            add = ps[d, 4:8, :].rearrange("p b (e c) -> p (b e) c", e=2)[:, :, c]
                            v.scalar_tensor_tensor(out=s0_r[d, :, c], in0=s0_r[d, :, c], scalar=float(np.exp(NL * LG[h])),
                                                   in1=add, op0=ALU.mult, op1=ALU.add).then_inc(dd.step(f"r{h}"), 1)
                    if not prompt:
                        last_b = g_eb[:, :, 0:ROWS_S].rearrange("p a (b l) -> p a b l", b=NB)[:, :, :, NL - 1:NL]
                        v.tensor_tensor(s0_h[:], s0_h[:], last_b.broadcast_to([P, 2, NB, P]), ALU.mult)\
                            .then_inc(dd.step("hm"), 1)
                        dve.wait_ge(dd.sem, dd.at("hm", l))
                        dve.wait_ge(dpe.sem, dpe.at("st_h", l))
                    for h in range(4):
                        pr, j = h // 2, h % 2
                        d = slice(64 * j, 64 * j + 64)
                        if prompt:
                            a = 256 + pr * P + 64 * j
                            v.scalar_tensor_tensor(out=st_h[d, pr, d], in0=st_h[d, pr, d], scalar=g_eb[d, pr, P - 1:P],
                                                   in1=ps[d, 2, a:a + 64], op0=ALU.mult, op1=ALU.add)\
                                .then_inc(sdv.step(f"h{h}"), 1)
                        else:
                            add = ps[d, 4 + 2 * pr:6 + 2 * pr, :].rearrange("p b (e c) -> p (b e) c", e=4)[:, :, d]
                            v.tensor_tensor(s0_h[d, pr, :, d], s0_h[d, pr, :, d], add, ALU.add)\
                                .then_inc(dd.step(f"h{h}"), 1)
                    dve.wait_ge(ca.sem, ca.at("hi", n))
                    if prompt:
                        tok = bass.ds(t * P, P)
                        v.tensor_tensor(u_lo[:, :, tok], ps[:, 2:4, :].rearrange("p b (k c) -> p (b k) c", c=P),
                                        u_hi[:, :, tok], ALU.subtract).then_inc(cd.step("lo"), 1)
                    else:
                        v.tensor_tensor(u_lo[:, 0:4, SEQ:TOK],
                                        ps[:, 2, :].rearrange("p (k c) -> p k c", c=P)[:, :, 0:rows],
                                        u_hi[:, 0:4, SEQ:TOK], ALU.subtract).then_inc(cd.step("lo"), 1)

                with dve.Fori(0, CHUNKS // 2) as i:
                    for p in range(2):
                        chunk(l * TILES + i * 2 + p, l * CHUNKS + i * 2 + p, p, i * 2 + p, P)
                chunk(l * TILES + CHUNKS, (l + 1) * CHUNKS, 0, CHUNKS, ROWS_S)
                barrier(dve, phase(l, 1))

                def split_wo(j, q, free):
                    J = l * KT + j
                    dve.wait_ge(wo_hi_done, J + 1)
                    if free:
                        dve.wait_ge(out_ready, (J - 1) * TCH)
                    v.tensor_tensor(wo_lo[q][:], wo_raw[:], wo_hi[q][:], ALU.subtract).then_inc(wo_lo_done, 1)

                def evacuate(j):
                    for c in range(TCH):
                        dve.wait_ge(out_ready, (l * KT + j) * TCH + (c + 1))
                        v.tensor_copy(acc[:, bass.ds(j, 1), c * NCH:(c + 1) * NCH].rearrange("p a b -> p (a b)"),
                                      ps[:, c, 0:NCH]).then_inc(out_free, 1)

                split_wo(0, 0, False)
                split_wo(1, 1, False)
                with dve.Fori(0, KT // 2 - 1) as i:
                    for q in range(2):
                        evacuate(i * 2 + q)
                        split_wo(i * 2 + (q + 2), q, True)
                evacuate(KT - 2)
                evacuate(KT - 1)
                barrier(dve, phase(l, 2))

                def norm_tiles(which):
                    base = (l * 2 + which) * TILES
                    hi, lo = ((v_hi, v_lo), (u_hi, u_lo))[which]

                    def norm(i, q, p, rows):
                        n = base + i * 2 + q
                        rs = slice(0, rows)
                        dve.wait_ge(x_in[p], x_count(l, which, q, i) * 16)
                        dve.wait_ge(npe.sem, npe.at("T", n))
                        v.scalar_tensor_tensor(out=xin[p][rs], in0=xin[p][rs], scalar=ALPHA,
                                               in1=ps[rs, 2 * p:2 * p + 2, :].rearrange("p a b -> p (a b)"),
                                               op0=ALU.mult, op1=ALU.add).then_inc(nd.step("res"), 1)
                        dve.wait_ge(nd.sem, nd.at("res", n))
                        for j in range(2):
                            v.bn_stats(stats[rs, p, j, :], xin[p][rs, 512 * j:512 * j + 512]).then_inc(nd.step(f"st{j}"), 1)
                        dve.wait_ge(nd.sem, nd.at("st1", n))
                        apart(dve)
                        v.bn_aggr(aggr[rs, p, :], stats[rs, p, :, :]).then_inc(nd.step("aggr"), 1)
                        dve.wait_ge(nd.sem, nd.at("aggr", n))
                        v.tensor_scalar(var[rs, p:p + 1], aggr[rs, p, 1:2], LN_EPS, None, ALU.add)\
                            .then_inc(nd.step("var"), 1)
                        dve.wait_ge(nr.sem, nr.at("r", n))
                        newton(rstd[rs, p:p + 1], var[rs, p:p + 1], newt[rs, p:p + 1], dve, nd, n)
                        dve.wait_ge(nd.sem, nd.at("rstd", n))
                        dve.wait_ge(x_out[p], x_count(l, which, q, i) * 16 - 16)
                        dve.wait_ge(spe.sem, spe.at("T", n + TILES - 2))
                        v.tensor_scalar(xn[p][rs], xin[p][rs], aggr[rs, p, 0:1], rstd[rs, p:p + 1],
                                        ALU.subtract, ALU.mult).then_inc(nd.step("xn"), 1)

                    with dve.Fori(0, CHUNKS // 2) as i:
                        for p in range(2):
                            norm(i, p, p, P)
                        for p in range(2):
                            split_tile(base + TILES + i * 2 + p, i * 2 + p, p, P, hi, lo)
                    norm(0, CHUNKS, 0, ROWS_S)
                    split_tile(base + TILES + CHUNKS, CHUNKS, 0, ROWS_S, hi, lo)

                norm_tiles(0)
                barrier(dve, phase(l, 3))

                def hidden(b, q, first=False):
                    B = l * FBLOCKS + b

                    def low(f, c):
                        dve.wait_ge(hid_hi_done, B * 6 + (f * TCH + c + 1))
                        cols = slice(c * NCH, (c + 1) * NCH)
                        v.tensor_tensor(hid_lo[q][:, f, cols], sq[c][:], hid_hi[q][:, f, cols], ALU.subtract)\
                            .then_inc(hid_lo_done, 1)

                    units = [(f, c) for f in range(2) for c in range(TCH)]
                    for u, (f, c) in enumerate(units):
                        dve.wait_ge(up_free, B * 6 + (u + 4))
                        if u >= TCH or not first:
                            dve.wait_ge(hid_lo_done, B * 6 + (u - 2))
                        v.tensor_tensor(sq[c][:], relu[c][:], relu[c][:], ALU.mult).then_inc(sq_done, 1)
                        if u:
                            low(*units[u - 1])
                    low(*units[-1])

                def collect(b):
                    V = (l * FBLOCKS + b) * (KT * TCH)
                    for d in range(KT):
                        for c in range(TCH):
                            dve.wait_ge(down_ready, V + (d * TCH + c + 1))
                            at = acc[:, d, c * NCH:(c + 1) * NCH]
                            v.tensor_tensor(at, ps[:, 3 + c, 0:NCH], at, ALU.add).then_inc(down_free, 1)

                dve.wait_ge(acc_zero, l + 1)
                hidden(0, 0, True)
                with dve.Fori(0, FBLOCKS // 2 - 1) as i:
                    for q in range(2):
                        hidden(i * 2 + (q + 1), 1 - q)
                        collect(i * 2 + q)
                hidden(FBLOCKS - 1, 1)
                collect(FBLOCKS - 2)
                collect(FBLOCKS - 1)
                barrier(dve, phase(l, 4))
                norm_tiles(1)
                barrier(dve, phase(l, 5))

        @block.gpsimd
        def _(pool):
            g_ = nc.gpsimd
            barrier(pool, 1)

            with pool.Fori(0, DEPTH) as l:
                barrier(pool, phase(l, 0))

                def chunk(n, w, p, rows, loads):
                    prompt = rows == P
                    var = "" if prompt else "s"
                    x, tab = hb[p], rt[p]
                    pool.wait_ge(h_in[p], loads * 32)
                    pool.wait_ge(tpe.sem, n * len(tpe.names))
                    if not prompt:
                        pool.wait_ge(kv_out, (l + 1) * 32)
                    xr = x[:, RQ:RQ + 256].rearrange("p (h s i) -> p h s i", h=8, s=2)
                    ra = rope_a[:, :].rearrange("p (h s i) -> p h s i", h=8, s=2)
                    rb = rope_b[:, :].rearrange("p (h s i) -> p h s i", h=8, s=2)
                    rr = rot_r[:, :].rearrange("p (h s i) -> p h s i", h=8, s=2)
                    g_.tensor_tensor(rope_a[:, :].rearrange("p (h i) -> p h i", i=16),
                                     x[:, RQ:RQ + 256].rearrange("p (h i) -> p h i", i=16),
                                     tab[:, 0:16].unsqueeze(1).broadcast_to([P, 16, 16]), ALU.mult)\
                        .then_inc(rp.step("ra"), 1)
                    sin = tab[:, 16:32].unsqueeze(1).broadcast_to([P, 8, 16])
                    g_.tensor_tensor(rb[:, :, 0, :], xr[:, :, 1, :], sin, ALU.mult).then_inc(rp.step("rb0"), 1)
                    g_.tensor_tensor(rb[:, :, 1, :], xr[:, :, 0, :], sin, ALU.mult).then_inc(rp.step("rb1"), 1)
                    pool.wait_ge(rp.sem, rp.at("rb1", n))
                    g_.tensor_tensor(rr[:, :, 0, :], ra[:, :, 0, :], rb[:, :, 0, :], ALU.subtract).then_inc(rp.step("r0"), 1)
                    g_.tensor_tensor(rr[:, :, 1, :], ra[:, :, 1, :], rb[:, :, 1, :], ALU.add).then_inc(rp.step("r1"), 1)
                    xs = x[:, SQ:SQ + 640].rearrange("p (h d) -> p h d", d=64)
                    cos = tab[:, 32:40].unsqueeze(1).broadcast_to([P, 10, 8])
                    sin = tab[:, 40:48].unsqueeze(1).broadcast_to([P, 10, 8])
                    g_.tensor_tensor(rope_sa[:, :, :, :],
                                     xs[:, :, 0:16].rearrange("p h (s i) -> p h s i", s=2),
                                     tab[:, 32:40].unsqueeze(1).unsqueeze(1).broadcast_to([P, 10, 2, 8]), ALU.mult)\
                        .then_inc(rp.step("sa"), 1)
                    g_.tensor_tensor(rope_sb[:, :, 0, :], xs[:, :, 8:16], sin, ALU.mult).then_inc(rp.step("sb0"), 1)
                    g_.tensor_tensor(rope_sb[:, :, 1, :], xs[:, :, 0:8], sin, ALU.mult).then_inc(rp.step("sb1"), 1)
                    pool.wait_ge(rp.sem, rp.at("sb1", n))
                    for s, op in ((0, ALU.subtract), (1, ALU.add)):
                        g_.tensor_tensor(rot_q[:, :, :, 8 * s:8 * s + 8].rearrange("p g k d -> p k g d"),
                                         rope_sa[:, 0:8, s, :].rearrange("p (k g) d -> p k g d", k=2),
                                         rope_sb[:, 0:8, s, :].rearrange("p (k g) d -> p k g d", k=2), op)\
                            .then_inc(rp.step(f"q{s}"), 1)
                    for s, op in ((0, ALU.subtract), (1, ALU.add)):
                        g_.tensor_tensor(rot_k[:, :, 8 * s:8 * s + 8], rope_sa[:, 8:10, s, :], rope_sb[:, 8:10, s, :], op)\
                            .then_inc(rp.step(f"k{s}"), 1)
                    g_.tensor_copy(rot_q[:, :, :, 16:64].rearrange("p g k d -> p k g d"),
                                   x[:, SQ:SK].rearrange("p (k g d) -> p k g d", k=2, g=4)[:, :, :, 16:64])\
                        .then_inc(rp.step("qc"), 1)
                    g_.tensor_copy(rot_k[:, :, 16:64], x[:, SK:SV].rearrange("p (k d) -> p k d", k=2)[:, :, 16:64])\
                        .then_inc(rp.step("kc"), 1)
                    gates = x[:, RG:RG + 2048].rearrange("p (a c) -> p a c", a=2)[:, :, 0:256]
                    pool.wait_ge(md.sem, n * len(md.names))
                    apart(pool)
                    g_.tensor_scalar(gate_e[:, 0, :], x[:, RG:RG + 256], -80.0, None, ALU.max)
                    g_.tensor_scalar(gate_e[:, 1, :], x[:, HGT:HGT + 256], -80.0, None, ALU.max)\
                        .then_inc(rp.step("gc"), 1)
                    pool.wait_ge(mpe.sem, n * len(mpe.names))
                    g_.tensor_tensor(r_kd[:], rot_r[:, P:2 * P].rearrange("p (h d) -> p h d", h=4),
                                     cst("kdec" + var).unsqueeze(2).broadcast_to([P, 4, 32]), ALU.mult)\
                        .then_inc(rp.step("kd"), 1)
                    pool.wait_ge(wpe.sem, w * len(wpe.names))
                    apart(pool)
                    g_.tensor_copy(s_v[:, p, :], x[:, SV:SV + P]).then_inc(rp.step("v"), 1)
                    pool.wait_ge(ga.sem, ga.at("eb", n))
                    g_.tensor_tensor(g_qe[:], g_q[:], g_eb[:], ALU.mult).then_inc(gp.step("qe"), 1)
                    pool.wait_ge(ga.sem, ga.at("ka", n))
                    g_.tensor_tensor(g_ka[:], g_k[:], g_ka[:], ALU.mult).then_inc(gp.step("kst"), 1)
                    for i, half in enumerate(HALVES):
                        for side, src, cols in (("r", g_q, slice(half, 2 * half)), ("l", g_k, slice(0, half))):
                            def at(a):
                                return a.rearrange("p a (k w) -> p (a k) w", w=2 * half)[:, :, cols]
                            g_.tensor_tensor(at(lev_x[:, i, :, :]), at(lev_e[:, i, :, :]), at(src[:, :, :]), ALU.mult)\
                                .then_inc(gp.step(f"{side}{i}"), 1)
                    pool.wait_ge(ga.sem, ga.at("eg", n))
                    apart(pool)
                    g_.tensor_scalar(gate_e[:], gate_e[:], 1.0, None, ALU.add).then_inc(rp.step("g1"), 1)
                    if not prompt:
                        pool.wait_ge(rd.sem, rd.at("qi", n))
                        bm = cst("bm").rearrange("p (b t) -> p b t", b=NB)
                        g_.tensor_tensor(qm_r[:], r_qi[:, 0:rows].unsqueeze(1).broadcast_to([P, NB, rows]), bm, ALU.mult)\
                            .then_inc(dp.step("qr"), 1)
                        pool.wait_ge(gp.sem, gp.at("qe", n))
                        for j in range(2):
                            g_.tensor_tensor(qm_h[:, j], g_qe[:, j, 0:rows].unsqueeze(1).broadcast_to([P, NB, rows]), bm,
                                             ALU.mult).then_inc(dp.step(f"qh{j}"), 1)
                        tb = cst("tb")[0:rows].unsqueeze(2).broadcast_to([rows, NB, P])
                        pool.wait_ge(rp.sem, rp.at("kd", n))
                        g_.tensor_tensor(kdm[0:rows], r_kd[0:rows].rearrange("p a b -> p (a b)").unsqueeze(1)
                                         .broadcast_to([rows, NB, P]), tb, ALU.mult).then_inc(dp.step("kd"), 1)
                        pool.wait_ge(hd.sem, hd.at("kt", n))
                        for j in range(2):
                            g_.tensor_tensor(ksm[0:rows, j], g_kt[0:rows, j, :].unsqueeze(1).broadcast_to([rows, NB, P]),
                                             tb, ALU.mult).then_inc(dp.step(f"ks{j}"), 1)
                    pool.wait_ge(md.sem, md.at("r", n))
                    g_.tensor_tensor(gate[:, 0], x[:, RG:RG + 256], gate_e[:, 0], ALU.mult)
                    g_.tensor_tensor(gate[:, 1], x[:, HGT:HGT + 256], gate_e[:, 1], ALU.mult).then_inc(rp.step("sg"), 1)
                    pool.wait_ge(rp.sem, rp.at("sg", n))
                    hg = gate[:, 1].rearrange("p (h d) -> p h d", h=4)
                    g_.tensor_tensor(hg, hg, hg_w[:, :].unsqueeze(1).broadcast_to([P, 4, 64]), ALU.mult)\
                        .then_inc(rp.step("sw"), 1)
                    pool.wait_ge(rp.sem, rp.at("sw", n))
                    pool.wait_ge(md.sem, md.at("rstd", n))
                    both = gate[0:rows].rearrange("p a (h d) -> p (a h) d", h=4)
                    g_.tensor_tensor(both, both, rms[0:rows].unsqueeze(2).broadcast_to([rows, 8, 64]), ALU.mult)\
                        .then_inc(rp.step("sr"), 1)

                pool.wait_ge(par_in, (l * 8 + 4) * 16)
                apart(pool)
                with pool.Fori(0, CHUNKS // 2) as i:
                    for p in range(2):
                        chunk(l * TILES + i * 2 + p, l * CHUNKS + i * 2 + p, p, P, l * (5 - p) + i + 1)
                chunk(l * TILES + CHUNKS, (l + 1) * CHUNKS, 0, ROWS_S, (l + 1) * 5)
                barrier(pool, phase(l, 1))
                barrier(pool, phase(l, 2))

                def norm_tiles(which):
                    base = (l * 2 + which) * TILES
                    pool.wait_ge(par_in, (l * 8 + (6 + 2 * which)) * 16)
                    apart(pool)

                    def scale(n, p, rows):
                        rs = slice(0, rows)
                        pool.wait_ge(nd.sem, nd.at("xn", n))
                        g_.tensor_tensor(xn[p][rs], xn[p][rs], ln_g[rs], ALU.mult).then_inc(npl.step("g"), 1)
                        pool.wait_ge(npl.sem, npl.at("g", n))
                        g_.tensor_tensor(xn[p][rs], xn[p][rs], ln_b[rs], ALU.add).then_inc(npl.step("b"), 1)

                    with pool.Fori(0, CHUNKS // 2) as i:
                        for p in range(2):
                            scale(base + i * 2 + p, p, P)
                    scale(base + CHUNKS, 0, ROWS_S)

                norm_tiles(0)
                barrier(pool, phase(l, 3))

                g_.memset(acc[:], 0.0).then_inc(acc_zero, 1)

                def split_wu(b):
                    B = l * FBLOCKS + b
                    pool.wait_ge(wu_hi_done, B + 1)
                    g_.tensor_tensor(wu_lo[:], wu_raw[:], wu_hi[:], ALU.subtract).then_inc(wu_lo_done, 1)

                def split_wd(b):
                    B = l * FBLOCKS + b
                    pool.wait_ge(wd_hi_done, B + 1)
                    g_.tensor_tensor(wd_lo[:], wd_raw[:], wd_hi[:], ALU.subtract).then_inc(wd_lo_done, 1)

                split_wu(0)
                with pool.Fori(0, FBLOCKS - 1) as b:
                    split_wu(b + 1)
                    split_wd(b)
                split_wd(FBLOCKS - 1)
                barrier(pool, phase(l, 4))
                norm_tiles(1)
                barrier(pool, phase(l, 5))


INPUTS = ("state_ret", "state_hgrn", "w_in", "w_out", "hg_lb_raw", "hg_norm_w", "ln_mix_g", "ln_mix_b", "w_up",
          "w_down", "ln_ffn_g", "ln_ffn_b", "swa_sinks")


def kernel(**inputs):
    import concourse.bacc as _bacc
    from concourse.bass_utils import run_bass_kernel_spmd as _run

    nc = _bacc.Bacc("TRN2", target_bir_lowering=False, num_devices=1)
    a = {k: np.asarray(v) for k, v in inputs.items()}
    data = {k: a[k] for k in INPUTS}
    data["x"] = np.concatenate([a["x_prompt"].reshape(SEQ, DM), a["x_sample"].reshape(ROWS_S, DM)])
    data["cache_swa_k"] = a["cache_swa_k"].reshape(DEPTH, NB, WIN, P)
    data["cache_swa_v"] = a["cache_swa_v"].reshape(DEPTH, NB, WIN, P)
    data["sink_rows"] = np.tile(np.repeat(a["swa_sinks"], NL, axis=1), (1, 4)).T
    data["c_const"], data["c_lev"], data["c_swa"], data["c_rope"] = shape_constants()
    arrays, A = {}, {}
    for name, value in data.items():
        value = np.ascontiguousarray(value)
        arrays[f"in_{name}"] = value
        A[name] = nc.dram_tensor(f"in_{name}", value.shape, mybir.dt.from_np(value.dtype), kind="ExternalInput").ap()
    outs = {"y": (TOK, DM), "p_state_ret": (DEPTH, 4, 32, 64), "p_state_hgrn": (DEPTH, 4, 64, 64),
            "p_swa_k": (DEPTH, WIN, P), "p_swa_v": (DEPTH, WIN, P), "s_state_ret": (DEPTH, NB, 4, 32, 64),
            "s_state_hgrn": (DEPTH, NB, 4, 64, 64), "s_swa_k": (DEPTH, NB, WIN, P), "s_swa_v": (DEPTH, NB, WIN, P)}
    for name, shape in outs.items():
        A[name] = nc.dram_tensor(f"out_{name}", shape, F32, kind="ExternalOutput").ap()
    A["hscr"] = nc.dram_tensor("hscr", (TOK, COLS), F32, kind="Internal").ap()
    build(nc, A)
    got = _run(nc, [arrays], core_ids=[0]).results[0]
    r = {name: got[f"out_{name}"] for name in outs}
    return (r["y"][0:SEQ].reshape(1, SEQ, DM), r["y"][SEQ:].reshape(NB, NL, DM),
            r["p_state_ret"].reshape(DEPTH, 1, 4, 32, 64), r["p_state_hgrn"].reshape(DEPTH, 1, 4, 64, 64),
            r["p_swa_k"].reshape(DEPTH, 1, WIN, 2, 64), r["p_swa_v"].reshape(DEPTH, 1, WIN, 2, 64),
            r["s_state_ret"], r["s_state_hgrn"],
            r["s_swa_k"].reshape(DEPTH, NB, WIN, 2, 64), r["s_swa_v"].reshape(DEPTH, NB, WIN, 2, 64))
```

```python
from contextlib import ExitStack
from typing import NamedTuple

import numpy as np

import concourse.bass as bass
from concourse import mybir

F32 = mybir.dt.float32
F32R = mybir.dt.float32r
I32 = mybir.dt.int32
ALU = mybir.AluOpType
ACT = mybir.ActivationFunctionType
AX = mybir.AxisListType.X

P = 128
DM = 1024
KT = DM // P
DEPTH = 2
SEQ = 1024
NB, NL = 8, 4
ROWS_S = NB * NL
TOK = SEQ + ROWS_S
CHUNKS = SEQ // P
TILES = CHUNKS + 1
COLS = 2560
GROUP = 320
GROUPS = COLS // GROUP
FF = 4 * DM
FBLOCK = 256
FBLOCKS = FF // FBLOCK
NCH = 352
TCH = TOK // NCH
RQ, RK, RG, HQ, HF, HGT, SQ, SK, SV = 0, 128, 256, 512, 768, 1024, 1280, 1792, 1920
RV, HI = 0, 256
FRONT = ((0, 256, 0), (512, 1280, 256), (1536, 2560, 1024))
VALUES = ((256, 512, RV), (1280, 1536, HI))
WIN = 128
ALPHA = (2.0 * DEPTH) ** 0.25
LN_EPS = 1e-5
RMS_EPS = 1e-6
NEG = -1e30
HALVES = [64, 32, 16, 8, 4, 2, 1]
NLEV = len(HALVES)
LEVEL_ORDER = [4, 5, 6, 0, 1, 2, 3]
LG = [float(np.log1p(-(2.0 ** (-5.0 - h)))) for h in range(4)]

CONST = {}
_at = 0
for _name, _w in (("ident", 128), ("sel", 2), ("band", 128), ("smask", 320), ("dec", 512), ("decs", 512),
                  ("inter", 128), ("inters", 128), ("kdec", 4), ("kdecs", 4), ("run", 1), ("runs", 128),
                  ("bm", 256), ("tb", 8)):
    CONST[_name] = (_at, _w)
    _at += _w
NCONST = _at


def shape_constants():
    p = np.arange(P)
    t = np.arange(P)
    c = np.zeros((P, NCONST), np.float32)

    def put(name, value):
        a, w = CONST[name]
        c[:, a:a + w] = np.asarray(value, np.float64).reshape(P, w)

    put("ident", np.eye(P))
    put("sel", p[:, None] // 64 == np.arange(2)[None])
    put("band", np.where(t[None] >= p[:, None], 0.0, NEG))
    sm = np.full((P, 2, WIN + ROWS_S), NEG)
    for r in range(P):
        b, l = r // 32, r % 4
        for rt in range(2):
            sm[r, rt, l:WIN] = 0.0
            sm[r, rt, WIN + 4 * (4 * rt + b):WIN + 4 * (4 * rt + b) + l + 1] = 0.0
    put("smask", sm)
    lg = np.array(LG)
    d = t[None, None, :] - p[:, None, None]
    dec = np.where(d >= 0, np.exp(np.maximum(d, 0) * lg[None, :, None]), 0.0) * 32 ** -0.5
    put("dec", dec)
    same = (t[None, None, :] // NL == p[:, None, None] // NL) & (t[None, None, :] < ROWS_S)
    put("decs", np.where(same, dec, 0.0))
    put("inter", np.exp((t[None] + 1) * lg[p // 32][:, None]))
    put("inters", np.exp((t[None] % NL + 1) * lg[p // 32][:, None]))
    put("kdec", np.exp((P - 1 - p)[:, None] * lg[None]) * 32 ** -0.5)
    put("kdecs", np.exp((NL - 1 - p % NL)[:, None] * lg[None]) * 32 ** -0.5)
    put("run", np.ones((P, 1)))
    put("runs", np.broadcast_to(t % NL != 0, (P, P)))
    put("bm", np.broadcast_to((np.arange(ROWS_S)[None] // NL == np.arange(NB)[:, None])[None], (P, NB, ROWS_S)))
    put("tb", p[:, None] // NL == np.arange(NB)[None])
    lev = np.zeros((P, 2, NLEV, 64), np.int32)
    for i, half in enumerate(HALVES):
        blk, off = np.divmod(np.arange(64), half)
        lo = blk * 2 * half
        m = (p[:, None] >= lo[None]) & (p[:, None] < lo[None] + half)
        lev[:, 0, i] = m
        lev[:, 1, i] = m if half < NL else 0
    swa = np.zeros((P, 3, WIN), np.float32)
    swa[:, 0] = swa[:, 2] = np.where(t[None] <= p[:, None], 0.0, NEG)
    swa[:, 1] = NEG
    pos = np.concatenate([np.arange(SEQ), np.tile(SEQ + np.arange(NL), NB)]).astype(np.float32)
    inv_r = (10000.0 ** (-np.linspace(0.0, 1.0, 16, dtype=np.float32))).astype(np.float32)
    inv_s = (500000.0 ** (-np.arange(0, 16, 2, dtype=np.float32) / 16)).astype(np.float32)
    ar = (pos[:, None] * inv_r[None]).astype(np.float32).astype(np.float64)
    as_ = (pos[:, None] * inv_s[None]).astype(np.float32).astype(np.float64)
    rope = np.concatenate([np.cos(ar), np.sin(ar), np.cos(as_), np.sin(as_)], 1).astype(np.float32)
    return c, lev, swa, rope


class Steps:

    def __init__(self, sem, names):
        self.sem, self.names, self.next = sem, names.split(), 0

    def step(self, name):
        assert self.names[self.next] == name, (self.names[self.next], name)
        self.next = (self.next + 1) % len(self.names)
        return self.sem

    def at(self, name, n):
        return n * len(self.names) + (self.names.index(name) + 2)

    def before(self, n):
        return n * len(self.names) + 1


class Chunk(NamedTuple):
    n: object
    w: object
    p: int
    t: object
    rows: int
    loads: object
    prompt: bool


def build(nc, A):
    ctx = ExitStack()
    with ctx:
        where = [16512]

        def place(name, shape, dt, at):
            n = 4
            for s in shape[1:]:
                n *= s
            assert at + n <= 229344, (name, at + n)
            return nc.alloc_sbuf_tensor_at(name, shape, dt, offset=at), at + n

        def region(start):
            here = [start]

            def sb(name, shape, dt=F32):
                t, end = place(name, shape, dt, here[0])
                here[0] = (end + 31) // 32 * 32
                return t
            sb.here = here
            return sb

        def sem(name):
            return ctx.enter_context(nc.semaphore(name))

        sb = region(where[0])
        const = sb("const", [P, NCONST])
        lev_mask = sb("lev_mask", [P, 2, NLEV, 64], I32)
        swa_mask = sb("swa_mask", [P, 3, WIN])
        lb_raw = sb("lb_raw", [P, DEPTH, 2])
        lb_exp = sb("lb_exp", [P, DEPTH, 2])
        lb_tmp = sb("lb_tmp", [P, 4])
        lb_all = sb("lb_all", [P, DEPTH, 2])
        lb = sb("lb", [P, 2])
        omlb = sb("omlb", [P, 2])
        hg_w = sb("hg_w", [P, 64])
        sink_b = sb("sink_b", [P, 8])
        sink_r = sb("sink_r", [P, 1])
        u0 = sb.here[0]
        sb = region(u0)
        u_hi = sb("u_hi", [P, KT, TOK], F32R)
        u_lo = sb("u_lo", [P, KT, TOK], F32R)
        v0 = sb.here[0]
        v_hi = sb("v_hi", [P, KT, TOK], F32R)
        v_lo = sb("v_lo", [P, KT, TOK], F32R)
        r0 = sb.here[0]

        def cst(name):
            a, w = CONST[name]
            return const[:, a:a + w]

        ident = cst("ident")

        sb = region(v0)
        wi_raw = sb("wi_raw", [P, KT, GROUP])
        wi_hi = [sb(f"wi_hi{i}", [P, KT, GROUP], F32R) for i in range(2)]
        wi_lo = [sb(f"wi_lo{i}", [P, KT, GROUP], F32R) for i in range(2)]
        h_out = [sb(f"h_out{i}", [P, GROUP]) for i in range(3)]

        sb = region(v0)
        hb0 = sb("hb0", [P, COLS - 512])
        hv0 = sb("hv0", [P, 512])
        hb1_at = sb.here[0]
        hb = [hb0, sb("hb1", [P, COLS - 512])]
        hv = [hv0, sb("hv1", [P, 512])]
        rt = [sb(f"rt{i}", [P, 48]) for i in range(2)]
        rope_a = sb("rope_a", [P, 256])
        rope_b = sb("rope_b", [P, 256])
        rope_sa = sb("rope_sa", [P, 10, 2, 8])
        rope_sb = sb("rope_sb", [P, 10, 2, 8])
        rot_r = sb("rot_r", [P, 256])
        rot_q = sb("rot_q", [P, 4, 2, 64])
        rot_k = sb("rot_k", [P, 2, 64])
        g_e = sb("g_e", [P, 2, P])
        g_r = sb("g_r", [P, 2, P])
        g_s = sb("g_s", [P, 2, P])
        g_k = sb("g_k", [P, 2, P])
        g_f = sb("g_f", [P, 2, P])
        g_b = sb("g_b", [P, 2, P])
        g_q = sb("g_q", [P, 2, P])
        g_p = [sb(f"g_p{i}", [P, 2, P]) for i in range(2)]
        g_eb = [sb(f"g_eb{i}", [P, 2, P]) for i in range(2)]
        g_qe = [sb(f"g_qe{i}", [P, 2, P]) for i in range(2)]
        g_ka = [sb(f"g_ka{i}", [P, 2, P]) for i in range(2)]
        g_kt = sb("g_kt", [P, 2, P])
        lev_e = sb("lev_e", [P, NLEV, 2, P])
        lev_x = sb("lev_x", [P, NLEV, 2, P])
        lev_r = sb("lev_r", [P, NLEV, 2, 2, 64])
        diag = sb("diag", [P, 4])
        hg_a = sb("hg_a", [P, 4, P])
        r_kT = sb("r_kT", [P, P])
        r_qx = sb("r_qx", [P, 4, P])
        r_qi = [sb(f"r_qi{i}", [P, P]) for i in range(2)]
        r_a0 = sb("r_a0", [P, 4, P])
        r_a1_at = sb.here[0]
        r_a = [r_a0, sb("r_a1", [P, 4, P])]
        r_kd = [sb(f"r_kd{i}", [P, 4, 32]) for i in range(2)]
        s_qT = sb("s_qT", [P, 4, P])
        s_kT = sb("s_kT", [P, 2, P])
        s_v = sb("s_v", [P, 2, P])
        st_r = sb("st_r", [P, 256])
        st_h = sb("st_h", [P, 2, P])
        mx = sb("mx", [P, 8])
        m = sb("m", [P, 8])
        nm = sb("nm", [P, 8])
        sk = sb("sk", [P, 8])
        esk = sb("esk", [P, 8])
        ssum = sb("ssum", [P, 8])
        den = sb("den", [P, 8])
        rden = sb("rden", [P, 8])
        gate0 = sb("gate0", [P, 2, 256])
        gate1_at = sb.here[0]
        gate = [gate0, sb("gate1", [P, 2, 256])]
        rms_sq = sb("rms_sq", [P, 8, 64])
        rms = sb("rms", [P, 8])
        rms_v = sb("rms_v", [P, 8])
        rms_l = sb("rms_l", [P, 8])
        rms_t = sb("rms_t", [P, 8])
        cat0 = sb("cat0", [P, DM])
        cat1_at = sb.here[0]
        cat = [cat0, sb("cat1", [P, DM])]
        p0 = sb.here[0]
        prob = sb("prob", [P, 8, 256])
        probT = sb("probT", [P, 16, P])
        p1 = sb.here[0]
        s0_r = sb("s0_r", [P, NB, 256])
        s0_h = sb("s0_h", [P, 2, NB, P])
        ksm, at = place("ksm", [P, 2, NB, P], F32, hb1_at)
        qm_h, at = place("qm_h", [P, 2, NB, ROWS_S], F32, at)
        assert at <= hb1_at + 4 * COLS
        qm_r, _ = place("qm_r", [P, NB, ROWS_S], F32, gate1_at)
        kdm, _ = place("kdm", [P, NB, P], F32, cat1_at)
        spT, at = place("spT", [P, 2, P], F32, r_a1_at)
        spN, _ = place("spN", [P, 2, P], F32, at)
        sb = region(p0)
        ck = sb("ck", [P, NB, P])
        cv = sb("cv", [P, NB, P])
        ckT = sb("ckT", [P, NB, P])
        qxs = sb("qxs", [P, NB, 2, 4, NL])
        s_prob = sb("s_prob", [P, 2, WIN + ROWS_S])
        assert sb.here[0] <= p1, (sb.here[0], p1)
        sb = region(v0)
        wo_raw = sb("wo_raw", [P, KT, P])
        wo_hi = [sb(f"wo_hi{i}", [P, KT, P], F32R) for i in range(2)]
        wo_lo = [sb(f"wo_lo{i}", [P, KT, P], F32R) for i in range(2)]
        sb = region(r0)
        acc = sb("acc", [P, KT, TOK])
        n0 = sb.here[0]
        wu_raw = sb("wu_raw", [P, KT, FBLOCK])
        wd_raw = sb("wd_raw", [P, 2, DM])
        n1 = sb.here[0]
        relu = [sb(f"relu{i}", [P, NCH]) for i in range(3)]
        sq = [sb(f"sq{i}", [P, NCH]) for i in range(3)]
        ln_b = sb("ln_b", [P, DM])
        stats = sb("stats", [P, 2, 2, 6])
        aggr = sb("aggr", [P, 2, 2])
        rstd = sb("rstd", [P, 2])
        var = sb("var", [P, 2])
        logv = sb("logv", [P, 2])
        newt = sb("newt", [P, 2])
        sb = region(u0)
        xn_0 = [sb(f"xn_0{i}", [P, DM]) for i in range(2)]
        stage_0 = sb("stage_0", [P, KT, P])
        ln_g_0 = sb("ln_g_0", [P, DM])
        sb = region(n1)
        xin_0 = [sb(f"xin_0{i}", [P, DM]) for i in range(2)]
        sb = region(n0)
        xn_1 = [sb(f"xn_1{i}", [P, DM]) for i in range(2)]
        stage_1 = sb("stage_1", [P, KT, P])
        sb = region(v0)
        xin_1 = [sb(f"xin_1{i}", [P, DM]) for i in range(2)]
        ln_g_1 = sb("ln_g_1", [P, DM])
        xn, stage, ln_g, xin = (xn_0, xn_1), (stage_0, stage_1), (ln_g_0, ln_g_1), (xin_0, xin_1)
        sb = region(u0)
        hid_hi = [sb(f"hid_hi{i}", [P, 2, TOK], F32R) for i in range(2)]
        hid_lo = [sb(f"hid_lo{i}", [P, 2, TOK], F32R) for i in range(2)]
        wu_hi = sb("wu_hi", [P, KT, FBLOCK], F32R)
        wu_lo = sb("wu_lo", [P, KT, FBLOCK], F32R)
        wd_hi = sb("wd_hi", [P, 2, DM], F32R)
        wd_lo = sb("wd_lo", [P, 2, DM], F32R)
        assert sb.here[0] <= v0

        ps = ctx.enter_context(nc.psum_tensor("ps", [P, 8, 512], F32))

        const_in = sem("const_in")
        par_in = sem("par_in")
        phase_end = sem("phase_end")
        marks = sem("marks")
        lbd = Steps(sem("bound_dve"), "max sub0 sub1 sum inv p0 p1 cum lb0 lb1")
        lba = Steps(sem("bound_act"), "exp")
        zd = Steps(sem("layer_dve"), "lb omlb r h kT v qx sr sh lx lr")
        x_in = [sem(f"x_in{i}") for i in range(2)]
        x_out = [sem(f"x_out{i}") for i in range(2)]
        na = Steps(sem("norm_act"), "stage")
        npe = Steps(sem("norm_pe"), "T")
        nd = Steps(sem("norm_dve"), "res st0 st1 aggr var n0 n1 rstd xn")
        nr = Steps(sem("norm_rstd_act"), "ln r")
        npl = Steps(sem("norm_pool"), "g b")
        spe = Steps(sem("split_pe"), "T")
        sa = Steps(sem("split_act"), "hi")
        sd = Steps(sem("split_dve"), "lo")
        wi_in = sem("wi_in")
        wi_hi_done = sem("wi_hi_done")
        wi_lo_done = sem("wi_lo_done")
        proj_ready = sem("proj_ready")
        proj_free = sem("proj_free")
        h_stored = [sem(f"h_stored{i}") for i in range(3)]
        wo_in = sem("wo_in")
        wo_hi_done = sem("wo_hi_done")
        wo_lo_done = sem("wo_lo_done")
        out_ready = sem("out_ready")
        out_free = sem("out_free")
        wu_in = sem("wu_in")
        wd_in = sem("wd_in")
        wu_hi_done = sem("wu_hi_done")
        wu_lo_done = sem("wu_lo_done")
        wd_hi_done = sem("wd_hi_done")
        wd_lo_done = sem("wd_lo_done")
        up_ready = sem("up_ready")
        up_free = sem("up_free")
        sq_done = sem("sq_done")
        hid_hi_done = sem("hid_hi_done")
        hid_lo_done = sem("hid_lo_done")
        down_ready = sem("down_ready")
        down_free = sem("down_free")
        acc_zero = sem("acc_zero")
        h_in = [sem(f"h_in{i}") for i in range(2)]
        v_in = [sem(f"v_in{i}") for i in range(2)]
        levels = [f"{i}" for i in range(NLEV)]
        rp = Steps(sem("rope_pool"), "ra rb0 rb1 r0 r1 sa sb0 sb1 q0 q1 k0 k1 qc kc kd v sw")
        tpe = Steps(sem("mixT_pe"), "h r q")
        ga = Steps(sem("gate_act"), "e q kTr kTs qT f eg eb E ka")
        gd = Steps(sem("gate_dve"), "clip one r s k0 k1 f0 f1 b0 b1 p ka " + " ".join(f"ar{i} al{i}" for i in levels))
        gp = Steps(sem("lev_pool"), "qe kst " + " ".join(f"l{i} r{i} s{i}" for i in LEVEL_ORDER))
        rd = Steps(sem("ret_dve"), "x0 x1 x2 x3 qi a")
        rpe = Steps(sem("ret_pe"), "ret")
        gg = Steps(sem("silu_dve"), "c0 c1 one r s0 s1")
        mpe = Steps(sem("heads_pe"), "kt lev1 lev0 o st")
        hd = Steps(sem("heads_dve"), "kt diag a " + " ".join(f"c{i}" for i in LEVEL_ORDER))
        md = Steps(sem("merge_dve"), "ss ms n0 n1 rstd sr rh")
        ma = Steps(sem("merge_act"), "sq ln r")
        cpe = Steps(sem("cat_pe"), "T0 T1")
        ca = Steps(sem("cat_act"), "hi")
        cd = Steps(sem("cat_dve"), "lo")
        wpe = Steps(sem("window_pe"), "s T0 T1 o")
        wd = Steps(sem("window_dve"), "s band mx m nm sk den rden T o")
        wa = Steps(sem("window_act"), "e0 e1 e2 e3 e4 e5 e6 e7 sk T")
        sdv = Steps(sem("state_dve"), "r0 r1 r2 r3 h0 h1 h2 h3")
        dp = Steps(sem("decode_pool"), "qr qh0 qh1 kd ks0 ks1")
        dpe = Steps(sem("decode_pe"), "ckT s T o st_h")
        dd = Steps(sem("decode_dve"), "zx x0 x1 s mx m nm sk den rden p0 p1 T o0 o1 r0 r1 r2 r3 hm h0 h1 h2 h3")
        da = Steps(sem("decode_act"), "ck e0 e1 sk T o0 o1")
        kv_out = sem("kv_out")
        state_out = sem("state_out")
        s0_in = sem("s0_in")
        cache_in = sem("cache_in")
        cache_out = sem("cache_out")

        block = ctx.enter_context(nc.Block())

        def apart(eng):
            eng.sem_inc(marks, 1)

        def barrier(eng, k):
            apart(eng)
            eng.drain().then_inc(phase_end, 1)
            eng.wait_ge(phase_end, 5 * k)
            apart(eng)

        def phase(l, j):
            return l * 6 + (2 + j)

        def prompt_chunk(l, i, p):
            return Chunk(n=l * TILES + (i * 2 + p), w=l * CHUNKS + (i * 2 + p), p=p, t=i * 2 + p, rows=P,
                         loads=l * (5 - p) + (i + 1), prompt=True)

        def decode_chunk(l):
            return Chunk(n=l * TILES + CHUNKS, w=(l + 1) * CHUNKS, p=0, t=CHUNKS, rows=ROWS_S, loads=(l + 1) * 5,
                         prompt=False)

        def tile_rows(t):
            return P if t < CHUNKS else ROWS_S

        def x_count(l, which, t, i=0):
            return (l * 2 + (which + 1)) * (5 - t % 2) + (i + (t // 2 + 1))

        @block.sync
        def _(sp):
            sp.dma_start(const[:], A["c_const"]).then_inc(const_in, 16)
            sp.dma_start(lev_mask[:], A["c_lev"]).then_inc(const_in, 16)
            with nc.allow_non_contiguous_dma(reason="512 words"):
                sp.dma_start(lb_raw[:], A["hg_lb_raw"].rearrange("l (t p) -> p l t", p=P)).then_inc(const_in, 16)
            for t in range(TILES):
                p, rows = t % 2, tile_rows(t)
                if t >= 2:
                    sp.wait_ge(spe.sem, spe.at("T", t - 2))
                    sp.wait_ge(x_out[p], 16 * (t // 2))
                sp.dma_start(xn_1[p][0:rows, :], A["x"][t * P:t * P + rows, :]).then_inc(x_in[p], 16)
                sp.wait_ge(x_in[p], 16 * (t // 2 + 1))
                sp.dma_start(A["y"][t * P:t * P + rows, :], xn_1[p][0:rows, :]).then_inc(x_out[p], 16)
            sp.wait_ge(x_out[0], 16 * 5)
            sp.wait_ge(x_out[1], 16 * 4)
            barrier(sp, 1)

            with sp.Fori(0, DEPTH) as l:
                sp.dma_start(swa_mask[:], A["c_swa"]).then_inc(par_in, 16)
                sp.dma_start(hg_w[:], A["hg_norm_w"][bass.ds(l, 1), :].broadcast_to([P, 64])).then_inc(par_in, 16)
                sp.dma_start(sink_b[:], A["swa_sinks"][bass.ds(l, 1), :].broadcast_to([P, 8])).then_inc(par_in, 16)
                with nc.allow_non_contiguous_dma(reason="128 words"):
                    sp.dma_start(sink_r[:], A["sink_rows"][:, bass.ds(l, 1)]).then_inc(par_in, 16)

                def load_wi(g):
                    G = l * GROUPS + g
                    sp.wait_ge(wi_hi_done, G)
                    sp.wait_ge(wi_lo_done, G)
                    sp.dma_start(wi_raw[:], A["w_in"][bass.ds(l, 1), :, bass.ds(g * GROUP, GROUP)]
                                 .rearrange("l (k p) c -> p (l k) c", p=P)).then_inc(wi_in, 16)

                def store_h(g):
                    for t in range(TILES):
                        rows = tile_rows(t)
                        sp.wait_ge(proj_free, (l * GROUPS + g) * TILES + (t + 4))
                        sp.dma_start(A["hscr"][t * P:t * P + rows, bass.ds(g * GROUP, GROUP)],
                                     h_out[t % 3][0:rows, :]).then_inc(h_stored[t % 3], 16)

                load_wi(0)
                load_wi(1)
                with sp.Fori(0, GROUPS // 2 - 1) as i:
                    for q in range(2):
                        store_h(i * 2 + q)
                        load_wi(i * 2 + (q + 2))
                store_h(GROUPS - 2)
                store_h(GROUPS - 1)
                for j in range(3):
                    sp.wait_ge(h_stored[j], (l + 1) * (16 * 3 * GROUPS))
                apart(sp)
                barrier(sp, phase(l, 0))

                def load_h(c, p, rows=P):
                    for a, b, to in FRONT:
                        sp.dma_start(hb[p][0:rows, to:to + b - a], A["hscr"][bass.ds(c * P, rows), a:b])\
                          .then_inc(h_in[p], 16)
                    sp.dma_start(rt[p][0:rows, :], A["c_rope"][bass.ds(c * P, rows), :]).then_inc(h_in[p], 16)

                def load_v(c, p, rows=P):
                    for a, b, to in VALUES:
                        sp.dma_start(hv[p][0:rows, to:to + b - a], A["hscr"][bass.ds(c * P, rows), a:b])\
                          .then_inc(v_in[p], 16)

                def next_h(n, c, p, rows=P):
                    sp.wait_ge(rp.sem, rp.at("v", n))
                    sp.wait_ge(gg.sem, gg.at("s1", n))
                    apart(sp)
                    load_h(c, p, rows)

                def next_v(n, c, p, rows=P):
                    sp.wait_ge(mpe.sem, mpe.at("st", n))
                    load_v(c, p, rows)

                load_h(0, 0)
                load_h(1, 1)
                load_v(0, 0)
                load_v(1, 1)
                sp.wait_ge(zd.sem, zd.at("sh", l))
                for h in range(4):
                    pr, j = h // 2, h % 2
                    sp.dma_start(s0_r[32 * h:32 * h + 32, :, 64 * h:64 * h + 64],
                                 A["state_ret"][bass.ds(l, 1), :, h, :, :].rearrange("l b k v -> k (l b) v"))\
                      .then_inc(s0_in, 16)
                    sp.dma_start(s0_h[64 * j:64 * j + 64, pr, :, 64 * j:64 * j + 64],
                                 A["state_hgrn"][bass.ds(l, 1), :, h, :, :].rearrange("l b k v -> k (l b) v"))\
                      .then_inc(s0_in, 16)
                for name, src in (("s_swa_k", "cache_swa_k"), ("s_swa_v", "cache_swa_v")):
                    sp.dma_start(A[name][bass.ds(l, 1), :, 0:WIN - NL, :],
                                 A[src][bass.ds(l, 1), :, NL:WIN, :]).then_inc(cache_out, 16)
                first = l * TILES
                next_h(first, 2, 0)
                next_h(first + 1, 3, 1)
                with sp.Fori(0, CHUNKS // 2 - 2) as i:
                    next_v(first + i * 2, i * 2 + 2, 0)
                    next_h(first + (i * 2 + 2), i * 2 + 4, 0)
                    next_v(first + (i * 2 + 1), i * 2 + 3, 1)
                    next_h(first + (i * 2 + 3), i * 2 + 5, 1)
                next_v(first + (CHUNKS - 4), CHUNKS - 2, 0)
                next_h(first + (CHUNKS - 2), CHUNKS, 0, ROWS_S)
                next_v(first + (CHUNKS - 3), CHUNKS - 1, 1)
                next_v(first + (CHUNKS - 2), CHUNKS, 0, ROWS_S)
                n7 = l * TILES + (CHUNKS - 1)
                sp.wait_ge(rp.sem, rp.at("v", n7))
                sp.dma_start(A["p_swa_k"][bass.ds(l, 1), :, :], rot_k[:, :, :]).then_inc(kv_out, 16)
                sp.dma_start(A["p_swa_v"][bass.ds(l, 1), :, :], s_v[:, 1, :]).then_inc(kv_out, 16)
                sp.wait_ge(wpe.sem, wpe.at("o", l * CHUNKS + (CHUNKS - 1)))
                sp.dma_start(ck[:], A["cache_swa_k"][bass.ds(l, 1)].rearrange("l b s c -> s (l b) c"))\
                  .then_inc(cache_in, 16)
                sp.dma_start(cv[:], A["cache_swa_v"][bass.ds(l, 1)].rearrange("l b s c -> s (l b) c"))\
                  .then_inc(cache_in, 16)
                sp.wait_ge(sdv.sem, sdv.at("h3", l * CHUNKS + (CHUNKS - 1)))
                for h in range(4):
                    pr, j = h // 2, h % 2
                    sp.dma_start(A["p_state_ret"][bass.ds(l, 1), h, :, :],
                                 st_r[32 * h:32 * h + 32, 64 * h:64 * h + 64]).then_inc(state_out, 16)
                    sp.dma_start(A["p_state_hgrn"][bass.ds(l, 1), h, :, :],
                                 st_h[64 * j:64 * j + 64, pr, 64 * j:64 * j + 64]).then_inc(state_out, 16)
                sp.wait_ge(rp.sem, rp.at("v", l * TILES + CHUNKS))
                for b in range(NB):
                    rows = slice(NL * b, NL * b + NL)
                    sp.dma_start(A["s_swa_k"][bass.ds(l, 1), b, WIN - NL:WIN, :], rot_k[rows, :, :])\
                      .then_inc(cache_out, 16)
                    sp.dma_start(A["s_swa_v"][bass.ds(l, 1), b, WIN - NL:WIN, :], s_v[rows, 0, :])\
                      .then_inc(cache_out, 16)
                sp.wait_ge(dd.sem, dd.at("h3", l))
                for h in range(4):
                    pr, j = h // 2, h % 2
                    sp.dma_start(A["s_state_ret"][bass.ds(l, 1), :, h, :, :].rearrange("l b k v -> k (l b) v"),
                                 s0_r[32 * h:32 * h + 32, :, 64 * h:64 * h + 64]).then_inc(state_out, 16)
                    sp.dma_start(A["s_state_hgrn"][bass.ds(l, 1), :, h, :, :].rearrange("l b k v -> k (l b) v"),
                                 s0_h[64 * j:64 * j + 64, pr, :, 64 * j:64 * j + 64]).then_inc(state_out, 16)
                sp.wait_ge(kv_out, (l + 1) * 32)
                apart(sp)
                sp.wait_ge(state_out, (l + 1) * 256)
                apart(sp)
                sp.wait_ge(cache_out, (l + 1) * (16 * (2 + 2 * NB)))
                apart(sp)
                barrier(sp, phase(l, 1))

                def load_x(which, t, p, rows=P):
                    sp.dma_start(xin[which][p][0:rows, :], A["y"][bass.ds(t * P, rows), :]).then_inc(x_in[p], 16)

                def load_b(name):
                    sp.dma_start(ln_b[:], A[name][bass.ds(l, 1), :].broadcast_to([P, DM])).then_inc(par_in, 16)

                def load_g(which, name):
                    sp.dma_start(ln_g[which][:], A[name][bass.ds(l, 1), :].broadcast_to([P, DM])).then_inc(par_in, 16)

                def load_wo(j):
                    J = l * KT + j
                    cols = bass.ds(j * P, P)
                    sp.wait_ge(wo_hi_done, J)
                    sp.wait_ge(wo_lo_done, J)
                    sp.dma_start(wo_raw[:, 0:4, :], A["w_out"][bass.ds(l, 1), 0:512, cols]
                                 .rearrange("l (k p) c -> p (l k) c", p=P)).then_inc(wo_in, 16)
                    for kv in range(2):
                        sp.dma_start(wo_raw[64 * kv:64 * kv + 64, 4:8, :],
                                     A["w_out"][bass.ds(l, 1), 512 + 256 * kv:768 + 256 * kv, cols]
                                     .rearrange("l (g d) c -> d (l g) c", d=64)).then_inc(wo_in, 16)

                load_wo(0)
                load_x(0, 0, 0)
                load_x(0, 1, 1)
                load_b("ln_mix_b")
                with sp.Fori(0, KT - 1) as j:
                    load_wo(j + 1)
                barrier(sp, phase(l, 2))

                def norm_tiles(which):
                    base = (l * 2 + which) * TILES

                    def step(t, p, rows=P, then=P):
                        if then:
                            sp.wait_ge(nd.sem, nd.at("xn", base + t))
                            apart(sp)
                            load_x(which, t + 2, p, then)
                        sp.wait_ge(npl.sem, npl.at("b", base + t))
                        apart(sp)
                        sp.dma_start(A["y"][bass.ds(t * P, rows), :], xn[which][p][0:rows, :]).then_inc(x_out[p], 16)

                    with sp.Fori(0, CHUNKS // 2 - 1) as i:
                        for p in range(2):
                            step(i * 2 + p, p)
                    step(CHUNKS - 2, 0, then=ROWS_S)
                    step(CHUNKS - 1, 1, then=0)
                    step(CHUNKS, 0, ROWS_S, then=0)
                    sp.wait_ge(x_out[0], (l * 2 + (which + 2)) * (5 * 16))
                    apart(sp)
                    sp.wait_ge(x_out[1], (l * 2 + (which + 2)) * (4 * 16))
                    apart(sp)

                def load_wu(b):
                    B = l * FBLOCKS + b
                    sp.wait_ge(wu_hi_done, B)
                    sp.wait_ge(wu_lo_done, B)
                    sp.dma_start(wu_raw[:], A["w_up"][bass.ds(l, 1), :, bass.ds(b * FBLOCK, FBLOCK)]
                                 .rearrange("l (k p) c -> p (l k) c", p=P)).then_inc(wu_in, 16)

                def load_wd(b):
                    B = l * FBLOCKS + b
                    sp.wait_ge(wd_hi_done, B)
                    sp.wait_ge(wd_lo_done, B)
                    sp.dma_start(wd_raw[:], A["w_down"][bass.ds(l, 1), bass.ds(b * FBLOCK, FBLOCK), :]
                                 .rearrange("l (f p) d -> p (l f) d", p=P)).then_inc(wd_in, 16)

                load_g(0, "ln_mix_g")
                load_wu(0)
                norm_tiles(0)
                barrier(sp, phase(l, 3))

                load_b("ln_ffn_b")
                with sp.Fori(0, FBLOCKS - 1) as b:
                    load_wu(b + 1)
                    load_wd(b)
                load_wd(FBLOCKS - 1)
                sp.wait_ge(up_ready, (l + 1) * (FBLOCKS * 6))
                apart(sp)
                load_x(1, 0, 0)
                load_x(1, 1, 1)
                load_g(1, "ln_ffn_g")
                barrier(sp, phase(l, 4))
                norm_tiles(1)
                barrier(sp, phase(l, 5))

        @block.tensor
        def _(pe):
            def transpose(out, in_, rows):
                return nc.tensor.transpose(out, in_, ident[0:rows, 0:rows])

            def three(out, a_hi, a_lo, b_hi, b_lo, start, stop):
                nc.tensor.matmul(out, a_hi, b_hi, start=start, stop=False)
                nc.tensor.matmul(out, a_hi, b_lo, start=False, stop=False)
                return nc.tensor.matmul(out, a_lo, b_hi, start=False, stop=stop)

            def split_tile(m, p, rows, src, first=False):
                if not first:
                    pe.wait_ge(sa.sem, sa.at("hi", m - 2))
                    pe.wait_ge(sd.sem, sd.at("lo", m - 2))
                    apart(pe)
                for k in range(KT):
                    last = transpose(ps[:, 4 + 2 * p + k // 4, (k % 4) * P:(k % 4) * P + rows],
                                     src[p][0:rows, k * P:(k + 1) * P], rows)
                last.then_inc(spe.step("T"), 1)

            for S in (npe, spe, tpe, rpe, mpe, cpe, wpe, dpe):
                pe.sem_inc(S.sem, 1)
            pe.wait_ge(const_in, 48)
            for t in range(TILES):
                pe.wait_ge(x_in[t % 2], 16 * (t // 2 + 1))
                split_tile(t, t % 2, tile_rows(t), xn_1, first=t < 2)
            barrier(pe, 1)

            with pe.Fori(0, DEPTH) as l:
                with pe.Fori(0, GROUPS // 2) as i:
                    for q in range(2):
                        G = l * GROUPS + i * 2 + q
                        pe.wait_ge(wi_hi_done, G + 1)
                        pe.wait_ge(wi_lo_done, G + 1)
                        for t in range(TILES):
                            rows = tile_rows(t)
                            pe.wait_ge(proj_free, G * TILES + (t + 1))
                            tok = slice(t * P, t * P + rows)
                            for k in range(KT):
                                last = three(ps[0:rows, t % 3, 0:GROUP], u_hi[:, k, tok], u_lo[:, k, tok],
                                             wi_hi[q][:, k, :], wi_lo[q][:, k, :], k == 0, k == KT - 1)
                            last.then_inc(proj_ready, 1)
                barrier(pe, phase(l, 0))

                def front_transposes(c, first):
                    x = hb[c.p]
                    pe.wait_ge(h_in[c.p], c.loads * 64)
                    for j in range(2):
                        transpose(ps[:, 0, j * P:(j + 1) * P], x[:, HF + j * P:HF + (j + 1) * P], P)
                    for j in range(2):
                        last = transpose(ps[:, 0, (2 + j) * P:(3 + j) * P], x[:, HQ + j * P:HQ + (j + 1) * P], P)
                    last.then_inc(tpe.step("h"), 1)
                    pe.wait_ge(rp.sem, rp.at("kc", c.n))
                    pe.wait_ge(wd.sem, wd.before(c.w))
                    transpose(ps[:, 1, 0:P], rot_r[:, 0:P], P)
                    transpose(ps[:, 1, P:2 * P], rot_r[:, P:2 * P], P)
                    transpose(ps[:, 1, 2 * P:3 * P], rot_k[:, :, :].rearrange("p a b -> p (a b)"), P)\
                        .then_inc(tpe.step("r"), 1)
                    pe.wait_ge(cd.sem, cd.before(c.n) if first else cd.before(c.n - 1))
                    for g in range(4):
                        last = transpose(ps[:, 2, g * P:(g + 1) * P],
                                         rot_q[:, g, :, :].rearrange("p a b -> p (a b)"), P)
                    last.then_inc(tpe.step("q"), 1)

                def heads_weights(c):
                    pe.wait_ge(gp.sem, gp.at("kst", c.n))
                    pe.wait_ge(cd.sem, cd.before(c.n))
                    for j in range(2):
                        last = transpose(ps[:, 3, j * P:(j + 1) * P], g_ka[c.p][:, j, :], P)
                    last.then_inc(mpe.step("kt"), 1)
                    if not c.prompt:
                        pe.wait_ge(da.sem, da.at("o1", l))
                        pe.wait_ge(dd.sem, dd.at("o1", l))
                    pe.wait_ge(gp.sem, gp.at("s6", c.n))
                    pe.wait_ge(gd.sem, gd.at("p", c.n))
                    apart(pe)
                    for pr in range(2):
                        nc.tensor.matmul(ps[:, 7, 256 + 2 * pr:258 + 2 * pr], g_p[c.p][:, pr, :], cst("sel"),
                                         start=True, stop=True)
                    for i in LEVEL_ORDER:
                        if i == 0:
                            pe.wait_ge(gp.sem, gp.at("s3", c.n))
                        for pr in range(2):
                            at = (i % 2) * 256 + pr * P
                            last = nc.tensor.matmul(ps[:, 4 + i // 2, at:at + P], lev_x[:, i, pr, :],
                                                    lev_r[:, i, pr, :, :].rearrange("p a b -> p (a b)"),
                                                    start=True, stop=True)
                        if i == NLEV - 1:
                            last.then_inc(mpe.step("lev1"), 1)
                    last.then_inc(mpe.step("lev0"), 1)

                def front_scores(c, h):
                    if h:
                        pe.wait_ge(hd.sem, hd.at("kt", h.n))
                    pe.wait_ge(ga.sem, ga.at("kTr", c.n))
                    pe.wait_ge(rd.sem, rd.at("qi", c.n))
                    nc.tensor.matmul(ps[:, 3, :], r_kT[:], r_qx[:, :, :].rearrange("p a b -> p (a b)"),
                                     start=True, stop=True).then_inc(rpe.step("ret"), 1)
                    pe.wait_ge(ga.sem, ga.at("qT", c.n))
                    if c.prompt:
                        for kv in (1, 0):
                            if h:
                                pe.wait_ge(hd.sem, hd.at("c6" if kv else "c3", h.n))
                            d = slice(64 * kv, 64 * kv + 64)
                            for g in range(4):
                                last = nc.tensor.matmul(ps[:, 4 + 2 * kv + g // 2, (g % 2) * 256:(g % 2) * 256 + 256],
                                                        s_qT[d, g, :], s_kT[d, :, :].rearrange("p a b -> p (a b)"),
                                                        start=True, stop=True)
                        last.then_inc(wpe.step("s"), 1)
                    else:
                        pe.wait_ge(cache_in, (l + 1) * 32)
                        pe.wait_ge(hd.sem, hd.at("c3", h.n))
                        for b in range(NB):
                            last = transpose(ps[:, 4 + b // 4, (b % 4) * P:(b % 4) * P + P], ck[:, b, :], P)
                        last.then_inc(dpe.step("ckT"), 1)
                        pe.wait_ge(dd.sem, dd.at("x1", l))
                        pe.wait_ge(da.sem, da.at("ck", l))
                        for b in range(NB):
                            r = slice(32 * (b % 4), 32 * (b % 4) + 32)
                            nc.tensor.matmul(ps[r, 6 + b // 4, 0:WIN], qxs[:, b, :, :, :].rearrange("p a b c -> p (a b c)"),
                                             ckT[:, b, :], start=True, stop=True)
                        for r in range(2):
                            last = nc.tensor.matmul(ps[:, 6 + r, WIN:WIN + ROWS_S],
                                                    qxs[:, 4 * r:4 * r + 4, :, :, :].rearrange("p e a b c -> p (e a b c)"),
                                                    s_kT[:, 0, 0:ROWS_S], start=True, stop=True)
                        last.then_inc(dpe.step("s"), 1)

                def heads_out(c, f):
                    x, rows = hv[c.p], c.rows
                    pe.wait_ge(v_in[c.p], c.loads * 32)
                    if f:
                        pe.wait_ge(ga.sem, ga.at("q", f.n))
                    pe.wait_ge(gp.sem, gp.at("qe", c.n))
                    pe.wait_ge(rd.sem, rd.at("a", c.n))
                    pe.wait_ge(hd.sem, hd.at("c3", c.n))
                    if c.prompt:
                        pe.wait_ge(sdv.sem, sdv.before(c.w))
                        pe.wait_ge(zd.sem, zd.at("h", l))
                        nc.tensor.matmul(ps[:, 0, 0:256], r_qi[c.p][:], st_r[:], start=True, stop=False)
                    else:
                        pe.wait_ge(dp.sem, dp.at("qh1", l))
                        pe.wait_ge(s0_in, (l + 1) * 128)
                        for b in range(NB):
                            nc.tensor.matmul(ps[0:rows, 0, 0:256], qm_r[:, b, :], s0_r[:, b, :], start=(b == 0), stop=False)
                    for h in range(4):
                        nc.tensor.matmul(ps[0:rows, 0, 64 * h:64 * h + 64], r_a[c.p][0:rows, h, 0:rows],
                                         x[0:rows, RV + 64 * h:RV + 64 * h + 64], start=False, stop=(h == 3))
                    for pr in range(2):
                        c0 = 256 + pr * P
                        if c.prompt:
                            nc.tensor.matmul(ps[:, 0, c0:c0 + P], g_qe[c.p][:, pr, :], st_h[:, pr, :], start=True, stop=False)
                        else:
                            for b in range(NB):
                                nc.tensor.matmul(ps[0:rows, 0, c0:c0 + P], qm_h[:, pr, b, :], s0_h[:, pr, b, :],
                                                 start=(b == 0), stop=False)
                        for j in range(2):
                            last = nc.tensor.matmul(ps[0:rows, 0, c0 + 64 * j:c0 + 64 * j + 64],
                                                    hg_a[0:rows, 2 * pr + j, 0:rows],
                                                    x[0:rows, HI + (c0 - 256) + 64 * j:HI + (c0 - 256) + 64 * j + 64],
                                                    start=False, stop=(j == 1))
                    last.then_inc(mpe.step("o"), 1)
                    pe.wait_ge(rp.sem, rp.at("kd", c.n))
                    pe.wait_ge(hd.sem, hd.at("kt", c.n))
                    if f and f.prompt:
                        pe.wait_ge(ga.sem, ga.at("qT", f.n))
                    elif f:
                        pe.wait_ge(dd.sem, dd.at("x1", l))
                    if c.prompt:
                        nc.tensor.matmul(ps[:, 2, 0:256], r_kd[c.p][:, :, :].rearrange("p a b -> p (a b)"),
                                         x[:, RV:RV + 256], start=True, stop=True)
                        for pr in range(2):
                            last = nc.tensor.matmul(ps[:, 2, 256 + pr * P:256 + (pr + 1) * P], g_kt[:, pr, :],
                                                    x[:, HI + pr * P:HI + (pr + 1) * P], start=True, stop=True)
                        last.then_inc(mpe.step("st"), 1)
                    else:
                        pe.wait_ge(dp.sem, dp.at("ks1", l))
                        for b in range(NB):
                            last = nc.tensor.matmul(ps[:, 4 + b // 2, (b % 2) * 256:(b % 2) * 256 + 256], kdm[0:rows, b, :],
                                                    x[0:rows, RV:RV + 256], start=True, stop=True)
                        last.then_inc(mpe.step("st"), 1)
                        pe.wait_ge(dd.sem, dd.at("hm", l))
                        for pr in range(2):
                            for b in range(NB):
                                last = nc.tensor.matmul(ps[:, 4 + 2 * pr + b // 4, (b % 4) * P:(b % 4) * P + P],
                                                        ksm[0:rows, pr, b, :], x[0:rows, HI + pr * P:HI + (pr + 1) * P],
                                                        start=True, stop=True)
                        last.then_inc(dpe.step("st_h"), 1)

                def front_window(c):
                    if c.prompt:
                        for half in range(2):
                            pe.wait_ge(wa.sem, wa.at("e7" if half else "e3", c.w))
                            for e in range(8 * half, 8 * half + 8):
                                last = transpose(ps[:, 4 + e // 4, (e % 4) * P:(e % 4) * P + P],
                                                 prob[:, e // 2, (e % 2) * P:(e % 2) * P + P], P)
                            last.then_inc(wpe.step(f"T{half}"), 1)
                        pe.wait_ge(wa.sem, wa.at("T", c.w))
                        pe.wait_ge(wd.sem, wd.at("T", c.w))
                        pe.wait_ge(rp.sem, rp.at("v", c.n))
                        for kv in range(2):
                            for g in range(4):
                                e = (kv * 4 + g) * 2
                                at = (g * 2 + kv) * 64
                                for s in range(2):
                                    last = nc.tensor.matmul(ps[:, 1, at:at + 64], probT[:, e + s, :],
                                                            s_v[:, s, 64 * kv:64 * kv + 64], start=(s == 0), stop=(s == 1))
                        last.then_inc(wpe.step("o"), 1)
                    else:
                        pe.wait_ge(dd.sem, dd.at("p1", l))
                        for r in range(2):
                            transpose(ps[:, 4, r * P:(r + 1) * P], s_prob[:, r, 0:WIN], P)
                        for r in range(2):
                            last = transpose(ps[0:ROWS_S, 4, (2 + r) * P:(3 + r) * P], s_prob[:, r, WIN:WIN + ROWS_S], P)
                        last.then_inc(dpe.step("T"), 1)
                        pe.wait_ge(da.sem, da.at("T", l))
                        pe.wait_ge(dd.sem, dd.at("T", l))
                        pe.wait_ge(rp.sem, rp.at("v", c.n))
                        for b in range(NB):
                            r = slice(32 * (b % 4), 32 * (b % 4) + 32)
                            nc.tensor.matmul(ps[:, 5, 32 * b:32 * b + 32], cv[:, b, :], spT[:, b // 4, r],
                                             start=True, stop=False)
                            last = nc.tensor.matmul(ps[:, 5, 32 * b:32 * b + 32], s_v[0:ROWS_S, 0, :],
                                                    spN[0:ROWS_S, b // 4, r], start=False, stop=True)
                        last.then_inc(dpe.step("o"), 1)

                def heads_transposed(c):
                    rows = c.rows
                    pe.wait_ge(md.sem, md.at("rh", c.n))
                    if c.prompt:
                        pe.wait_ge(sdv.sem, sdv.at("h3", c.w))
                    apart(pe)
                    for k in range(4):
                        last = transpose(ps[:, 2, k * P:k * P + rows], cat[c.p][0:rows, k * P:(k + 1) * P], rows)
                    last.then_inc(cpe.step("T0"), 1)
                    if c.prompt:
                        pe.wait_ge(wd.sem, wd.at("o", c.w))
                        for k in range(4):
                            last = transpose(ps[:, 3, k * P:(k + 1) * P], cat[c.p][:, 512 + k * P:512 + (k + 1) * P], P)
                        last.then_inc(cpe.step("T1"), 1)
                    else:
                        pe.sem_inc(cpe.step("T1"), 1)

                def mix_step(f, h):
                    if f:
                        front_transposes(f, h is None)
                    if h:
                        heads_weights(h)
                    if f:
                        front_scores(f, h)
                    if h:
                        heads_out(h, f)
                    if f:
                        front_window(f)
                    if h:
                        heads_transposed(h)

                mix_step(prompt_chunk(l, 0, 0), None)
                with pe.Fori(0, CHUNKS // 2 - 1) as i:
                    mix_step(prompt_chunk(l, i, 1), prompt_chunk(l, i, 0))
                    mix_step(prompt_chunk(l, i + 1, 0), prompt_chunk(l, i, 1))
                mix_step(prompt_chunk(l, CHUNKS // 2 - 1, 1), prompt_chunk(l, CHUNKS // 2 - 1, 0))
                mix_step(decode_chunk(l), prompt_chunk(l, CHUNKS // 2 - 1, 1))
                mix_step(None, decode_chunk(l))
                barrier(pe, phase(l, 1))

                with pe.Fori(0, KT // 2) as i:
                    for q in range(2):
                        J = l * KT + i * 2 + q
                        pe.wait_ge(wo_hi_done, J + 1)
                        pe.wait_ge(wo_lo_done, J + 1)
                        for c in range(TCH):
                            pe.wait_ge(out_free, J * TCH + (c + 1))
                            tok = slice(c * NCH, (c + 1) * NCH)
                            for k in range(KT):
                                last = three(ps[:, c, 0:NCH], wo_hi[q][:, k, :], wo_lo[q][:, k, :],
                                             u_hi[:, k, tok], u_lo[:, k, tok], k == 0, k == KT - 1)
                            last.then_inc(out_ready, 1)
                barrier(pe, phase(l, 2))

                def norm_tiles(which):
                    base = (l * 2 + which) * TILES

                    def back(t, p, rows, first=False):
                        n = base + t
                        pe.wait_ge(na.sem, na.at("stage", n))
                        if not first:
                            pe.wait_ge(nd.sem, nd.at("res", n - 2))
                        for k in range(KT):
                            last = transpose(ps[0:rows, 2 * p + k // 4, (k % 4) * P:(k % 4 + 1) * P],
                                             stage[which][:, k, 0:rows], P)
                        last.then_inc(npe.step("T"), 1)

                    def again(t, p, rows):
                        pe.wait_ge(npl.sem, npl.at("b", base + t))
                        split_tile(base + TILES + t, p, rows, xn[which])

                    back(0, 0, P, first=True)
                    back(1, 1, P, first=True)
                    with pe.Fori(0, CHUNKS // 2 - 1) as i:
                        for p in range(2):
                            back(i * 2 + (p + 2), p, P)
                            again(i * 2 + p, p, P)
                    back(CHUNKS, 0, ROWS_S)
                    again(CHUNKS - 2, 0, P)
                    again(CHUNKS - 1, 1, P)
                    again(CHUNKS, 0, ROWS_S)

                norm_tiles(0)
                barrier(pe, phase(l, 3))

                def up(b, q):
                    B = l * FBLOCKS + b
                    pe.wait_ge(wu_hi_done, B + 1)
                    pe.wait_ge(wu_lo_done, B + 1)
                    for f in range(2):
                        for c in range(TCH):
                            pe.wait_ge(up_free, B * 6 + (f * TCH + c + 1))
                            tok = slice(c * NCH, (c + 1) * NCH)
                            cols = slice(f * P, (f + 1) * P)
                            for k in range(KT):
                                last = three(ps[:, c, 0:NCH], wu_hi[:, k, cols], wu_lo[:, k, cols],
                                             v_hi[:, k, tok], v_lo[:, k, tok], k == 0, k == KT - 1)
                            last.then_inc(up_ready, 1)

                def down(b, q):
                    B = l * FBLOCKS + b
                    pe.wait_ge(wd_hi_done, B + 1)
                    pe.wait_ge(wd_lo_done, B + 1)
                    pe.wait_ge(hid_lo_done, (B + 1) * 6)
                    for d in range(KT):
                        for c in range(TCH):
                            pe.wait_ge(down_free, B * (KT * TCH) + (d * TCH + c + 1))
                            tok = slice(c * NCH, (c + 1) * NCH)
                            cols = slice(d * P, (d + 1) * P)
                            for f in range(2):
                                last = three(ps[:, 3 + c, 0:NCH], wd_hi[:, f, cols], wd_lo[:, f, cols],
                                             hid_hi[q][:, f, tok], hid_lo[q][:, f, tok], f == 0, f == 1)
                            last.then_inc(down_ready, 1)

                up(0, 0)
                with pe.Fori(0, FBLOCKS // 2 - 1) as i:
                    for q in range(2):
                        up(i * 2 + (q + 1), 1 - q)
                        down(i * 2 + q, q)
                up(FBLOCKS - 1, 1)
                down(FBLOCKS - 2, 0)
                down(FBLOCKS - 1, 1)
                barrier(pe, phase(l, 4))
                norm_tiles(1)
                barrier(pe, phase(l, 5))

        @block.scalar
        def _(act):
            nc.scalar.preload_act_table_set("natural_log_exp_and_others")
            for S in (lba, na, nr, sa, ga, ma, ca, wa, da):
                act.sem_inc(S.sem, 1)
            act.sem_inc(proj_free, 3)
            copy = nc.scalar.copy
            dest = (u_hi, v_hi)

            def split_tile(m, t, p, rows, out):
                act.wait_ge(spe.sem, spe.at("T", m))
                copy(out[:, :, bass.ds(t * P, rows)],
                     ps[:, 4 + 2 * p:6 + 2 * p, :].rearrange("p b (k c) -> p (b k) c", c=P)[:, :, 0:rows])\
                    .then_inc(sa.step("hi"), 1)

            act.wait_ge(lbd.sem, lbd.at("sub1", 0))
            nc.scalar.activation(lb_exp[:], lb_raw[:], ACT.Exp).then_inc(lba.step("exp"), 1)
            for t in range(TILES):
                split_tile(t, t, t % 2, tile_rows(t), u_hi)
            barrier(act, 1)

            with act.Fori(0, DEPTH) as l:
                def split_wi(g, q, free):
                    G = l * GROUPS + g
                    act.wait_ge(wi_in, (G + 1) * 16)
                    if free:
                        act.wait_ge(proj_ready, (G - 1) * TILES)
                    copy(wi_hi[q][:], wi_raw[:]).then_inc(wi_hi_done, 1)

                def evacuate(g, q, i):
                    G = l * GROUPS + g
                    for t in range(TILES):
                        rows = tile_rows(t)
                        act.wait_ge(proj_ready, G * TILES + (t + 1))
                        act.wait_ge(h_stored[t % 3], (G * 3 + t // 3) * 16)
                        copy(h_out[t % 3][0:rows, :], ps[0:rows, t % 3, 0:GROUP]).then_inc(proj_free, 1)

                split_wi(0, 0, False)
                split_wi(1, 1, False)
                with act.Fori(0, GROUPS // 2 - 1) as i:
                    for q in range(2):
                        evacuate(i * 2 + q, q, i)
                        split_wi(i * 2 + (q + 2), q, True)
                evacuate(GROUPS - 2, 0, 0)
                evacuate(GROUPS - 1, 1, 0)
                barrier(act, phase(l, 0))

                def front_gates(c):
                    act.wait_ge(gd.sem, gd.at("clip", c.n))
                    nc.scalar.activation(g_e[:], g_e[:], ACT.Exp).then_inc(ga.step("e"), 1)
                    act.wait_ge(tpe.sem, tpe.at("h", c.n))
                    act.wait_ge(gp.sem, gp.before(c.n))
                    act.wait_ge(gd.sem, gd.at("clip", c.n))
                    copy(g_q[:], ps[:, 0, 256:512].rearrange("p (a b) -> p a b", a=2)).then_inc(ga.step("q"), 1)
                    act.wait_ge(tpe.sem, tpe.at("r", c.n))
                    act.wait_ge(rd.sem, rd.at("qi", c.n))
                    copy(r_kT[:], ps[:, 1, P:2 * P]).then_inc(ga.step("kTr"), 1)
                    copy(s_kT[:, c.p, :], ps[:, 1, 2 * P:3 * P]).then_inc(ga.step("kTs"), 1)
                    act.wait_ge(tpe.sem, tpe.at("q", c.n))
                    copy(s_qT[:], ps[:, 2, :].rearrange("p (a b) -> p a b", a=4)).then_inc(ga.step("qT"), 1)
                    act.wait_ge(gd.sem, gd.at("f1", c.n))
                    nc.scalar.activation(g_f[:], g_f[:], ACT.Ln).then_inc(ga.step("f"), 1)
                    act.wait_ge(gg.sem, gg.at("c1", c.n))
                    nc.scalar.activation(gate[c.p][:], gate[c.p][:], ACT.Exp, scale=-1.0).then_inc(ga.step("eg"), 1)
                    act.wait_ge(gd.sem, gd.at("b1", c.n))
                    nc.scalar.activation(g_eb[c.p][:], g_b[:], ACT.Exp).then_inc(ga.step("eb"), 1)
                    act.wait_ge(gd.sem, gd.at("al6", c.n))
                    nc.scalar.activation(lev_e[:], lev_e[:], ACT.Exp).then_inc(ga.step("E"), 1)
                    nc.scalar.activation(g_ka[c.p][:], g_ka[c.p][:], ACT.Exp).then_inc(ga.step("ka"), 1)
                    if not c.prompt:
                        act.wait_ge(dpe.sem, dpe.at("ckT", l))
                        copy(ckT[:], ps[:, 4:6, :].rearrange("p b (k c) -> p (b k) c", c=P)).then_inc(da.step("ck"), 1)

                def heads_rms(c):
                    rows = c.rows
                    act.wait_ge(mpe.sem, mpe.at("o", c.n))
                    nc.scalar.activation(rms_sq[0:rows], ps[0:rows, 0, :].rearrange("p (a b) -> p a b", a=8), ACT.Square)\
                        .then_inc(ma.step("sq"), 1)
                    act.wait_ge(md.sem, md.at("ms", c.n))
                    nc.scalar.activation(rms_l[0:rows], rms_v[0:rows], ACT.Ln).then_inc(ma.step("ln"), 1)
                    act.wait_ge(ma.sem, ma.at("ln", c.n))
                    nc.scalar.activation(rms[0:rows], rms_l[0:rows], ACT.Exp, scale=-0.5).then_inc(ma.step("r"), 1)

                def front_window(c):
                    rows = c.rows
                    if c.prompt:
                        act.wait_ge(wd.sem, wd.at("sk", c.w))
                        for h in range(8):
                            nc.scalar.activation(prob[:, h, :], prob[:, h, :], ACT.Exp, bias=nm[:, h:h + 1], scale=0.125,
                                                 accum_out=ssum[:, h:h + 1]).then_inc(wa.step(f"e{h}"), 1)
                        nc.scalar.activation(esk[:], sk[:], ACT.Exp).then_inc(wa.step("sk"), 1)
                        act.wait_ge(wpe.sem, wpe.at("T0", c.w))
                        copy(probT[:, 0:8, :], ps[:, 4:6, :].rearrange("p b (k c) -> p (b k) c", c=P))\
                            .then_inc(wa.step("T"), 1)
                    else:
                        act.wait_ge(dd.sem, dd.at("sk", l))
                        for r in range(2):
                            nc.scalar.activation(s_prob[:, r, :], s_prob[:, r, :], ACT.Exp, bias=nm[:, r:r + 1], scale=0.125,
                                                 accum_out=ssum[:, r:r + 1]).then_inc(da.step(f"e{r}"), 1)
                        nc.scalar.activation(esk[:, 0:2], sk[:, 0:2], ACT.Exp).then_inc(da.step("sk"), 1)
                        act.wait_ge(dpe.sem, dpe.at("T", l))
                        act.wait_ge(dd.sem, dd.at("T", l))
                        copy(spN[0:rows, :, :], ps[0:rows, 4, 256:512].rearrange("p (a b) -> p a b", a=2))\
                            .then_inc(da.step("T"), 1)
                        act.wait_ge(dpe.sem, dpe.at("o", l))
                        for kv in range(2):
                            d = slice(64 * kv, 64 * kv + 64)
                            src = ps[d, 5, 0:256].rearrange("p (b kv g l) -> p kv g b l", b=NB, kv=2, g=4)[:, kv]
                            copy(u_hi[d, 4:8, SEQ:TOK].rearrange("p g (b l) -> p g b l", b=NB), src)\
                                .then_inc(da.step(f"o{kv}"), 1)

                def heads_high(c):
                    act.wait_ge(cpe.sem, cpe.at("T1", c.n))
                    if c.prompt:
                        copy(u_hi[:, :, bass.ds(c.t * P, P)], ps[:, 2:4, :].rearrange("p b (k c) -> p (b k) c", c=P))\
                            .then_inc(ca.step("hi"), 1)
                    else:
                        copy(u_hi[:, 0:4, SEQ:TOK], ps[:, 2, :].rearrange("p (k c) -> p k c", c=P)[:, :, 0:c.rows])\
                            .then_inc(ca.step("hi"), 1)

                def mix_step(f, h):
                    if f:
                        front_gates(f)
                    if h:
                        heads_rms(h)
                    if f:
                        front_window(f)
                    if h:
                        heads_high(h)

                mix_step(prompt_chunk(l, 0, 0), None)
                with act.Fori(0, CHUNKS // 2 - 1) as i:
                    mix_step(prompt_chunk(l, i, 1), prompt_chunk(l, i, 0))
                    mix_step(prompt_chunk(l, i + 1, 0), prompt_chunk(l, i, 1))
                mix_step(prompt_chunk(l, CHUNKS // 2 - 1, 1), prompt_chunk(l, CHUNKS // 2 - 1, 0))
                mix_step(decode_chunk(l), prompt_chunk(l, CHUNKS // 2 - 1, 1))
                mix_step(None, decode_chunk(l))
                barrier(act, phase(l, 1))

                def split_wo(j, q, free):
                    J = l * KT + j
                    act.wait_ge(wo_in, (J + 1) * 48)
                    if free:
                        act.wait_ge(out_ready, (J - 1) * TCH)
                    copy(wo_hi[q][:], wo_raw[:]).then_inc(wo_hi_done, 1)

                split_wo(0, 0, False)
                split_wo(1, 1, False)
                with act.Fori(0, KT // 2 - 1) as i:
                    for q in range(2):
                        split_wo(i * 2 + (q + 2), q, True)
                barrier(act, phase(l, 2))

                def norm_tiles(which):
                    base = (l * 2 + which) * TILES
                    out = (v_hi, u_hi)[which]

                    def back(t, p, rows):
                        n = base + t
                        act.wait_ge(npe.sem, npe.before(n))
                        copy(stage[which][:, :, 0:rows], acc[:, :, bass.ds(t * P, rows)]).then_inc(na.step("stage"), 1)

                    def root(t, p, rows):
                        n = base + t
                        rs = slice(0, rows)
                        act.wait_ge(nd.sem, nd.at("var", n))
                        nc.scalar.activation(logv[rs, p:p + 1], var[rs, p:p + 1], ACT.Ln).then_inc(nr.step("ln"), 1)
                        act.wait_ge(nr.sem, nr.at("ln", n))
                        nc.scalar.activation(rstd[rs, p:p + 1], logv[rs, p:p + 1], ACT.Exp, scale=-0.5)\
                            .then_inc(nr.step("r"), 1)

                    def high(t, p, rows):
                        split_tile(base + TILES + t, t, p, rows, out)

                    back(0, 0, P)
                    back(1, 1, P)
                    root(0, 0, P)
                    back(2, 0, P)
                    with act.Fori(0, CHUNKS // 2 - 2) as i:
                        for q in range(2):
                            root(i * 2 + (1 + q), 1 - q, P)
                            back(i * 2 + (3 + q), 1 - q, P)
                            high(i * 2 + q, q, P)
                    root(CHUNKS - 3, 1, P)
                    back(CHUNKS - 1, 1, P)
                    high(CHUNKS - 4, 0, P)
                    root(CHUNKS - 2, 0, P)
                    back(CHUNKS, 0, ROWS_S)
                    high(CHUNKS - 3, 1, P)
                    root(CHUNKS - 1, 1, P)
                    high(CHUNKS - 2, 0, P)
                    root(CHUNKS, 0, ROWS_S)
                    high(CHUNKS - 1, 1, P)
                    high(CHUNKS, 0, ROWS_S)

                def split_wu(b):
                    B = l * FBLOCKS + b
                    act.wait_ge(wu_in, (B + 1) * 16)
                    act.wait_ge(up_ready, B * 6)
                    copy(wu_hi[:], wu_raw[:]).then_inc(wu_hi_done, 1)

                norm_tiles(0)
                split_wu(0)
                barrier(act, phase(l, 3))

                def split_wd(b):
                    B = l * FBLOCKS + b
                    act.wait_ge(wd_in, (B + 1) * 16)
                    act.wait_ge(down_ready, B * (KT * TCH))
                    copy(wd_hi[:], wd_raw[:]).then_inc(wd_hi_done, 1)

                def hidden(b, q):
                    B = l * FBLOCKS + b
                    def high(f, c):
                        act.wait_ge(sq_done, B * 6 + (f * TCH + c + 1))
                        copy(hid_hi[q][:, f, c * NCH:(c + 1) * NCH], sq[c][:]).then_inc(hid_hi_done, 1)

                    units = [(f, c) for f in range(2) for c in range(TCH)]
                    for u, (f, c) in enumerate(units):
                        act.wait_ge(up_ready, B * 6 + (u + 1))
                        nc.scalar.activation(relu[c][:], ps[:, c, 0:NCH], ACT.Relu).then_inc(up_free, 1)
                        if u:
                            high(*units[u - 1])
                    high(*units[-1])

                hidden(0, 0)
                with act.Fori(0, FBLOCKS // 2 - 1) as i:
                    for q in range(2):
                        split_wu(i * 2 + (q + 1))
                        split_wd(i * 2 + q)
                        hidden(i * 2 + (q + 1), 1 - q)
                split_wu(FBLOCKS - 1)
                split_wd(FBLOCKS - 2)
                hidden(FBLOCKS - 1, 1)
                split_wd(FBLOCKS - 1)
                barrier(act, phase(l, 4))
                norm_tiles(1)
                barrier(act, phase(l, 5))

        @block.vector
        def _(dve):
            v = nc.vector
            for S in (lbd, zd, nd, sd, gd, gg, rd, hd, md, cd, wd, sdv, dd):
                dve.sem_inc(S.sem, 1)
            dve.sem_inc(out_free, 3)
            dve.sem_inc(up_free, 3)
            dve.sem_inc(down_free, 3)

            def split_tile(m, t, p, rows, hi, lo):
                dve.wait_ge(sa.sem, sa.at("hi", m))
                tok = bass.ds(t * P, rows)
                v.tensor_tensor(lo[:, :, tok], ps[:, 4 + 2 * p:6 + 2 * p, :]
                                .rearrange("p b (k c) -> p (b k) c", c=P)[:, :, 0:rows], hi[:, :, tok], ALU.subtract)\
                    .then_inc(sd.step("lo"), 1)

            def newton(r, x, t, dve, S, n):
                v.tensor_tensor(t, r, r, ALU.mult).then_inc(S.step("n0"), 1)
                dve.wait_ge(S.sem, S.at("n0", n))
                v.scalar_tensor_tensor(out=t, in0=t, scalar=-0.5, in1=x, op0=ALU.mult, op1=ALU.mult)\
                    .then_inc(S.step("n1"), 1)
                dve.wait_ge(S.sem, S.at("n1", n))
                v.scalar_tensor_tensor(out=r, in0=t, scalar=1.5, in1=r, op0=ALU.add, op1=ALU.mult)\
                    .then_inc(S.step("rstd"), 1)

            dve.wait_ge(const_in, 48)
            v.tensor_tensor(lb_tmp[:, 0:2], lb_raw[:, 0, :], lb_raw[:, 1, :], ALU.max).then_inc(lbd.step("max"), 1)
            dve.wait_ge(lbd.sem, lbd.at("max", 0))
            v.tensor_tensor(lb_raw[:, 0, :], lb_raw[:, 0, :], lb_tmp[:, 0:2], ALU.subtract).then_inc(lbd.step("sub0"), 1)
            v.tensor_tensor(lb_raw[:, 1, :], lb_raw[:, 1, :], lb_tmp[:, 0:2], ALU.subtract).then_inc(lbd.step("sub1"), 1)
            dve.wait_ge(lba.sem, lba.at("exp", 0))
            v.tensor_tensor(lb_tmp[:, 2:4], lb_exp[:, 0, :], lb_exp[:, 1, :], ALU.add).then_inc(lbd.step("sum"), 1)
            dve.wait_ge(lbd.sem, lbd.at("sum", 0))
            v.reciprocal(lb_tmp[:, 2:4], lb_tmp[:, 2:4]).then_inc(lbd.step("inv"), 1)
            dve.wait_ge(lbd.sem, lbd.at("inv", 0))
            v.tensor_tensor(lb_exp[:, 0, :], lb_exp[:, 0, :], lb_tmp[:, 2:4], ALU.mult).then_inc(lbd.step("p0"), 1)
            v.tensor_tensor(lb_exp[:, 1, :], lb_exp[:, 1, :], lb_tmp[:, 2:4], ALU.mult).then_inc(lbd.step("p1"), 1)
            dve.wait_ge(lbd.sem, lbd.at("p1", 0))
            v.tensor_tensor(lb_tmp[:, 0:2], lb_exp[:, 0, :], lb_exp[:, 1, :], ALU.add).then_inc(lbd.step("cum"), 1)
            v.tensor_tensor(lb_all[:, 0, :], lb_exp[:, 0, :], lb_exp[:, 0, :], ALU.subtract).then_inc(lbd.step("lb0"), 1)
            dve.wait_ge(lbd.sem, lbd.at("cum", 0))
            v.tensor_tensor(lb_all[:, 1, :], lb_tmp[:, 0:2], lb_exp[:, 0, :], ALU.subtract).then_inc(lbd.step("lb1"), 1)
            for t in range(TILES):
                split_tile(t, t, t % 2, tile_rows(t), u_hi, u_lo)
            barrier(dve, 1)

            with dve.Fori(0, DEPTH) as l:
                def split_wi(g, q, free):
                    G = l * GROUPS + g
                    dve.wait_ge(wi_hi_done, G + 1)
                    if free:
                        dve.wait_ge(proj_ready, (G - 1) * TILES)
                    v.tensor_tensor(wi_lo[q][:], wi_raw[:], wi_hi[q][:], ALU.subtract).then_inc(wi_lo_done, 1)

                split_wi(0, 0, False)
                split_wi(1, 1, False)
                with dve.Fori(0, GROUPS // 2 - 1) as i:
                    for q in range(2):
                        split_wi(i * 2 + (q + 2), q, True)
                barrier(dve, phase(l, 0))

                v.tensor_copy(lb[:], lb_all[:, bass.ds(l, 1), :].rearrange("p l t -> p (l t)"))\
                    .then_inc(zd.step("lb"), 1)
                dve.wait_ge(zd.sem, zd.at("lb", l))
                v.tensor_scalar(omlb[:], lb[:], -1.0, 1.0, ALU.mult, ALU.add).then_inc(zd.step("omlb"), 1)
                v.memset(st_r[:], 0.0).then_inc(zd.step("r"), 1)
                v.memset(st_h[:], 0.0).then_inc(zd.step("h"), 1)
                v.memset(s_kT[:, 1, :], 0.0).then_inc(zd.step("kT"), 1)
                v.memset(s_v[:, 1, :], 0.0).then_inc(zd.step("v"), 1)
                v.memset(r_qx[:], 0.0).then_inc(zd.step("qx"), 1)
                v.memset(s0_r[:], 0.0).then_inc(zd.step("sr"), 1)
                v.memset(s0_h[:], 0.0).then_inc(zd.step("sh"), 1)
                v.memset(lev_x[:], 0.0).then_inc(zd.step("lx"), 1)
                v.memset(lev_r[:], 0.0).then_inc(zd.step("lr"), 1)
                dve.wait_ge(zd.sem, zd.at("lr", l))
                dve.wait_ge(par_in, (l * 8 + 4) * 16)
                apart(dve)

                def front_gates(c):
                    var = "" if c.prompt else "s"
                    dve.wait_ge(tpe.sem, tpe.at("h", c.n))
                    v.tensor_scalar(g_e[:], ps[:, 0, 0:256].rearrange("p (a b) -> p a b", a=2), -1.0, 80.0,
                                    ALU.mult, ALU.min).then_inc(gd.step("clip"), 1)
                    dve.wait_ge(tpe.sem, tpe.at("r", c.n))
                    for h in range(4):
                        d = slice(32 * h, 32 * h + 32)
                        v.tensor_copy(r_qx[d, h, :], ps[d, 1, 0:P]).then_inc(rd.step(f"x{h}"), 1)
                    v.tensor_tensor(r_qi[c.p][:], ps[:, 1, 0:P], cst("inter" + var), ALU.mult).then_inc(rd.step("qi"), 1)
                    dve.wait_ge(ga.sem, ga.at("e", c.n))
                    v.tensor_scalar(g_r[:], g_e[:], 1.0, None, ALU.add).then_inc(gd.step("one"), 1)
                    dve.wait_ge(gd.sem, gd.at("one", c.n))
                    v.reciprocal(g_r[:], g_r[:]).then_inc(gd.step("r"), 1)
                    dve.wait_ge(gd.sem, gd.at("r", c.n))
                    v.tensor_tensor(g_s[:], g_e[:], g_r[:], ALU.mult).then_inc(gd.step("s"), 1)
                    dve.wait_ge(gd.sem, gd.at("s", c.n))
                    dve.wait_ge(gp.sem, gp.before(c.n))
                    for j in range(2):
                        v.tensor_scalar(g_k[:, j, :], g_s[:, j, :], omlb[:, j:j + 1], None, ALU.mult)\
                            .then_inc(gd.step(f"k{j}"), 1)
                    for j in range(2):
                        v.scalar_tensor_tensor(out=g_f[:, j, :], in0=g_s[:, j, :], scalar=lb[:, j:j + 1], in1=g_r[:, j, :],
                                               op0=ALU.mult, op1=ALU.add).then_inc(gd.step(f"f{j}"), 1)
                    for j, at in enumerate((RG, HGT)):
                        v.tensor_scalar(gate[c.p][:, j, :], hb[c.p][:, at:at + 256], -80.0, None, ALU.max)\
                            .then_inc(gg.step(f"c{j}"), 1)

                def heads_keys(c):
                    dve.wait_ge(mpe.sem, mpe.at("kt", c.n))
                    v.tensor_copy(g_kt[:], ps[:, 3, 0:256].rearrange("p (a b) -> p a b", a=2)).then_inc(hd.step("kt"), 1)

                def heads_weights(c):
                    dve.wait_ge(mpe.sem, mpe.at("lev1", c.n))
                    v.tensor_copy(diag[:], ps[:, 7, 256:260]).then_inc(hd.step("diag"), 1)
                    dve.wait_ge(hd.sem, hd.at("diag", c.n))
                    v.tensor_tensor(hg_a[:], ident.unsqueeze(1).broadcast_to([P, 4, P]),
                                    diag[:, :].unsqueeze(2).broadcast_to([P, 4, P]), ALU.mult).then_inc(hd.step("a"), 1)
                    before = "a"
                    for i in LEVEL_ORDER:
                        half = HALVES[i]
                        dve.wait_ge(hd.sem, hd.at(before, c.n))
                        if i == 0:
                            dve.wait_ge(mpe.sem, mpe.at("lev0", c.n))
                        apart(dve)
                        at = (i % 2) * 256
                        v.copy_predicated(hg_a[:, :, :].rearrange("p h (k w) -> p h k w", w=2 * half)[:, :, :, half:],
                                          lev_mask[:, 0 if c.prompt else 1, i, :].unsqueeze(1).broadcast_to([P, 4, 64])
                                          .rearrange("p h (k w) -> p h k w", w=half),
                                          ps[:, 4 + i // 2, at:at + 256].rearrange("p (h k w) -> p h k w", h=4, w=half))\
                            .then_inc(hd.step(f"c{i}"), 1)
                        before = f"c{i}"

                def front_levels(c):
                    dve.wait_ge(ga.sem, ga.at("f", c.n))
                    carry = cst("run").broadcast_to([P, P]) if c.prompt else cst("runs")
                    for j in range(2):
                        v.tensor_tensor_scan(g_b[:, j, :], carry, g_f[:, j, :], 0.0, ALU.mult, ALU.add)\
                            .then_inc(gd.step(f"b{j}"), 1)
                    v.tensor_tensor(g_p[c.p][:], g_q[:], g_k[:], ALU.mult).then_inc(gd.step("p"), 1)
                    dve.wait_ge(gd.sem, gd.at("b1", c.n))
                    if c.prompt:
                        v.tensor_tensor(g_ka[c.p][:], g_b[:, :, P - 1:P].broadcast_to([P, 2, P]), g_b[:], ALU.subtract)\
                            .then_inc(gd.step("ka"), 1)
                    else:
                        gb4 = g_b[:, :, :].rearrange("p a (k w) -> p (a k) w", w=NL)
                        v.tensor_tensor(g_ka[c.p][:, :, :].rearrange("p a (k w) -> p (a k) w", w=NL),
                                        gb4[:, :, NL - 1:NL].broadcast_to([P, 2 * P // NL, NL]), gb4, ALU.subtract)\
                            .then_inc(gd.step("ka"), 1)
                    for i, half in enumerate(HALVES):
                        gb = g_b[:, :, :].rearrange("p a (k w) -> p (a k) w", w=2 * half)
                        to = lev_e[:, i, :, :].rearrange("p a (k w) -> p (a k) w", w=2 * half)
                        mid = gb[:, :, half - 1:half].broadcast_to([P, P // half, half])
                        v.tensor_tensor(to[:, :, half:], gb[:, :, half:], mid, ALU.subtract).then_inc(gd.step(f"ar{i}"), 1)
                        v.tensor_tensor(to[:, :, 0:half], mid, gb[:, :, 0:half], ALU.subtract)\
                            .then_inc(gd.step(f"al{i}"), 1)

                def front_masks(c):
                    var = "" if c.prompt else "s"
                    dve.wait_ge(rpe.sem, rpe.at("ret", c.n))
                    v.tensor_tensor(r_a[c.p][:], ps[:, 3, :].rearrange("p (a b) -> p a b", a=4),
                                    cst("dec" + var).rearrange("p (a b) -> p a b", a=4), ALU.mult).then_inc(rd.step("a"), 1)
                    if c.prompt:
                        dve.wait_ge(wpe.sem, wpe.at("s", c.w))
                        v.tensor_tensor(prob[:], ps[:, 4:8, :].rearrange("p b (h s) -> p (b h) s", s=256),
                                        swa_mask[:, c.p:c.p + 2, :].rearrange("p a b -> p (a b)").unsqueeze(1)
                                        .broadcast_to([P, 8, 256]), ALU.add).then_inc(wd.step("s"), 1)
                        dve.wait_ge(wd.sem, wd.at("s", c.w))
                        v.tensor_copy(swa_mask[:, 1, :], cst("band")).then_inc(wd.step("band"), 1)
                        v.tensor_reduce(mx[:], prob[:], axis=AX, op=ALU.max).then_inc(wd.step("mx"), 1)
                        S, L, K, sink = wd, c.w, 8, sink_b[:]
                    else:
                        v.memset(qxs[:], 0.0).then_inc(dd.step("zx"), 1)
                        dve.wait_ge(ga.sem, ga.at("qT", c.n))
                        dve.wait_ge(dd.sem, dd.at("zx", l))
                        for kv in range(2):
                            d = slice(64 * kv, 64 * kv + 64)
                            v.tensor_copy(qxs[d, :, kv, :, :],
                                          ps[d, 2, :].rearrange("p (g t) -> p g t", g=4)[:, :, 0:ROWS_S]
                                          .rearrange("p g (b l) -> p b g l", b=NB)).then_inc(dd.step(f"x{kv}"), 1)
                        dve.wait_ge(dpe.sem, dpe.at("s", l))
                        v.tensor_tensor(s_prob[:], ps[:, 6:8, 0:WIN + ROWS_S],
                                        cst("smask").rearrange("p (a b) -> p a b", a=2), ALU.add).then_inc(dd.step("s"), 1)
                        dve.wait_ge(dd.sem, dd.at("s", l))
                        v.tensor_reduce(mx[:, 0:2], s_prob[:], axis=AX, op=ALU.max).then_inc(dd.step("mx"), 1)
                        S, L, K, sink = dd, l, 2, sink_r[:, 0:1].broadcast_to([P, 2])
                    dve.wait_ge(S.sem, S.at("mx", L))
                    v.scalar_tensor_tensor(out=m[:, 0:K], in0=mx[:, 0:K], scalar=0.125, in1=sink, op0=ALU.mult,
                                           op1=ALU.max).then_inc(S.step("m"), 1)
                    dve.wait_ge(S.sem, S.at("m", L))
                    v.tensor_scalar(nm[:, 0:K], m[:, 0:K], -1.0, None, ALU.mult).then_inc(S.step("nm"), 1)
                    v.tensor_tensor(sk[:, 0:K], sink, m[:, 0:K], ALU.subtract).then_inc(S.step("sk"), 1)

                def front_silu(c):
                    x, to = hb[c.p], gate[c.p]
                    dve.wait_ge(ga.sem, ga.at("eg", c.n))
                    v.tensor_scalar(to[:], to[:], 1.0, None, ALU.add).then_inc(gg.step("one"), 1)
                    dve.wait_ge(gg.sem, gg.at("one", c.n))
                    v.reciprocal(to[:], to[:]).then_inc(gg.step("r"), 1)
                    dve.wait_ge(gg.sem, gg.at("r", c.n))
                    v.tensor_tensor(to[:, 0, :], x[:, RG:RG + 256], to[:, 0, :], ALU.mult).then_inc(gg.step("s0"), 1)
                    v.tensor_tensor(to[:, 1, :], x[:, HGT:HGT + 256], to[:, 1, :], ALU.mult).then_inc(gg.step("s1"), 1)

                def heads_merge(c):
                    rows = c.rows
                    dve.wait_ge(ma.sem, ma.at("sq", c.n))
                    v.tensor_reduce(rms[0:rows], rms_sq[0:rows], axis=AX, op=ALU.add).then_inc(md.step("ss"), 1)
                    dve.wait_ge(md.sem, md.at("ss", c.n))
                    v.tensor_scalar(rms_v[0:rows], rms[0:rows], 1.0 / 64, RMS_EPS, ALU.mult, ALU.add)\
                        .then_inc(md.step("ms"), 1)
                    dve.wait_ge(ma.sem, ma.at("r", c.n))
                    newton(rms[0:rows], rms_v[0:rows], rms_t[0:rows], dve, md, c.n)
                    dve.wait_ge(md.sem, md.at("rstd", c.n))
                    dve.wait_ge(rp.sem, rp.at("sw", c.n))
                    both = gate[c.p][0:rows].rearrange("p a (h d) -> p (a h) d", h=4)
                    v.tensor_tensor(both, both, rms[0:rows].unsqueeze(2).broadcast_to([rows, 8, 64]), ALU.mult)\
                        .then_inc(md.step("sr"), 1)
                    dve.wait_ge(mpe.sem, mpe.at("st", c.n))
                    for h in range(4):
                        d, e = slice(32 * h, 32 * h + 32), slice(64 * h, 64 * h + 64)
                        if c.prompt:
                            v.scalar_tensor_tensor(out=st_r[d, e], in0=st_r[d, e], scalar=float(np.exp(P * LG[h])),
                                                   in1=ps[d, 2, e], op0=ALU.mult, op1=ALU.add).then_inc(sdv.step(f"r{h}"), 1)
                        else:
                            add = ps[d, 4:8, :].rearrange("p b (e c) -> p (b e) c", e=2)[:, :, e]
                            v.scalar_tensor_tensor(out=s0_r[d, :, e], in0=s0_r[d, :, e], scalar=float(np.exp(NL * LG[h])),
                                                   in1=add, op0=ALU.mult, op1=ALU.add).then_inc(dd.step(f"r{h}"), 1)
                    if not c.prompt:
                        last_b = g_eb[c.p][:, :, 0:ROWS_S].rearrange("p a (b l) -> p a b l", b=NB)[:, :, :, NL - 1:NL]
                        v.tensor_tensor(s0_h[:], s0_h[:], last_b.broadcast_to([P, 2, NB, P]), ALU.mult)\
                            .then_inc(dd.step("hm"), 1)
                        dve.wait_ge(dd.sem, dd.at("hm", l))
                        dve.wait_ge(dpe.sem, dpe.at("st_h", l))
                    for h in range(4):
                        pr, j = h // 2, h % 2
                        d = slice(64 * j, 64 * j + 64)
                        if c.prompt:
                            a = 256 + pr * P + 64 * j
                            v.scalar_tensor_tensor(out=st_h[d, pr, d], in0=st_h[d, pr, d],
                                                   scalar=g_eb[c.p][d, pr, P - 1:P],
                                                   in1=ps[d, 2, a:a + 64], op0=ALU.mult, op1=ALU.add)\
                                .then_inc(sdv.step(f"h{h}"), 1)
                        else:
                            add = ps[d, 4 + 2 * pr:6 + 2 * pr, :].rearrange("p b (e c) -> p (b e) c", e=4)[:, :, d]
                            v.tensor_tensor(s0_h[d, pr, :, d], s0_h[d, pr, :, d], add, ALU.add)\
                                .then_inc(dd.step(f"h{h}"), 1)
                    dve.wait_ge(md.sem, md.at("sr", c.n))
                    v.tensor_tensor(cat[c.p][0:rows, 0:512], ps[0:rows, 0, :], gate[c.p][0:rows]
                                    .rearrange("p a b -> p (a b)"), ALU.mult).then_inc(md.step("rh"), 1)

                def front_window(c):
                    S2, S, L, K = (wa, wd, c.w, 8) if c.prompt else (da, dd, l, 2)
                    dve.wait_ge(S2.sem, S2.at("sk", L))
                    v.tensor_tensor(den[:, 0:K], ssum[:, 0:K], esk[:, 0:K], ALU.add).then_inc(S.step("den"), 1)
                    dve.wait_ge(S.sem, S.at("den", L))
                    v.reciprocal(rden[:, 0:K], den[:, 0:K]).then_inc(S.step("rden"), 1)
                    dve.wait_ge(S.sem, S.at("rden", L))
                    if c.prompt:
                        dve.wait_ge(wpe.sem, wpe.at("T1", c.w))
                        v.tensor_copy(probT[:, 8:16, :], ps[:, 6:8, :].rearrange("p b (k c) -> p (b k) c", c=P))\
                            .then_inc(wd.step("T"), 1)
                        dve.wait_ge(wpe.sem, wpe.at("o", c.w))
                        v.tensor_tensor(cat[c.p][:, 512:1024].rearrange("p (g k d) -> p g k d", g=4, k=2),
                                        ps[:, 1, :].rearrange("p (g k d) -> p g k d", g=4, k=2),
                                        rden[:, :].rearrange("p (k g) -> p g k", k=2).unsqueeze(3)
                                        .broadcast_to([P, 4, 2, 64]), ALU.mult).then_inc(wd.step("o"), 1)
                    else:
                        for r in range(2):
                            v.tensor_scalar(s_prob[:, r, :], s_prob[:, r, :], rden[:, r:r + 1], None, ALU.mult)\
                                .then_inc(dd.step(f"p{r}"), 1)
                        dve.wait_ge(dpe.sem, dpe.at("T", l))
                        v.tensor_copy(spT[:], ps[:, 4, 0:256].rearrange("p (a b) -> p a b", a=2)).then_inc(dd.step("T"), 1)
                        for kv in range(2):
                            d = slice(64 * kv, 64 * kv + 64)
                            dve.wait_ge(da.sem, da.at(f"o{kv}", l))
                            src = ps[d, 5, 0:256].rearrange("p (b kv g l) -> p kv g b l", b=NB, kv=2, g=4)[:, kv]
                            tok = (d, slice(4, 8), slice(SEQ, TOK))
                            v.tensor_tensor(u_lo[tok].rearrange("p g (b l) -> p g b l", b=NB), src,
                                            u_hi[tok].rearrange("p g (b l) -> p g b l", b=NB), ALU.subtract)\
                                .then_inc(dd.step(f"o{kv}"), 1)

                def heads_low(c):
                    dve.wait_ge(ca.sem, ca.at("hi", c.n))
                    if c.prompt:
                        tok = bass.ds(c.t * P, P)
                        v.tensor_tensor(u_lo[:, :, tok], ps[:, 2:4, :].rearrange("p b (k c) -> p (b k) c", c=P),
                                        u_hi[:, :, tok], ALU.subtract).then_inc(cd.step("lo"), 1)
                    else:
                        v.tensor_tensor(u_lo[:, 0:4, SEQ:TOK],
                                        ps[:, 2, :].rearrange("p (k c) -> p k c", c=P)[:, :, 0:c.rows],
                                        u_hi[:, 0:4, SEQ:TOK], ALU.subtract).then_inc(cd.step("lo"), 1)

                def mix_step(f, h):
                    if f:
                        front_gates(f)
                    if h:
                        heads_keys(h)
                    if f:
                        front_levels(f)
                    if h:
                        heads_weights(h)
                    if f:
                        front_masks(f)
                        front_silu(f)
                    if h:
                        heads_merge(h)
                    if f:
                        front_window(f)
                    if h:
                        heads_low(h)

                mix_step(prompt_chunk(l, 0, 0), None)
                with dve.Fori(0, CHUNKS // 2 - 1) as i:
                    mix_step(prompt_chunk(l, i, 1), prompt_chunk(l, i, 0))
                    mix_step(prompt_chunk(l, i + 1, 0), prompt_chunk(l, i, 1))
                mix_step(prompt_chunk(l, CHUNKS // 2 - 1, 1), prompt_chunk(l, CHUNKS // 2 - 1, 0))
                mix_step(decode_chunk(l), prompt_chunk(l, CHUNKS // 2 - 1, 1))
                mix_step(None, decode_chunk(l))
                barrier(dve, phase(l, 1))

                def split_wo(j, q, free):
                    J = l * KT + j
                    dve.wait_ge(wo_hi_done, J + 1)
                    if free:
                        dve.wait_ge(out_ready, (J - 1) * TCH)
                    v.tensor_tensor(wo_lo[q][:], wo_raw[:], wo_hi[q][:], ALU.subtract).then_inc(wo_lo_done, 1)

                def evacuate(j):
                    for c in range(TCH):
                        dve.wait_ge(out_ready, (l * KT + j) * TCH + (c + 1))
                        v.tensor_copy(acc[:, bass.ds(j, 1), c * NCH:(c + 1) * NCH].rearrange("p a b -> p (a b)"),
                                      ps[:, c, 0:NCH]).then_inc(out_free, 1)

                split_wo(0, 0, False)
                split_wo(1, 1, False)
                with dve.Fori(0, KT // 2 - 1) as i:
                    for q in range(2):
                        evacuate(i * 2 + q)
                        split_wo(i * 2 + (q + 2), q, True)
                evacuate(KT - 2)
                evacuate(KT - 1)
                barrier(dve, phase(l, 2))

                def norm_tiles(which):
                    base = (l * 2 + which) * TILES
                    hi, lo = ((v_hi, v_lo), (u_hi, u_lo))[which]

                    def moments(i, q, p, rows):
                        n = base + i * 2 + q
                        rs = slice(0, rows)
                        x = xin[which][p]
                        dve.wait_ge(x_in[p], x_count(l, which, q, i) * 16)
                        dve.wait_ge(npe.sem, npe.at("T", n))
                        v.scalar_tensor_tensor(out=x[rs], in0=x[rs], scalar=ALPHA,
                                               in1=ps[rs, 2 * p:2 * p + 2, :].rearrange("p a b -> p (a b)"),
                                               op0=ALU.mult, op1=ALU.add).then_inc(nd.step("res"), 1)
                        dve.wait_ge(nd.sem, nd.at("res", n))
                        for j in range(2):
                            v.bn_stats(stats[rs, p, j, :], x[rs, 512 * j:512 * j + 512]).then_inc(nd.step(f"st{j}"), 1)
                        dve.wait_ge(nd.sem, nd.at("st1", n))
                        apart(dve)
                        v.bn_aggr(aggr[rs, p, :], stats[rs, p, :, :]).then_inc(nd.step("aggr"), 1)
                        dve.wait_ge(nd.sem, nd.at("aggr", n))
                        v.tensor_scalar(var[rs, p:p + 1], aggr[rs, p, 1:2], LN_EPS, None, ALU.add)\
                            .then_inc(nd.step("var"), 1)

                    def norm(i, q, p, rows):
                        n = base + i * 2 + q
                        rs = slice(0, rows)
                        dve.wait_ge(nr.sem, nr.at("r", n))
                        newton(rstd[rs, p:p + 1], var[rs, p:p + 1], newt[rs, p:p + 1], dve, nd, n)
                        dve.wait_ge(nd.sem, nd.at("rstd", n))
                        dve.wait_ge(x_out[p], x_count(l, which, q, i) * 16 - 16)
                        dve.wait_ge(spe.sem, spe.at("T", n + TILES - 2))
                        v.tensor_scalar(xn[which][p][rs], xin[which][p][rs], aggr[rs, p, 0:1], rstd[rs, p:p + 1],
                                        ALU.subtract, ALU.mult).then_inc(nd.step("xn"), 1)

                    def low(t, p, rows):
                        split_tile(base + TILES + t, t, p, rows, hi, lo)

                    for p in range(2):
                        moments(0, p, p, P)
                        norm(0, p, p, P)
                    with dve.Fori(0, CHUNKS // 2 - 1) as i:
                        for p in range(2):
                            moments(i, p + 2, p, P)
                            low(i * 2 + p, p, P)
                            norm(i, p + 2, p, P)
                    moments(0, CHUNKS, 0, ROWS_S)
                    low(CHUNKS - 2, 0, P)
                    norm(0, CHUNKS, 0, ROWS_S)
                    low(CHUNKS - 1, 1, P)
                    low(CHUNKS, 0, ROWS_S)

                norm_tiles(0)
                barrier(dve, phase(l, 3))

                def hidden(b, q, first=False):
                    B = l * FBLOCKS + b

                    def low(f, c):
                        dve.wait_ge(hid_hi_done, B * 6 + (f * TCH + c + 1))
                        cols = slice(c * NCH, (c + 1) * NCH)
                        v.tensor_tensor(hid_lo[q][:, f, cols], sq[c][:], hid_hi[q][:, f, cols], ALU.subtract)\
                            .then_inc(hid_lo_done, 1)

                    units = [(f, c) for f in range(2) for c in range(TCH)]
                    for u, (f, c) in enumerate(units):
                        dve.wait_ge(up_free, B * 6 + (u + 4))
                        if u >= TCH or not first:
                            dve.wait_ge(hid_lo_done, B * 6 + (u - 2))
                        v.tensor_tensor(sq[c][:], relu[c][:], relu[c][:], ALU.mult).then_inc(sq_done, 1)
                        if u:
                            low(*units[u - 1])
                    low(*units[-1])

                def collect(b):
                    V = (l * FBLOCKS + b) * (KT * TCH)
                    for d in range(KT):
                        for c in range(TCH):
                            dve.wait_ge(down_ready, V + (d * TCH + c + 1))
                            at = acc[:, d, c * NCH:(c + 1) * NCH]
                            v.tensor_tensor(at, ps[:, 3 + c, 0:NCH], at, ALU.add).then_inc(down_free, 1)

                hidden(0, 0, True)
                dve.wait_ge(acc_zero, l + 1)
                apart(dve)
                with dve.Fori(0, FBLOCKS // 2 - 1) as i:
                    for q in range(2):
                        hidden(i * 2 + (q + 1), 1 - q)
                        collect(i * 2 + q)
                hidden(FBLOCKS - 1, 1)
                collect(FBLOCKS - 2)
                collect(FBLOCKS - 1)
                barrier(dve, phase(l, 4))
                norm_tiles(1)
                barrier(dve, phase(l, 5))

        @block.gpsimd
        def _(pool):
            g_ = nc.gpsimd
            for S in (npl, rp, gp, dp):
                pool.sem_inc(S.sem, 1)
            barrier(pool, 1)

            with pool.Fori(0, DEPTH) as l:
                barrier(pool, phase(l, 0))

                def front(c, h):
                    n, w, p, rows, prompt = c.n, c.w, c.p, c.rows, c.prompt
                    var = "" if prompt else "s"
                    x, tab = hb[p], rt[p]
                    pool.wait_ge(h_in[p], c.loads * 64)
                    pool.wait_ge(tpe.sem, tpe.before(n))
                    if not prompt:
                        pool.wait_ge(kv_out, (l + 1) * 32)
                    xr = x[:, RQ:RQ + 256].rearrange("p (h s i) -> p h s i", h=8, s=2)
                    ra = rope_a[:, :].rearrange("p (h s i) -> p h s i", h=8, s=2)
                    rb = rope_b[:, :].rearrange("p (h s i) -> p h s i", h=8, s=2)
                    rr = rot_r[:, :].rearrange("p (h s i) -> p h s i", h=8, s=2)
                    g_.tensor_tensor(rope_a[:, :].rearrange("p (h i) -> p h i", i=16),
                                     x[:, RQ:RQ + 256].rearrange("p (h i) -> p h i", i=16),
                                     tab[:, 0:16].unsqueeze(1).broadcast_to([P, 16, 16]), ALU.mult)\
                        .then_inc(rp.step("ra"), 1)
                    sin = tab[:, 16:32].unsqueeze(1).broadcast_to([P, 8, 16])
                    g_.tensor_tensor(rb[:, :, 0, :], xr[:, :, 1, :], sin, ALU.mult).then_inc(rp.step("rb0"), 1)
                    g_.tensor_tensor(rb[:, :, 1, :], xr[:, :, 0, :], sin, ALU.mult).then_inc(rp.step("rb1"), 1)
                    pool.wait_ge(rp.sem, rp.at("rb1", n))
                    g_.tensor_tensor(rr[:, :, 0, :], ra[:, :, 0, :], rb[:, :, 0, :], ALU.subtract).then_inc(rp.step("r0"), 1)
                    g_.tensor_tensor(rr[:, :, 1, :], ra[:, :, 1, :], rb[:, :, 1, :], ALU.add).then_inc(rp.step("r1"), 1)
                    xs = x[:, SQ:SQ + 640].rearrange("p (h d) -> p h d", d=64)
                    cos = tab[:, 32:40].unsqueeze(1).broadcast_to([P, 10, 8])
                    sin = tab[:, 40:48].unsqueeze(1).broadcast_to([P, 10, 8])
                    g_.tensor_tensor(rope_sa[:, :, :, :],
                                     xs[:, :, 0:16].rearrange("p h (s i) -> p h s i", s=2),
                                     tab[:, 32:40].unsqueeze(1).unsqueeze(1).broadcast_to([P, 10, 2, 8]), ALU.mult)\
                        .then_inc(rp.step("sa"), 1)
                    g_.tensor_tensor(rope_sb[:, :, 0, :], xs[:, :, 8:16], sin, ALU.mult).then_inc(rp.step("sb0"), 1)
                    g_.tensor_tensor(rope_sb[:, :, 1, :], xs[:, :, 0:8], sin, ALU.mult).then_inc(rp.step("sb1"), 1)
                    pool.wait_ge(rp.sem, rp.at("sb1", n))
                    for s, op in ((0, ALU.subtract), (1, ALU.add)):
                        g_.tensor_tensor(rot_q[:, :, :, 8 * s:8 * s + 8].rearrange("p g k d -> p k g d"),
                                         rope_sa[:, 0:8, s, :].rearrange("p (k g) d -> p k g d", k=2),
                                         rope_sb[:, 0:8, s, :].rearrange("p (k g) d -> p k g d", k=2), op)\
                            .then_inc(rp.step(f"q{s}"), 1)
                    for s, op in ((0, ALU.subtract), (1, ALU.add)):
                        g_.tensor_tensor(rot_k[:, :, 8 * s:8 * s + 8], rope_sa[:, 8:10, s, :], rope_sb[:, 8:10, s, :], op)\
                            .then_inc(rp.step(f"k{s}"), 1)
                    g_.tensor_copy(rot_q[:, :, :, 16:64].rearrange("p g k d -> p k g d"),
                                   x[:, SQ:SK].rearrange("p (k g d) -> p k g d", k=2, g=4)[:, :, :, 16:64])\
                        .then_inc(rp.step("qc"), 1)
                    g_.tensor_copy(rot_k[:, :, 16:64], x[:, SK:SV].rearrange("p (k d) -> p k d", k=2)[:, :, 16:64])\
                        .then_inc(rp.step("kc"), 1)
                    if h:
                        pool.wait_ge(mpe.sem, mpe.before(h.n))
                    g_.tensor_tensor(r_kd[p][:], rot_r[:, P:2 * P].rearrange("p (h d) -> p h d", h=4),
                                     cst("kdec" + var).unsqueeze(2).broadcast_to([P, 4, 32]), ALU.mult)\
                        .then_inc(rp.step("kd"), 1)
                    pool.wait_ge(wpe.sem, wpe.before(w))
                    apart(pool)
                    g_.tensor_copy(s_v[:, p, :], x[:, SV:SV + P]).then_inc(rp.step("v"), 1)
                    pool.wait_ge(ga.sem, ga.at("eb", n))
                    g_.tensor_tensor(g_qe[p][:], g_q[:], g_eb[p][:], ALU.mult).then_inc(gp.step("qe"), 1)
                    pool.wait_ge(ga.sem, ga.at("ka", n))
                    g_.tensor_tensor(g_ka[p][:], g_k[:], g_ka[p][:], ALU.mult).then_inc(gp.step("kst"), 1)
                    if h:
                        pool.wait_ge(mpe.sem, mpe.at("lev0", h.n))
                    else:
                        pool.wait_ge(zd.sem, zd.at("lr", l))
                    for i in LEVEL_ORDER:
                        half = HALVES[i]

                        def side(a, cols):
                            return a.rearrange("p a (k w) -> p a k w", w=2 * half)[:, :, :, cols]

                        left, right = slice(0, half), slice(half, 2 * half)
                        g_.tensor_tensor(side(lev_x[:, i, :, :], left), side(lev_e[:, i, :, :], left),
                                         side(g_k[:, :, :], left), ALU.mult).then_inc(gp.step(f"l{i}"), 1)
                        for j in range(2):
                            d = slice(64 * j, 64 * j + 64)
                            if j:
                                pool.wait_ge(gp.sem, gp.at(f"r{i}", n))
                            g_.tensor_tensor(lev_r[d, i, :, j, :].rearrange("p a (k w) -> p a k w", w=half),
                                             side(lev_e[d, i, :, :], right), side(g_q[d, :, :], right), ALU.mult)\
                                .then_inc(gp.step(f"{'rs'[j]}{i}"), 1)
                        pool.wait_ge(gp.sem, gp.at(f"s{i}", n))
                    pool.wait_ge(gg.sem, gg.at("s1", n))
                    hg = gate[p][:, 1].rearrange("p (h d) -> p h d", h=4)
                    g_.tensor_tensor(hg, hg, hg_w[:, :].unsqueeze(1).broadcast_to([P, 4, 64]), ALU.mult)\
                        .then_inc(rp.step("sw"), 1)

                def heads(c):
                    n, p, rows = c.n, c.p, c.rows
                    if not c.prompt:
                        pool.wait_ge(hd.sem, hd.at("kt", n))
                        bm = cst("bm").rearrange("p (b t) -> p b t", b=NB)
                        g_.tensor_tensor(qm_r[:], r_qi[p][:, 0:rows].unsqueeze(1).broadcast_to([P, NB, rows]), bm, ALU.mult)\
                            .then_inc(dp.step("qr"), 1)
                        pool.wait_ge(gp.sem, gp.at("qe", n))
                        for j in range(2):
                            g_.tensor_tensor(qm_h[:, j], g_qe[p][:, j, 0:rows].unsqueeze(1).broadcast_to([P, NB, rows]), bm,
                                             ALU.mult).then_inc(dp.step(f"qh{j}"), 1)
                        tb = cst("tb")[0:rows].unsqueeze(2).broadcast_to([rows, NB, P])
                        pool.wait_ge(rp.sem, rp.at("kd", n))
                        g_.tensor_tensor(kdm[0:rows], r_kd[p][0:rows].rearrange("p a b -> p (a b)").unsqueeze(1)
                                         .broadcast_to([rows, NB, P]), tb, ALU.mult).then_inc(dp.step("kd"), 1)
                        for j in range(2):
                            g_.tensor_tensor(ksm[0:rows, j], g_kt[0:rows, j, :].unsqueeze(1).broadcast_to([rows, NB, P]),
                                             tb, ALU.mult).then_inc(dp.step(f"ks{j}"), 1)
                def mix_step(f, h):
                    if f:
                        front(f, h)
                    if h:
                        heads(h)

                pool.wait_ge(par_in, (l * 8 + 4) * 16)
                apart(pool)
                mix_step(prompt_chunk(l, 0, 0), None)
                with pool.Fori(0, CHUNKS // 2 - 1) as i:
                    mix_step(prompt_chunk(l, i, 1), prompt_chunk(l, i, 0))
                    mix_step(prompt_chunk(l, i + 1, 0), prompt_chunk(l, i, 1))
                mix_step(prompt_chunk(l, CHUNKS // 2 - 1, 1), prompt_chunk(l, CHUNKS // 2 - 1, 0))
                mix_step(decode_chunk(l), prompt_chunk(l, CHUNKS // 2 - 1, 1))
                mix_step(None, decode_chunk(l))
                barrier(pool, phase(l, 1))
                barrier(pool, phase(l, 2))

                def norm_tiles(which):
                    base = (l * 2 + which) * TILES
                    pool.wait_ge(par_in, (l * 8 + (6 + 2 * which)) * 16)
                    apart(pool)

                    def scale(n, p, rows):
                        rs = slice(0, rows)
                        x = xn[which][p]
                        pool.wait_ge(nd.sem, nd.at("xn", n))
                        g_.tensor_tensor(x[rs], x[rs], ln_g[which][rs], ALU.mult).then_inc(npl.step("g"), 1)
                        pool.wait_ge(npl.sem, npl.at("g", n))
                        g_.tensor_tensor(x[rs], x[rs], ln_b[rs], ALU.add).then_inc(npl.step("b"), 1)

                    with pool.Fori(0, CHUNKS // 2) as i:
                        for p in range(2):
                            scale(base + i * 2 + p, p, P)
                    scale(base + CHUNKS, 0, ROWS_S)

                def split_wu(b):
                    B = l * FBLOCKS + b
                    pool.wait_ge(wu_hi_done, B + 1)
                    g_.tensor_tensor(wu_lo[:], wu_raw[:], wu_hi[:], ALU.subtract).then_inc(wu_lo_done, 1)

                norm_tiles(0)
                split_wu(0)
                barrier(pool, phase(l, 3))

                g_.memset(acc[:], 0.0).then_inc(acc_zero, 1)

                def split_wd(b):
                    B = l * FBLOCKS + b
                    pool.wait_ge(wd_hi_done, B + 1)
                    g_.tensor_tensor(wd_lo[:], wd_raw[:], wd_hi[:], ALU.subtract).then_inc(wd_lo_done, 1)

                with pool.Fori(0, FBLOCKS - 1) as b:
                    split_wu(b + 1)
                    split_wd(b)
                split_wd(FBLOCKS - 1)
                barrier(pool, phase(l, 4))
                norm_tiles(1)
                barrier(pool, phase(l, 5))


INPUTS = ("state_ret", "state_hgrn", "w_in", "w_out", "hg_lb_raw", "hg_norm_w", "ln_mix_g", "ln_mix_b", "w_up",
          "w_down", "ln_ffn_g", "ln_ffn_b", "swa_sinks")


def kernel(**inputs):
    import concourse.bacc as _bacc
    from concourse.bass_utils import run_bass_kernel_spmd as _run

    nc = _bacc.Bacc("TRN2", target_bir_lowering=False, num_devices=1)
    a = {k: np.asarray(v) for k, v in inputs.items()}
    data = {k: a[k] for k in INPUTS}
    data["x"] = np.concatenate([a["x_prompt"].reshape(SEQ, DM), a["x_sample"].reshape(ROWS_S, DM)])
    data["cache_swa_k"] = a["cache_swa_k"].reshape(DEPTH, NB, WIN, P)
    data["cache_swa_v"] = a["cache_swa_v"].reshape(DEPTH, NB, WIN, P)
    data["sink_rows"] = np.tile(np.repeat(a["swa_sinks"], NL, axis=1), (1, 4)).T
    data["c_const"], data["c_lev"], data["c_swa"], data["c_rope"] = shape_constants()
    arrays, A = {}, {}
    for name, value in data.items():
        value = np.ascontiguousarray(value)
        arrays[f"in_{name}"] = value
        A[name] = nc.dram_tensor(f"in_{name}", value.shape, mybir.dt.from_np(value.dtype), kind="ExternalInput").ap()
    outs = {"y": (TOK, DM), "p_state_ret": (DEPTH, 4, 32, 64), "p_state_hgrn": (DEPTH, 4, 64, 64),
            "p_swa_k": (DEPTH, WIN, P), "p_swa_v": (DEPTH, WIN, P), "s_state_ret": (DEPTH, NB, 4, 32, 64),
            "s_state_hgrn": (DEPTH, NB, 4, 64, 64), "s_swa_k": (DEPTH, NB, WIN, P), "s_swa_v": (DEPTH, NB, WIN, P)}
    for name, shape in outs.items():
        A[name] = nc.dram_tensor(f"out_{name}", shape, F32, kind="ExternalOutput").ap()
    A["hscr"] = nc.dram_tensor("hscr", (TOK, COLS), F32, kind="Internal").ap()
    build(nc, A)
    got = _run(nc, [arrays], core_ids=[0]).results[0]
    r = {name: got[f"out_{name}"] for name in outs}
    return (r["y"][0:SEQ].reshape(1, SEQ, DM), r["y"][SEQ:].reshape(NB, NL, DM),
            r["p_state_ret"].reshape(DEPTH, 1, 4, 32, 64), r["p_state_hgrn"].reshape(DEPTH, 1, 4, 64, 64),
            r["p_swa_k"].reshape(DEPTH, 1, WIN, 2, 64), r["p_swa_v"].reshape(DEPTH, 1, WIN, 2, 64),
            r["s_state_ret"], r["s_state_hgrn"],
            r["s_swa_k"].reshape(DEPTH, NB, WIN, 2, 64), r["s_swa_v"].reshape(DEPTH, NB, WIN, 2, 64))
```
